# Optimizing a Trainium2 kernel written in Bass

```python
import jax, jax.numpy as jnp
from jax import lax
import numpy as np

D_MODEL = 1024
BATCH = 1
SEQ = 1024
DEPTH = 1
DEC_BATCH = 1
DEC_SEQ = 64
PAST_LEN = 1024

CHUNK = 64
Q_BLOCK = 128
MIX_WIDTH = D_MODEL // 2
H_A = 4
DV_A = MIX_WIDTH // H_A
DK_A = DV_A // 2
QK_A = H_A * DK_A
GATE_RANK = 16
GATE_TAU = 16.0
H_B = 8
DH_B = MIX_WIDTH // H_B
N_BRANCH = 2
N_GROUPS = 4
EXPERTS_PER_GROUP = 8
N_EXPERTS = N_GROUPS * EXPERTS_PER_GROUP
TOP_K = 2
D_EXPERT = D_MODEL // 2
MOE_BLOCK = 128
RMS_EPS = 1e-6
SPLIT_POINTS = (QK_A, 2 * QK_A, 2 * QK_A + MIX_WIDTH, 2 * QK_A + 2 * MIX_WIDTH,
                2 * QK_A + 2 * MIX_WIDTH + GATE_RANK, 2 * QK_A + 3 * MIX_WIDTH + GATE_RANK,
                2 * QK_A + 4 * MIX_WIDTH + GATE_RANK, 2 * QK_A + 5 * MIX_WIDTH + GATE_RANK)
IN_WIDTH = 2 * QK_A + 5 * MIX_WIDTH + GATE_RANK + N_BRANCH * D_MODEL

kernel_name = 'gla_stickbreak_hmoe_stream_step'

def rms_norm(x, gain):
    xf = x.astype(jnp.float32)
    xf = xf * lax.rsqrt(jnp.mean(xf * xf, axis=-1, keepdims=True) + RMS_EPS)
    return (xf * gain.astype(jnp.float32)).astype(x.dtype)

def gla_recurrence(q, k, v, log_a, s0):
    B, S, H, DK = q.shape
    DV = v.shape[-1]
    C = min(CHUNK, S)
    N = S // C
    f32 = jnp.float32

    def chunks(t):
        return jnp.moveaxis(t.astype(f32).reshape(B, N, C, *t.shape[2:]), 1, 0)

    causal = jnp.tril(jnp.ones((C, C), dtype=bool))[None, :, :, None, None]

    def step(state, inp):
        qc, kc, vc, gc = inp
        b = jnp.cumsum(gc, axis=1)
        b_last = b[:, -1]
        inter = jnp.einsum('bthk,bhkv->bthv', qc * jnp.exp(b), state)
        decay = jnp.exp(jnp.where(causal, b[:, :, None] - b[:, None, :], -jnp.inf))
        att = jnp.einsum('bthk,bshk,btshk->bhts', qc, kc, decay)
        intra = jnp.einsum('bhts,bshv->bthv', att, vc)
        state = state * jnp.exp(b_last)[..., None] + jnp.einsum(
            'bshk,bshv->bhkv', kc * jnp.exp(b_last[:, None] - b), vc)
        return state, inter + intra

    s_fin, out = lax.scan(step, s0.astype(f32), (chunks(q), chunks(k), chunks(v), chunks(log_a)))
    out = jnp.moveaxis(out, 0, 1).reshape(B, S, H, DV)
    return out, s_fin

def stick_breaking(q, k, v, q_pos, k_pos):
    B, Sq, H, D = q.shape
    blk = min(Q_BLOCK, Sq)
    nb = Sq // blk
    qb = jnp.moveaxis(q.reshape(B, nb, blk, H, D), 1, 0)
    pb = q_pos.reshape(nb, blk)
    scale = D ** -0.5

    def one_block(args):
        qc, pc = args
        z = jnp.einsum('bqhd,bkhd->bhqk', qc, k).astype(jnp.float32) * scale
        mask = (k_pos[None, :] < pc[:, None])[None, None]
        log_beta = jax.nn.log_sigmoid(z)
        log_keep = jnp.where(mask, jax.nn.log_sigmoid(-z), 0.0)
        between = lax.cumsum(log_keep, axis=3, reverse=True) - log_keep
        w = jnp.where(mask, jnp.exp(log_beta + between), 0.0)
        return jnp.einsum('bhqk,bkhd->bqhd', w.astype(v.dtype), v)

    out = lax.map(one_block, (qb, pb))
    return jnp.moveaxis(out, 0, 1).reshape(B, Sq, H, D)

def routed_experts(h, expert_idx, expert_w, w_gate, w_up, w_down):
    T = h.shape[0]
    A = T * TOP_K
    n_blocks = -(-(A + N_EXPERTS * (MOE_BLOCK - 1)) // MOE_BLOCK)
    P = n_blocks * MOE_BLOCK
    flat_e = expert_idx.reshape(A)
    order = jnp.argsort(flat_e)
    sorted_e = flat_e[order]
    counts = jnp.bincount(flat_e, length=N_EXPERTS)
    padded = (counts + MOE_BLOCK - 1) // MOE_BLOCK * MOE_BLOCK
    pad_end = jnp.cumsum(padded)
    pad_start = pad_end - padded
    start = jnp.cumsum(counts) - counts
    dest = pad_start[sorted_e] + jnp.arange(A) - start[sorted_e]
    tok_sorted = order // TOP_K
    slot_tok = jnp.zeros((P,), jnp.int32).at[dest].set(tok_sorted.astype(jnp.int32))
    block_e = jnp.minimum(jnp.searchsorted(pad_end, jnp.arange(n_blocks) * MOE_BLOCK, side='right'),
                          N_EXPERTS - 1)
    xb = h[slot_tok].reshape(n_blocks, MOE_BLOCK, h.shape[1])

    def run_block(args):
        xblk, e = args
        return (jax.nn.silu(xblk @ w_gate[e]) * (xblk @ w_up[e])) @ w_down[e]

    yb = lax.map(run_block, (xb, block_e)).reshape(P, h.shape[1])
    y_sorted = yb[dest] * expert_w.reshape(A)[order][:, None]
    return jax.ops.segment_sum(y_sorted, tok_sorted, num_segments=T).astype(h.dtype)

def hier_moe(h, w_router_group, b_router_group, w_router_expert, b_router_expert, w_exp_gate, w_exp_up, w_exp_down):
    T = h.shape[0]
    g_prob = jax.nn.softmax((h @ w_router_group).astype(jnp.float32) + b_router_group, axis=-1)
    g_p, g_idx = lax.top_k(g_prob, 1)
    e_logits = ((h @ w_router_expert).astype(jnp.float32) + b_router_expert).reshape(T, N_GROUPS, EXPERTS_PER_GROUP)
    e_logits = jnp.take_along_axis(e_logits, g_idx[:, :, None], axis=1)[:, 0]
    e_p, e_idx = lax.top_k(jax.nn.softmax(e_logits, axis=-1), TOP_K)
    weights = g_p * (e_p / jnp.sum(e_p, axis=-1, keepdims=True))
    experts = g_idx * EXPERTS_PER_GROUP + e_idx
    return routed_experts(h, experts, weights, w_exp_gate, w_exp_up, w_exp_down)

def trunk_layer(x, gla_s0, k_past, v_past, norm_mix_gain, w_in, w_gla_gate_up, b_gla_gate, gla_norm_gain,
                w_branch, w_out, norm_ffn_gain, w_router_group, b_router_group, w_router_expert,
                b_router_expert, w_exp_gate, w_exp_up, w_exp_down):
    B, S, _ = x.shape
    past = 0 if k_past is None else k_past.shape[1]
    h = rms_norm(x, norm_mix_gain)
    q_a, k_a, v_a, r_a, lr_a, q_b, k_b, v_b, g_br = jnp.split(h @ w_in, SPLIT_POINTS, axis=-1)

    log_a = jax.nn.log_sigmoid((lr_a @ w_gla_gate_up + b_gla_gate).astype(jnp.float32)) / GATE_TAU
    o_a, s_new = gla_recurrence(q_a.reshape(B, S, H_A, DK_A) * (DK_A ** -0.5), k_a.reshape(B, S, H_A, DK_A),
                                v_a.reshape(B, S, H_A, DV_A), log_a.reshape(B, S, H_A, DK_A), gla_s0)
    o_a = rms_norm(o_a, gla_norm_gain).astype(x.dtype) * jax.nn.silu(r_a.reshape(B, S, H_A, DV_A))

    k_new = k_b.reshape(B, S, H_B, DH_B)
    v_new = v_b.reshape(B, S, H_B, DH_B)
    if k_past is None:
        k_all, v_all = k_new, v_new
    else:
        k_all = jnp.concatenate([k_past.astype(k_new.dtype), k_new], axis=1)
        v_all = jnp.concatenate([v_past.astype(v_new.dtype), v_new], axis=1)
    o_b = stick_breaking(q_b.reshape(B, S, H_B, DH_B), k_all, v_all,
                         past + jnp.arange(S, dtype=jnp.int32), jnp.arange(past + S, dtype=jnp.int32))

    y_a = o_a.reshape(B, S, MIX_WIDTH) @ w_branch[0]
    y_b = o_b.reshape(B, S, MIX_WIDTH) @ w_branch[1]
    gates = jax.nn.sigmoid(g_br.reshape(B, S, N_BRANCH, D_MODEL))
    x = x + ((gates[:, :, 0] * y_a + gates[:, :, 1] * y_b) @ w_out).astype(x.dtype)

    h2 = rms_norm(x, norm_ffn_gain).reshape(B * S, D_MODEL)
    x = x + hier_moe(h2, w_router_group, b_router_group, w_router_expert, b_router_expert,
                     w_exp_gate, w_exp_up, w_exp_down).reshape(B, S, D_MODEL).astype(x.dtype)
    return x, s_new.astype(gla_s0.dtype), k_new, v_new

def setup_inputs(seed: int = 0) -> dict:
    key = jax.random.key(seed)
    ks = jax.random.split(key, 24)
    f32 = jnp.float32

    def nrm(k, shape, scale):
        return jax.random.normal(k, shape, f32) * scale

    return {
        'x_prompt': nrm(ks[0], (BATCH, SEQ, D_MODEL), 1.0),
        'x_sample': nrm(ks[1], (DEC_BATCH, DEC_SEQ, D_MODEL), 1.0),
        'state_gla': nrm(ks[2], (DEPTH, DEC_BATCH, H_A, DK_A, DV_A), 0.5),
        'cache_sb_k': nrm(ks[3], (DEPTH, DEC_BATCH, PAST_LEN, H_B, DH_B), 1.0),
        'cache_sb_v': nrm(ks[4], (DEPTH, DEC_BATCH, PAST_LEN, H_B, DH_B), 1.0),
        'norm_mix_gain': 1.0 + nrm(ks[5], (DEPTH, D_MODEL), 0.02),
        'w_in': nrm(ks[6], (DEPTH, D_MODEL, IN_WIDTH), D_MODEL ** -0.5),
        'w_gla_gate_up': nrm(ks[7], (DEPTH, GATE_RANK, QK_A), GATE_RANK ** -0.5),
        'b_gla_gate': nrm(ks[8], (DEPTH, QK_A), 0.02),
        'gla_norm_gain': 1.0 + nrm(ks[9], (DEPTH, DV_A), 0.02),
        'w_branch': nrm(ks[10], (DEPTH, N_BRANCH, MIX_WIDTH, D_MODEL), MIX_WIDTH ** -0.5),
        'w_out': nrm(ks[11], (DEPTH, D_MODEL, D_MODEL), D_MODEL ** -0.5),
        'norm_ffn_gain': 1.0 + nrm(ks[12], (DEPTH, D_MODEL), 0.02),
        'w_router_group': nrm(ks[13], (DEPTH, D_MODEL, N_GROUPS), D_MODEL ** -0.5),
        'b_router_group': nrm(ks[14], (DEPTH, N_GROUPS), 0.01),
        'w_router_expert': nrm(ks[15], (DEPTH, D_MODEL, N_EXPERTS), D_MODEL ** -0.5),
        'b_router_expert': nrm(ks[16], (DEPTH, N_EXPERTS), 0.01),
        'w_exp_gate': nrm(ks[17], (DEPTH, N_EXPERTS, D_MODEL, D_EXPERT), D_MODEL ** -0.5),
        'w_exp_up': nrm(ks[18], (DEPTH, N_EXPERTS, D_MODEL, D_EXPERT), D_MODEL ** -0.5),
        'w_exp_down': nrm(ks[19], (DEPTH, N_EXPERTS, D_EXPERT, D_MODEL), D_EXPERT ** -0.5),
        'norm_final_gain': 1.0 + nrm(ks[20], (D_MODEL,), 0.02),
    }

def reference(x_prompt, x_sample, state_gla, cache_sb_k, cache_sb_v, norm_mix_gain, w_in, w_gla_gate_up,
              b_gla_gate, gla_norm_gain, w_branch, w_out, norm_ffn_gain, w_router_group, b_router_group,
              w_router_expert, b_router_expert, w_exp_gate, w_exp_up, w_exp_down, norm_final_gain):
    yp, ys = x_prompt, x_sample
    gla_p, k_p, v_p, gla_s, k_s, v_s = [], [], [], [], [], []
    for l in range(DEPTH):
        lw = (norm_mix_gain[l], w_in[l], w_gla_gate_up[l], b_gla_gate[l], gla_norm_gain[l], w_branch[l],
              w_out[l], norm_ffn_gain[l], w_router_group[l], b_router_group[l], w_router_expert[l],
              b_router_expert[l], w_exp_gate[l], w_exp_up[l], w_exp_down[l])
        s0 = jnp.zeros((yp.shape[0], H_A, DK_A, DV_A), yp.dtype)
        yp, sp, kp, vp = trunk_layer(yp, s0, None, None, *lw)
        ys, ss, kn, vn = trunk_layer(ys, state_gla[l], cache_sb_k[l], cache_sb_v[l], *lw)
        gla_p.append(sp); k_p.append(kp); v_p.append(vp)
        gla_s.append(ss); k_s.append(kn); v_s.append(vn)
    y_prompt = rms_norm(yp, norm_final_gain)
    y_sample = rms_norm(ys, norm_final_gain)
    return (y_prompt, y_sample, jnp.stack(gla_p), jnp.stack(k_p), jnp.stack(v_p),
            jnp.stack(gla_s), jnp.stack(k_s), jnp.stack(v_s))


_drawn_inputs = setup_inputs


def setup_inputs(seed=0):
    import zlib

    import numpy as np

    out = dict(_drawn_inputs(seed))
    spreads = {}
    factors = {'b_gla_gate': 6.45,
     'b_router_group': 4.42,
     'b_router_expert': 3.395,
     'norm_final_gain': 25.504,
     'gla_norm_gain': 3.158,
     'cache_sb_k': 2.791}
    for name, (base, spread) in spreads.items():
        noise = np.random.default_rng([zlib.crc32(name.encode()), seed]).standard_normal(out[name].shape)
        drawn = base * np.exp(spread * noise) if base else spread * noise
        out[name] = __import__('jax').numpy.asarray(drawn.astype(out[name].dtype))
    for name, factor in factors.items():
        out[name] = (out[name] * factor).astype(out[name].dtype)
    return out
```

```python
from contextlib import ExitStack

import numpy as np

import concourse.bass as bass
from concourse import mybir

P = 128
D = 1024
SEQ, DEC, PAST = 1024, 64, 1024
TILES = (SEQ + DEC + P - 1) // P
PROMPT_TILES = SEQ // P
ROWS = TILES * P
SAMPLE = TILES - 1
KD = D // P
MIX = D // 2
H_A, DV = 4, 128
DK = 64
QK = H_A * DK
H_B, DH = 8, 64
PAIRS = H_B // 2
RANK = 16
GATE_TAU = 16.0
GROUPS, PER_GROUP, EXPERTS = 4, 8, 32
ROUTES = GROUPS + EXPERTS
FF = D // 2
EPS = 1e-6
N = 512
CHUNKS = 10
MAIN = CHUNKS * N
COL_QKVR = 0
COL_QB, COL_KB, COL_VB = 1536, 2048, 2560
COL_GATES = 3072
ASSIGNED = 2 * (SEQ + DEC)
BLOCKS = EXPERTS + ASSIGNED // P
SLOTS = (BLOCKS + 1) * P
NOWHERE = 1 << 20
MASKED = -1e30

F32 = mybir.dt.float32
F32R = mybir.dt.float32r
BF16 = mybir.dt.bfloat16
I32 = mybir.dt.int32
ALU = mybir.AluOpType
ACT = mybir.ActivationFunctionType
X = mybir.AxisListType.X


def semaphores(nc, ctx):
    given = []

    def clear():
        nc.clear_and_free_semaphores(given)
        nc.all_engine_barrier()

    ctx.callback(clear)

    def named(name):
        given.append(nc.alloc_semaphore(name=name))
        return given[-1]

    return named


class Chain:

    def __init__(self, engine, sem, start=0):
        self.engine, self.sem, self.start, self.count = engine, sem, start, 0

    def link(self, ins):
        self.mark(ins)
        self.wait()

    def mark(self, ins):
        ins.then_inc(self.sem, 1)
        self.count += 1

    def wait(self):
        self.engine.wait_ge(self.sem, self.start + self.count)


def columns(i, size=P):
    return bass.ds(i * size, size)


def constants(nc, s):
    with ExitStack() as ctx:
        made = ctx.enter_context(nc.semaphore("constants_filled"))
        done = ctx.enter_context(nc.semaphore("constants_selected"))
        turned = ctx.enter_context(nc.semaphore("constants_cast"))
        iota = ctx.enter_context(nc.sbuf_tensor("iota_int", [P, EXPERTS + GROUPS], I32))
        tri = ctx.enter_context(nc.sbuf_tensor("tri_whole", [P, P], F32))
        block = ctx.enter_context(nc.Block())

        @block.gpsimd
        def _(pool):
            fills = [
                (s.ident[:], 0.0), (s.ident_b[:], 0.0), (s.later_b[:], 0.0), (s.causal[:], 1.0), (tri[:], 1 / GATE_TAU),
                (s.before_b[:], 1.0), (s.ones_b[:], 1.0), (s.spans[:], 0.0), (s.valid[:], 1.0), (s.nowhere[:], 0.0), (s.root[:], -0.5),
            ]
            for where, value in fills:
                pool.memset(where, value).then_inc(made, 1)
            pool.wait_ge(made, len(fills))
            selects = [
                (s.ident[:], ALU.not_equal, 1.0, 0, -1, 1),
                (s.ident_b[:], ALU.not_equal, 1.0, 0, -1, 1),
                (s.later_b[:], ALU.is_gt, MASKED, 0, -1, 1),
                (s.causal[:], ALU.is_ge, 0.0, 0, 1, -1),
                (tri[:], ALU.is_ge, 0.0, 0, 1, -1),
                (s.before_b[:], ALU.is_gt, 0.0, 0, 1, -1),
            ]
            for where, op, fill, base, step, mult in selects:
                pool.affine_select(out=where, in_=where, compare_op=op, fill=fill, base=base, pattern=[[step, P]],
                                   channel_multiplier=mult).then_inc(done, 1)
            pool.iota(iota[:, 0:EXPERTS], pattern=[[1, EXPERTS]], base=0, channel_multiplier=0).then_inc(done, 1)
            pool.iota(iota[:, EXPERTS:], pattern=[[1, GROUPS]], base=0, channel_multiplier=0).then_inc(done, 1)
            pool.iota(s.assignment[:], pattern=[[2 * P, TILES], [1, 2]], base=0, channel_multiplier=2).then_inc(done, 1)

        @block.vector
        def _(dve):
            dve.wait_ge(done, 9)
            dve.memset(s.spans[0:64, 0:1], 1 / GATE_TAU).then_inc(turned, 1)
            dve.memset(s.spans[64:P, 1:2], 1 / GATE_TAU).then_inc(turned, 1)
            dve.memset(s.valid[DEC:P, SAMPLE:TILES], 0.0).then_inc(turned, 1)
            dve.memset(s.nowhere[DEC:P, SAMPLE:TILES], float(NOWHERE)).then_inc(turned, 1)
            dve.tensor_copy(s.iota[:], iota[:]).then_inc(turned, 1)
            dve.tensor_scalar(s.tri_mid[0:64, :], tri[0:64, :], -1 / GATE_TAU, None, ALU.add).then_inc(turned, 1)
            dve.tensor_copy(s.tri_mid[64:P, :], tri[64:P, :]).then_inc(turned, 1)
            dve.wait_ge(turned, 7)


def project(nc, s, io):
    RAW, PIECES, STAGES, BANKS = 4, 4, 6, 6
    PER_PIECE = KD // PIECES
    with ExitStack() as ctx:
        sb = lambda name, shape, dt=F32: ctx.enter_context(nc.sbuf_tensor(name, shape, dt))
        sem = semaphores(nc, ctx)
        ht_hi = sb("ht_hi", [P, KD, ROWS], F32R)
        ht_lo = sb("ht_lo", [P, KD, ROWS], F32R)
        w_raw = sb("w_raw", [P, RAW, PER_PIECE, N])
        w_hi = sb("w_hi", [P, 2, KD, N], F32R)
        w_lo = sb("w_lo", [P, 2, KD, N], F32R)
        stage = sb("stage", [P, STAGES, N])
        x_in = sb("x_in", [P, 2, D])
        x_norm = sb("x_norm", [P, 2, D])
        gain = sb("gain_mix", [P, D])
        stat = sb("stat_mix", [P, 2, 3])
        square = w_raw[:, 0].rearrange("p k n -> p (k n)")
        rank_raw = sb("rank_raw", [P, KD, RANK])
        rank_hi = sb("rank_hi", [P, KD, P], F32R)
        rank_lo = sb("rank_lo", [P, KD, P], F32R)
        banks = ctx.enter_context(nc.psum_tensor("banks", [P, 8, N], F32))

        gain_in = sem("gain_in")
        x_loaded = [sem("x_loaded0"), sem("x_loaded1")]
        x_zeroed = sem("x_zeroed")
        x_kept = sem("x_kept")
        rank_in = sem("rank_in")
        rank_zero = sem("rank_zero")
        rank_high = sem("rank_high")
        rank_low = sem("rank_low")
        squared = sem("squared")
        normed = sem("normed")
        rooted = sem("rooted_mix")
        turned = sem("turned")
        ht_high = sem("ht_high")
        ht_low = sem("ht_low")
        w_loaded = [sem(f"w_loaded{j}") for j in range(RAW)]
        w_high = sem("w_high")
        w_split = sem("w_split")
        product = sem("product")
        evacuated = sem("evacuated")
        stored = [sem(f"stored{j}") for j in range(STAGES)]
        rank_product = sem("rank_product")
        rank_kept = sem("rank_kept")
        block = ctx.enter_context(nc.Block())

        def turned_banks(t):
            return banks[:, 2 * (t % 2):2 * (t % 2) + 2].rearrange("p b (k c) -> p (b k) c", c=P)

        def high_part(act, t):
            act.wait_ge(turned, t + 1)
            act.activation(ht_hi[:, :, t * P:(t + 1) * P], turned_banks(t), ACT.Copy).then_inc(ht_high, 1)

        def low_part(dve, t):
            dve.wait_ge(ht_high, t + 1)
            dve.tensor_tensor(ht_lo[:, :, t * P:(t + 1) * P], turned_banks(t),
                              ht_hi[:, :, t * P:(t + 1) * P].bitcast(F32), ALU.subtract).then_inc(ht_low, 1)

        def load_chunk(sp, c):
            for j in range(PIECES):
                sp.wait_ge(w_split, c * PIECES + (j + 1))
                sp.dma_start(w_raw[:, j], io["w_main"][j * PER_PIECE * P:(j + 1) * PER_PIECE * P, columns(c, N)].rearrange(
                    "(k p) n -> p k n", p=P)).then_inc(w_loaded[j], 16)

        def store_pair(sp, pair, last):
            for half in range(2):
                if not (last and half):
                    load_chunk(sp, pair * 2 + (half + 1))
                for t in range(TILES):
                    g = half * TILES + t
                    sp.wait_ge(evacuated, pair * (2 * TILES) + (BANKS + g + 1))
                    sp.dma_start(io["projected"][t * P:(t + 1) * P, bass.ds(pair * (2 * N) + half * N, N)],
                                 stage[:, g % STAGES]).then_inc(stored[g % STAGES], 16)

        @block.sync
        def _(sp):
            for t in range(TILES):
                if t >= 2:
                    sp.wait_ge(normed, t - 1)
                    if t == SAMPLE:
                        sp.wait_ge(x_zeroed, 1)
                if t < SAMPLE:
                    sp.dma_start(x_in[:, t % 2], io["x_prompt"][t * P:(t + 1) * P, :]).then_inc(x_loaded[t % 2], 16)
                else:
                    sp.dma_start(x_in[0:DEC, t % 2], io["x_sample"]).then_inc(x_loaded[t % 2], 16)
                if t == 0:
                    sp.dma_start(gain[:], io["norm_mix_gain"].partition_broadcast(P)).then_inc(gain_in, 16)
                    sp.dma_start(rank_raw[:], io["w_rank"].rearrange("(k p) n -> p k n", p=P)).then_inc(rank_in, 16)
            sp.wait_ge(squared, TILES)
            load_chunk(sp, 0)
            sp.dma_start(io["x_rows"][SEQ:ROWS, :], x_in[:, SAMPLE % 2]).then_inc(x_kept, 16)
            with sp.Fori(0, CHUNKS // 2 - 1) as pair:
                store_pair(sp, pair, False)
            store_pair(sp, CHUNKS // 2 - 1, True)
            for j in range(STAGES):
                sp.wait_ge(stored[j], 16 + 16 * CHUNKS * TILES // STAGES)
            sp.wait_ge(x_kept, 16)

        @block.gpsimd
        def _(pool):
            pool.memset(rank_hi[:].bitcast(F32), 0.0).then_inc(rank_zero, 1)
            pool.memset(rank_lo[:].bitcast(F32), 0.0).then_inc(rank_zero, 1)
            chain = Chain(pool, rooted)
            for t in range(TILES):
                if t == SAMPLE - 1:
                    pool.wait_ge(normed, SAMPLE - 1)
                    pool.memset(x_in[DEC:P, SAMPLE % 2], 0.0).then_inc(x_zeroed, 1)
                    pool.wait_ge(x_zeroed, 1)
                st = stat[:, t % 2]
                pool.wait_ge(squared, t + 1)
                chain.link(pool.tensor_scalar(st[:, 1:2], st[:, 0:1], 1.0 / D, EPS, ALU.mult, ALU.add))
                chain.mark(pool.tensor_tensor(st[:, 2:3], st[:, 1:2], s.root[:, 0:1], ALU.pow))
            with pool.Fori(0, CHUNKS // 2) as pair:
                for half in range(2):
                    for j in range(PIECES):
                        pool.wait_ge(w_high, pair * (2 * PIECES) + (half * PIECES + j + 1))
                        pool.wait_ge(rank_zero, 2)
                        ks = slice(j * PER_PIECE, (j + 1) * PER_PIECE)
                        pool.tensor_tensor(w_lo[:, half, ks], w_raw[:, j], w_hi[:, half, ks].bitcast(F32),
                                           ALU.subtract).then_inc(w_split, 1)

        @block.scalar
        def _(act):
            act.sem_inc(w_split, PIECES)
            for t in range(TILES):
                act.wait_ge(x_loaded[t % 2], 16 * (t // 2 + 1))
                if t == SAMPLE:
                    act.wait_ge(x_zeroed, 1)
                if t:
                    act.wait_ge(squared, t)
                if t >= 2:
                    act.wait_ge(normed, t - 1)
                act.activation(square, x_in[:, t % 2], ACT.Square, accum_out=stat[:, t % 2, 0:1]).then_inc(squared, 1)
                if t:
                    high_part(act, t - 1)
            high_part(act, TILES - 1)
            act.wait_ge(rank_in, 16)
            act.wait_ge(rank_zero, 2)
            act.activation(rank_hi[:, :, 0:RANK], rank_raw[:], ACT.Copy).then_inc(rank_high, 1)
            with act.Fori(0, CHUNKS // 2) as pair:
                for half in range(2):
                    act.wait_ge(product, pair * (2 * TILES) + TILES * (half + 1))
                    for j in range(PIECES):
                        act.wait_ge(w_loaded[j], pair * 32 + 16 * (half + 1))
                        act.activation(w_hi[:, half, j * PER_PIECE:(j + 1) * PER_PIECE], w_raw[:, j],
                                       ACT.Copy).then_inc(w_high, 1)
            act.wait_ge(rank_product, 1)
            act.activation(s.rank_t[:], banks[0:RANK, 0:3, :].rearrange("p b n -> p (b n)")[:, 0:ROWS],
                           ACT.Copy).then_inc(rank_kept, 1)
            act.wait_ge(rank_kept, 1)

        @block.vector
        def _(dve):
            dve.sem_inc(evacuated, BANKS)
            for j in range(STAGES):
                dve.sem_inc(stored[j], 16)
            dve.wait_ge(gain_in, 16)
            for t in range(TILES):
                st = stat[:, t % 2]
                dve.wait_ge(rooted, 2 * t + 2)
                if t >= 2:
                    dve.wait_ge(turned, t - 1)
                dve.scalar_tensor_tensor(x_norm[:, t % 2], x_in[:, t % 2], st[:, 2:3], gain[:],
                                         ALU.mult, ALU.mult).then_inc(normed, 1)
                if t:
                    low_part(dve, t - 1)
            low_part(dve, TILES - 1)
            dve.wait_ge(rank_high, 1)
            dve.tensor_tensor(rank_lo[:, :, 0:RANK], rank_raw[:], rank_hi[:, :, 0:RANK].bitcast(F32),
                              ALU.subtract).then_inc(rank_low, 1)
            with dve.Fori(0, CHUNKS // 2) as pair:
                for g in range(2 * TILES):
                    dve.wait_ge(product, pair * (2 * TILES) + (2 * TILES + g + 1))
                    dve.wait_ge(stored[g % STAGES], pair * (16 * 2 * TILES // STAGES) + 16 * (g // STAGES + 1))
                    dve.tensor_copy(stage[:, g % STAGES], banks[:, g % BANKS]).then_inc(evacuated, 1)

        @block.tensor
        def _(pe):
            pe.sem_inc(product, 2 * TILES)
            for t in range(TILES):
                pe.wait_ge(normed, t + 1)
                if t >= 2:
                    pe.wait_ge(ht_low, t - 1)
                for k in range(KD):
                    last = pe.transpose(turned_banks(t)[:, k], x_norm[:, t % 2, k * P:(k + 1) * P], s.ident[:])
                last.then_inc(turned, 1)
            pe.wait_ge(ht_low, TILES)
            with pe.Fori(0, CHUNKS // 2) as pair:
                for half in range(2):
                    pe.wait_ge(w_split, pair * (2 * PIECES) + PIECES * (half + 2))
                    for t in range(TILES):
                        g = half * TILES + t
                        rows = slice(t * P, (t + 1) * P)
                        pe.wait_ge(evacuated, pair * (2 * TILES) + (g + 1))
                        for k in range(KD):
                            out = banks[:, g % BANKS]
                            pe.matmul(out, ht_hi[:, k, rows], w_hi[:, half, k], start=(k == 0), stop=False)
                            pe.matmul(out, ht_hi[:, k, rows], w_lo[:, half, k], start=False, stop=False)
                            last = pe.matmul(out, ht_lo[:, k, rows], w_hi[:, half, k], start=False, stop=(k == KD - 1))
                        last.then_inc(product, 1)
            pe.wait_ge(rank_low, 1)
            pe.wait_ge(evacuated, BANKS + CHUNKS * TILES)
            for b, width in enumerate((N, N, P)):
                cols = slice(b * N, b * N + width)
                for k in range(KD):
                    out = banks[:, b, 0:width]
                    pe.matmul(out, rank_hi[:, k], ht_hi[:, k, cols], start=(k == 0), stop=False)
                    pe.matmul(out, rank_hi[:, k], ht_lo[:, k, cols], start=False, stop=False)
                    last = pe.matmul(out, rank_lo[:, k], ht_hi[:, k, cols], start=False, stop=(k == KD - 1))
            last.then_inc(rank_product, 1)


def stick(nc, s, io):
    CHUNK = 4
    LAG_T, LAG_AV = 4, 5
    Z, KEEP, BETA, W, WT, PROD, TB = 3, 3, 4, 4, 3, 3, 2
    NAT_K, NAT_C, NATS = TILES, 2 * TILES, 2 * TILES + PROMPT_TILES
    GROUP_STARTS = list(range(0, NATS, 4))
    chunks = []
    for i in range(TILES):
        starts = [i] + list(range(0, i, CHUNK)) [::-1] if i == SAMPLE else list(range(0, i + 1, CHUNK))[::-1]
        ends = [i + 1] + starts[:-1]
        chunks += [(i, a, b - a) for a, b in zip(starts, ends)]
    PER_PAIR = 2 * len(chunks)
    PER_BODY = 2 * PER_PAIR
    UNITS_BODY = 4 * TILES

    def work(u):
        return (u // PER_PAIR, u % PER_PAIR // len(chunks), *chunks[u % len(chunks)])

    steps = []
    turns = 0
    for step in range(PER_BODY + LAG_AV):
        ev = {"z": None, "t": None, "prep": None, "av": None}
        if step < PER_BODY:
            ev["z"] = step
        if 0 <= step - LAG_T < PER_BODY:
            ev["t"] = (step - LAG_T, turns)
            turns += 1
        half, local = divmod(step, PER_PAIR)
        if half < 2 and local % 3 == 1 and 4 <= local < 4 + 3 * len(GROUP_STARTS):
            ev["prep"] = (half, (local - 4) // 3, turns)
            turns += 1
        if step >= LAG_AV:
            ev["av"] = step - LAG_AV
        steps.append(ev)
    turn_of = {ev["t"][0]: ev["t"][1] for ev in steps if ev["t"]}
    PREPS = len(GROUP_STARTS)
    pair_one_ready = max(ev["prep"][2] for ev in steps if ev["prep"] and ev["prep"][0] == 0) + 1
    assert turns % TB == 0 and PER_BODY % Z == 0 and PER_BODY % W == 0 and UNITS_BODY % PROD == 0 and PREPS % 2 == 1

    with ExitStack() as ctx:
        sb = lambda name, shape, dt=F32: ctx.enter_context(nc.sbuf_tensor(name, shape, dt))
        sem = semaphores(nc, ctx)
        nat = sb("nat_qk", [P, 2, NATS, P])
        nat_v = sb("nat_v", [P, 2, TILES + PROMPT_TILES, P])
        qk_hi = sb("qk_hi", [P, 2, NATS * P], F32R)
        qk_lo = sb("qk_lo", [P, 2, NATS * P], F32R)
        keep = sb("keep", [P, KEEP, CHUNK * P])
        beta = sb("beta", [P, BETA, CHUNK * P])
        weight = sb("weight", [P, W, CHUNK * P])
        weight_t = sb("weight_t", [P, WT, CHUNK * P])
        prod = sb("prod", [P, PROD, ROWS + 1])
        o_nat = sb("o_nat_b", [P, 2, TILES, P])
        z_bank = ctx.enter_context(nc.psum_tensor("z_bank", [P, Z, N], F32))
        t_bank = ctx.enter_context(nc.psum_tensor("t_bank", [P, TB, N], F32))
        o_bank = ctx.enter_context(nc.psum_tensor("o_bank", [P, 2, N], F32))
        o_last = ctx.enter_context(nc.psum_tensor("o_last", [P, 2, DH], F32))

        qk_loaded = [sem("qk_loaded0"), sem("qk_loaded1")]
        v_loaded = [sem("v_loaded0"), sem("v_loaded1")]
        ones_set = sem("ones_set")
        scored = sem("scored")
        kept = sem("kept")
        betaed = sem("betaed")
        scanned = sem("scanned")
        weighed = sem("weighed")
        turned = sem("turned_b")
        high = sem("qk_high")
        moved = sem("moved")
        attended = sem("attended")
        o_moved = sem("o_moved")
        o_stored = [sem("o_stored0"), sem("o_stored1")]
        kv_out = sem("kv_out")
        block = ctx.enter_context(nc.Block())

        def last_before(u):
            pair, head, i, _, _ = work(u)
            unit = (pair * 2 + head) * TILES + i - PROD
            return max([v + 1 for v in range(u) if unit_of(v) <= unit], default=0)

        def unit_of(u):
            pair, head, i, _, _ = work(u)
            return (pair * 2 + head) * TILES + i

        def key_columns(i, a, n):
            first = NAT_C + a if i == SAMPLE and a < SAMPLE else NAT_K + a
            return slice(first * P, (first + n) * P)

        def load_qk(sp, col, half):
            for j, (src, at, first, n) in enumerate((
                    (io["projected"], COL_QB, 0, TILES), (io["projected"], COL_KB, NAT_K, TILES),
                    (io["cache_k"], 0, NAT_C, PROMPT_TILES))):
                sp.dma_start(nat[:, half, first:first + n], src[:, bass.ds(col + at, P)].rearrange(
                    "(t p) c -> p t c", p=P)).then_inc(qk_loaded[half], 16)

        def load_v(sp, col, half):
            for src, at, first, n in ((io["projected"], COL_VB, 0, TILES), (io["cache_v"], 0, TILES, PROMPT_TILES)):
                sp.dma_start(nat_v[:, half, first:first + n], src[:, bass.ds(col + at, P)].rearrange(
                    "(t p) c -> p t c", p=P)).then_inc(v_loaded[half], 16)

        @block.sync
        def _(sp):
            for half in range(2):
                load_qk(sp, half * P, half)
                load_v(sp, half * P, half)
            for at, prompt, sample in ((COL_KB, io["k_prompt"], io["k_sample"]), (COL_VB, io["v_prompt"], io["v_sample"])):
                sp.dma_start(prompt.rearrange("a b s h d -> (a b s) (h d)"),
                             io["projected"][0:SEQ, at:at + MIX]).then_inc(kv_out, 16)
                sp.dma_start(sample.rearrange("a b s h d -> (a b s) (h d)"),
                             io["projected"][SEQ:SEQ + DEC, at:at + MIX]).then_inc(kv_out, 16)
            with sp.Fori(0, PAIRS // 2) as body:
                for half in range(2):
                    col = (body * -2 + (2 + half)) * P
                    out_col = body * (2 * P) + (half * P + MIX)
                    sp.wait_ge(moved, body * turns + (TB + PREPS + (pair_one_ready if half else 0)))
                    load_qk(sp, col, half)
                    sp.wait_ge(attended, body * PER_BODY + (WT + PER_PAIR * (half + 1)))
                    load_v(sp, col, half)
                    sp.wait_ge(o_moved, body * 8 + (4 + 4 * (half + 1)))
                    sp.dma_start(io["mixed"][:, bass.ds(out_col, P)].rearrange(
                        "(t p) c -> p t c", p=P), o_nat[:, half]).then_inc(o_stored[half], 16)
            for half in range(2):
                sp.wait_ge(o_stored[half], 16 + 16 * (PAIRS // 2))
                sp.wait_ge(qk_loaded[half], 48 * (PAIRS // 2 + 1))
                sp.wait_ge(v_loaded[half], 32 * (PAIRS // 2 + 1))
            sp.wait_ge(kv_out, 64)

        def sigmoids(act, body, u):
            _, _, i, a, n = work(u)
            act.wait_ge(scored, body * PER_BODY + (u + 1))
            act.wait_ge(scanned, body * PER_BODY + (u + 1))
            act.activation(keep[:, u % KEEP, 0:n * P], z_bank[:, u % Z, 0:n * P], ACT.Sigmoid,
                           scale=-DH ** -0.5).then_inc(kept, 1)
            act.wait_ge(weighed, body * PER_BODY + (u + 1))
            act.activation(beta[:, u % BETA, 0:n * P], z_bank[:, u % Z, 0:n * P], ACT.Sigmoid,
                           scale=DH ** -0.5).then_inc(betaed, 1)

        def prep_columns(group):
            first = GROUP_STARTS[group]
            return first, min(4, NATS - first)

        def high_part(act, half, group, turn, turn_count):
            first, n = prep_columns(group)
            act.wait_ge(turned, turn_count)
            act.activation(qk_hi[:, half, first * P:(first + n) * P], t_bank[:, turn % TB, 0:n * P],
                           ACT.Copy).then_inc(high, 1)

        def output(act, body, u):
            pair, head, i, a, n = work(u)
            if a or i < PROMPT_TILES - 1:
                return
            act.wait_ge(attended, body * PER_BODY + (WT + u + 1))
            act.wait_ge(o_stored[pair], body * 16 + 16)
            if i < SAMPLE:
                act.activation(o_nat[:, pair, 0:PROMPT_TILES, head * DH:(head + 1) * DH],
                               o_bank[:, head].rearrange("p (t d) -> p t d", d=DH), ACT.Copy).then_inc(o_moved, 1)
            else:
                act.activation(o_nat[:, pair, SAMPLE, head * DH:(head + 1) * DH], o_last[:, head],
                               ACT.Copy).then_inc(o_moved, 1)

        @block.scalar
        def _(act):
            act.sem_inc(betaed, Z)
            act.sem_inc(o_moved, 4)
            for half in range(2):
                act.sem_inc(o_stored[half], 16)
            for group in range(PREPS):
                high_part(act, 0, group, group, group + 1)
            with act.Fori(0, PAIRS // 2) as body:
                for ev in steps:
                    if ev["z"] is not None:
                        sigmoids(act, body, ev["z"])
                    if ev["prep"]:
                        half, group, turn = ev["prep"]
                        high_part(act, 1 - half, group, turn + PREPS, body * turns + (PREPS + turn + 1))
                    if ev["av"] is not None:
                        output(act, body, ev["av"])

        @block.vector
        def _(dve):
            dve.sem_inc(scanned, KEEP)
            dve.sem_inc(moved, TB)
            dve.memset(prod[:, :, ROWS:ROWS + 1], 1.0).then_inc(ones_set, 1)

            def low_part(half, group, turn, high_count):
                first, n = prep_columns(group)
                cols = slice(first * P, (first + n) * P)
                dve.wait_ge(high, high_count)
                dve.tensor_tensor(qk_lo[:, half, cols], t_bank[:, turn % TB, 0:n * P],
                                  qk_hi[:, half, cols].bitcast(F32), ALU.subtract).then_inc(moved, 1)

            for group in range(PREPS):
                low_part(0, group, group, group + 1)
            dve.wait_ge(ones_set, 1)
            with dve.Fori(0, PAIRS // 2) as body:
                for ev in steps:
                    if ev["z"] is not None:
                        u = ev["z"]
                        pair, head, i, a, n = work(u)
                        unit = (pair * 2 + head) * TILES + i
                        at = ROWS - (i + 1) * P + a * P
                        dve.wait_ge(kept, body * PER_BODY + (u + 1))
                        dve.wait_ge(weighed, body * PER_BODY + (BETA + last_before(u)))
                        if a + n <= i:
                            dve.wait_ge(scanned, body * PER_BODY + (KEEP + u))
                        line = keep[:, u % KEEP, 0:n * P][:, ::-1]
                        dve.tensor_tensor_scan(prod[:, unit % PROD, at:at + n * P][:, ::-1], line, line,
                                               prod[:, unit % PROD, at + n * P:at + n * P + 1], ALU.mult,
                                               ALU.min).then_inc(scanned, 1)
                    if ev["t"]:
                        u, turn = ev["t"]
                        n = work(u)[4]
                        dve.wait_ge(turned, body * turns + (PREPS + turn + 1))
                        dve.wait_ge(attended, body * PER_BODY + (u + 1))
                        dve.tensor_copy(weight_t[:, u % WT, 0:n * P],
                                        t_bank[:, (PREPS + turn) % TB, 0:n * P]).then_inc(moved, 1)
                    if ev["prep"]:
                        half, group, turn = ev["prep"]
                        low_part(1 - half, group, PREPS + turn,
                                 body * (2 * PREPS) + (PREPS + half * PREPS + group + 1))

        @block.gpsimd
        def _(pool):
            pool.sem_inc(weighed, BETA)
            with pool.Fori(0, PAIRS // 2) as body:
                for u in range(PER_BODY):
                    _, _, i, a, n = work(u)
                    at = ROWS - (i + 1) * P + a * P
                    pool.wait_ge(scanned, body * PER_BODY + (KEEP + u + 1))
                    pool.wait_ge(betaed, body * PER_BODY + (Z + u + 1))
                    back = turn_of[u - W] + 1 if u >= W else 0
                    pool.wait_ge(turned, body * turns + (PREPS + back))
                    pool.tensor_tensor(weight[:, u % W, 0:n * P], beta[:, u % BETA, 0:n * P],
                                       prod[:, unit_of(u) % PROD, at + 1:at + 1 + n * P], ALU.mult).then_inc(weighed, 1)

        @block.tensor
        def _(pe):
            pe.sem_inc(attended, WT)

            def prep(half, group, turn, moved_count):
                first, n = prep_columns(group)
                pe.wait_ge(moved, moved_count)
                for j in range(n):
                    last = pe.transpose(t_bank[:, turn % TB, j * P:(j + 1) * P], nat[:, half, first + j], s.ident[:])
                last.then_inc(turned, 1)

            pe.wait_ge(qk_loaded[0], 48)
            for group in range(PREPS):
                prep(0, group, group, group + 1)
            with pe.Fori(0, PAIRS // 2) as body:
                for ev in steps:
                    if ev["z"] is not None:
                        u = ev["z"]
                        pair, head, i, a, n = work(u)
                        if u % PER_PAIR == 0:
                            pe.wait_ge(moved, body * turns + (TB + PREPS + (pair_one_ready if pair else 0)))
                        pe.wait_ge(betaed, body * PER_BODY + (u + 1))
                        rows = slice(head * DH, (head + 1) * DH)
                        q = slice(i * P, (i + 1) * P)
                        keys = key_columns(i, a, n)
                        out = z_bank[:, u % Z, 0:n * P]
                        masked = a + n == i + 1
                        pe.matmul(out, qk_hi[rows, pair, q], qk_hi[rows, pair, keys], start=True, stop=False)
                        pe.matmul(out, qk_hi[rows, pair, q], qk_lo[rows, pair, keys], start=False, stop=False)
                        last = pe.matmul(out, qk_lo[rows, pair, q], qk_hi[rows, pair, keys], start=False, stop=not masked)
                        if masked:
                            last = pe.matmul(z_bank[:, u % Z, (n - 1) * P:n * P], s.ident_b[:], s.later_b[:],
                                             start=False, stop=True)
                        last.then_inc(scored, 1)
                    if ev["t"]:
                        u, turn = ev["t"]
                        n = work(u)[4]
                        pe.wait_ge(weighed, body * PER_BODY + (BETA + u + 1))
                        pe.wait_ge(moved, body * turns + (PREPS + turn + 1))
                        for j in range(n):
                            last = pe.transpose(t_bank[:, (PREPS + turn) % TB, j * P:(j + 1) * P],
                                                weight[:, u % W, j * P:(j + 1) * P], s.ident[:])
                        last.then_inc(turned, 1)
                    if ev["prep"]:
                        half, group, turn = ev["prep"]
                        if group == 0:
                            pe.wait_ge(qk_loaded[1 - half], body * 48 + (48 + 48 * half))
                        prep(1 - half, group, PREPS + turn, body * turns + (PREPS + turn + 1))
                    if ev["av"] is not None:
                        u = ev["av"]
                        pair, head, i, a, n = work(u)
                        if u % PER_PAIR == 0:
                            pe.wait_ge(v_loaded[pair], body * 32 + 32)
                        pe.wait_ge(moved, body * turns + (TB + PREPS + turn_of[u] + 1))
                        if i == 0 or a == SAMPLE:
                            pe.wait_ge(o_moved, body * 8 + 2 * (2 * pair + head) + (2 if i else 1))
                        out = o_last[:, head] if i == SAMPLE else o_bank[:, head, i * DH:(i + 1) * DH]
                        for j in range(n):
                            v = TILES + a + j if i == SAMPLE and a < SAMPLE else a + j
                            last = pe.matmul(out, weight_t[:, u % WT, j * P:(j + 1) * P],
                                             nat_v[:, pair, v, head * DH:(head + 1) * DH],
                                             start=(a + n == i + 1 and j == 0), stop=(a == 0 and j == n - 1))
                        last.then_inc(attended, 1)


def gla(nc, s, io):
    LIMIT = 40.0
    G = 2
    WIDTH = TILES * QK
    SPREAD = [(b, b * N, min(N, WIDTH - b * N)) for b in range((WIDTH + N - 1) // N)]
    with ExitStack() as ctx:
        sb = lambda name, shape, dt=F32: ctx.enter_context(nc.sbuf_tensor(name, shape, dt))
        sem = semaphores(nc, ctx)
        qkvr = sb("qkvr", [P, TILES, COL_QB])
        q, k = qkvr[:, :, 0:QK], qkvr[:, :, QK:2 * QK]
        v, r = qkvr[:, :, 2 * QK:2 * QK + MIX], qkvr[:, :, 2 * QK + MIX:COL_QB]
        gate_up = sb("gate_up", [RANK, QK])
        bias = sb("gate_bias", [P, 2, QK])
        gain = sb("gain_gla", [P, DV])
        gate = sb("gate", [P, WIDTH])
        decay = sb("decay", [P, WIDTH])
        log_a = sb("log_a", [P, WIDTH])
        grow = sb("grow", [P, WIDTH])
        shrink = sb("shrink", [P, WIDTH])
        ends = sb("ends", [P, TILES, G, 2])
        turned_q = sb("turned_q", [P, TILES, 2, G, P])
        turned_k = sb("turned_k", [P, TILES, G, P])
        att = sb("att", [P, TILES, H_A, P])
        clean = sb("att_clean", [P, 2, H_A, P])
        state = sb("state", [P, 2, G, DV])
        state_mid = sb("state_mid", [P, TILES, G, DV])
        added = sb("state_added", [P, G, DV])
        square = sb("square_gla", [P, 2, MIX])
        stat = sb("stat_gla", [P, 3, TILES, H_A])
        swish = sb("swish", [P, TILES, MIX])
        normed = sb("normed_gla", [P, 2, MIX])
        bank = ctx.enter_context(nc.psum_tensor("bank_gla", [P, 8, N], F32))
        flat = bank[:].rearrange("p b n -> p (b n)")

        small_in, qkvr_in, state_in = sem("gla_small_in"), sem("qkvr_in"), sem("state_in")
        gated, biased, gate_act, log_done = sem("gated"), sem("biased"), sem("gate_act"), sem("log_done")
        summed, clamped, grown, ended = sem("summed"), sem("clamped"), sem("grown"), sem("ended")
        scaled, turned, turned_out = sem("scaled"), sem("turned_gla"), sem("turned_out_gla")
        atted, masked, kved = sem("atted"), sem("masked"), sem("kved")
        state_zero, chain_s, stated = sem("state_zero"), sem("chain_state"), sem("stated")
        mixed, squared, summed_sq, rooted = sem("mixed_gla"), sem("squared_gla"), sem("summed_sq"), sem("rooted_gla")
        opened, swish_gain = sem("opened"), sem("swish_gain")
        scaled_o, gated_o = sem("scaled_o"), sem("gated_o")
        zeroed = sem("turned_q_zeroed")
        o_out, state_out = sem("gla_out"), sem("state_out")
        block = ctx.enter_context(nc.Block())

        def attend(pe, t):
            pe.wait_ge(turned_out, 3 * t + 3)
            pe.wait_ge(ended, 1)
            if t >= 2:
                pe.wait_ge(masked, 2 * t - 2)
            for h in range(H_A):
                g, u = divmod(h, 2)
                last = pe.matmul(bank[:, 4 + t % 2, h * P:(h + 1) * P], turned_k[:, t, g], turned_q[:, t, u, g],
                                 start=True, stop=True)
            last.then_inc(atted, 1)

        def mix(pe, t):
            pe.wait_ge(masked, 2 * t + 2)
            pe.wait_ge(stated, t + 1)
            for h in range(H_A):
                g, u = divmod(h, 2)
                out = bank[:, t % 4, h * DV:(h + 1) * DV]
                pe.matmul(out, att[:, t, h], v[:, t, h * DV:(h + 1) * DV], start=True, stop=False)
                last = pe.matmul(out, turned_q[:, t, u, g], state_mid[:, t, g], start=False, stop=True)
            last.then_inc(mixed, 1)

        def squares(act, t):
            act.wait_ge(mixed, t + 1)
            if t >= 2:
                act.wait_ge(summed_sq, t - 1)
            act.activation(square[:, t % 2], bank[:, t % 4], ACT.Square).then_inc(squared, 1)

        def state_step(dve, chain, t):
            j = 1 if t == SAMPLE else 0
            dve.wait_ge(kved, t + 1)
            dve.wait_ge(ended, 1)
            if t == 0:
                dve.wait_ge(state_zero, 1)
            elif t == SAMPLE:
                dve.wait_ge(state_in, 64)
            else:
                dve.wait_ge(stated, t)
            for g in range(G):
                chain.mark(dve.tensor_scalar(state_mid[:, t, g], state[:, j, g], ends[:, t, g, 0:1], None, ALU.mult))
            chain.wait()
            chain.link(dve.tensor_tensor(added[:], bank[:, 6 + t % 2, 0:G * DV].rearrange("p (g v) -> p g v", g=G),
                                         state_mid[:, t], ALU.add))
            chain.link(dve.tensor_scalar(state[:, j, 0], added[:, 0], ends[:, t, 0, 1:2], None, ALU.mult))
            dve.tensor_scalar(state[:, j, 1], added[:, 1], ends[:, t, 1, 1:2], None, ALU.mult).then_inc(stated, 1)

        def output(dve, t):
            dve.wait_ge(squared, t + 1)
            dve.tensor_reduce(stat[:, 0, t], square[:, t % 2].rearrange("p (h v) -> p h v", v=DV), X,
                              ALU.add).then_inc(summed_sq, 1)
            dve.wait_ge(rooted, 2 * t + 2)
            if t >= 2:
                dve.wait_ge(gated_o, t - 1)
            dve.tensor_tensor(normed[:, t % 2].rearrange("p (h v) -> p h v", v=DV),
                              bank[:, t % 4].rearrange("p (h v) -> p h v", v=DV),
                              stat[:, 2, t].unsqueeze(2).to_broadcast([P, H_A, DV]), ALU.mult).then_inc(scaled_o, 1)

        @block.sync
        def _(sp):
            sp.dma_start(gate_up[:], io["w_gate_up"]).then_inc(small_in, 16)
            for j in range(2):
                sp.dma_start(bias[:, j], io["b_gate"].partition_broadcast(P)).then_inc(small_in, 16)
            sp.dma_start(gain[:], io["gla_gain"].partition_broadcast(P)).then_inc(small_in, 16)
            for t in range(TILES):
                sp.dma_start(qkvr[:, t], io["projected"][t * P:(t + 1) * P, 0:COL_QB]).then_inc(qkvr_in, 16)
            for g in range(G):
                for u in range(2):
                    sp.dma_start(state[u * DK:(u + 1) * DK, 1, g], io["state_gla"][2 * g + u]).then_inc(state_in, 16)
            for t in range(TILES):
                sp.wait_ge(gated_o, t + 1)
                sp.dma_start(io["mixed"][t * P:(t + 1) * P, 0:MIX], swish[:, t]).then_inc(o_out, 16)
            sp.wait_ge(stated, TILES)
            for j, out in ((0, io["gla_prompt"]), (1, io["gla_sample"])):
                rows = out.rearrange("a b h k v -> (a b h) k v")
                for g in range(G):
                    for u in range(2):
                        sp.dma_start(rows[2 * g + u], state[u * DK:(u + 1) * DK, j, g]).then_inc(state_out, 16)
            sp.wait_ge(o_out, 16 * TILES)
            sp.wait_ge(state_out, 16 * 8)

        @block.tensor
        def _(pe):
            pe.wait_ge(small_in, 64)
            for t in range(TILES):
                last = pe.matmul(flat[:, t * QK:(t + 1) * QK], s.rank_t[:, t * P:(t + 1) * P], gate_up[:],
                                 start=True, stop=True)
            last.then_inc(gated, 1)
            for b, at, width in SPREAD:
                pe.wait_ge(log_done, b + 1)
                pe.matmul(bank[:, b, 0:width], s.tri_mid[:], log_a[:, at:at + width], start=True,
                          stop=True).then_inc(summed, 1)
            for t in range(TILES):
                spans = s.spans[:, 0:3:2] if t == SAMPLE else s.spans[:, 0:2]
                for g in range(G):
                    at = t * QK + g * P
                    last = pe.matmul(bank[:, 5, 4 * t + 2 * g:4 * t + 2 * g + 2], log_a[:, at:at + P], spans,
                                     start=True, stop=True)
            last.then_inc(summed, 1)
            for t in range(TILES):
                pe.wait_ge(scaled, 2 * t + 2)
                pe.wait_ge(clamped, len(SPREAD))
                if t >= 4:
                    pe.wait_ge(scaled_o, t - 3)
                for j in range(4):
                    last = pe.transpose(bank[:, t % 4, j * P:(j + 1) * P], qkvr[:, t, j * P:(j + 1) * P], s.ident[:])
                last.then_inc(turned, 1)
                if t >= 2:
                    pe.wait_ge(stated, t - 1)
                for h in range(H_A):
                    g, u = divmod(h, 2)
                    last = pe.matmul(bank[u * DK:(u + 1) * DK, 6 + t % 2, g * DV:(g + 1) * DV],
                                     k[:, t, h * DK:(h + 1) * DK], v[:, t, h * DV:(h + 1) * DV], start=True, stop=True)
                last.then_inc(kved, 1)
                if t:
                    attend(pe, t - 1)
                if t > 1:
                    mix(pe, t - 2)
            attend(pe, TILES - 1)
            mix(pe, TILES - 2)
            mix(pe, TILES - 1)

        @block.scalar
        def _(act):
            chain = Chain(act, gate_act)
            act.wait_ge(biased, len(SPREAD))
            chain.link(act.activation(decay[:], gate[:], ACT.Abs))
            chain.link(act.activation(decay[:], decay[:], ACT.Exp, scale=-1.0))
            chain.mark(act.activation(decay[:], decay[:], ACT.Ln, bias=1.0))
            for b, at, width in SPREAD:
                act.wait_ge(clamped, b + 1)
                cols = slice(at, at + width)
                act.activation(grow[:, cols], gate[:, cols], ACT.Exp).then_inc(grown, 1)
                act.activation(shrink[:, cols], gate[:, cols], ACT.Exp, scale=-1.0).then_inc(grown, 1)
            act.wait_ge(summed, len(SPREAD) + 1)
            act.activation(ends[:].rearrange("p t g c -> p (t g c)"), bank[:, 5, 0:4 * TILES], ACT.Exp).then_inc(ended, 1)
            act.wait_ge(qkvr_in, 16 * TILES)
            act.wait_ge(zeroed, 1)
            for t in range(TILES):
                act.activation(swish[:, t], r[:, t], ACT.Sigmoid).then_inc(opened, 1)
            for t in range(TILES):
                if t > 3:
                    squares(act, t - 4)
                act.wait_ge(turned, t + 1)
                blocks = bank[:, t % 4].rearrange("p (j c) -> p j c", c=P)
                for u in range(2):
                    rows = slice(u * DK, (u + 1) * DK)
                    act.activation(turned_q[rows, t, u], blocks[rows, 0:G], ACT.Copy).then_inc(turned_out, 1)
                act.activation(turned_k[:, t], blocks[:, G:2 * G], ACT.Copy).then_inc(turned_out, 1)
            for t in range(TILES - 4, TILES):
                squares(act, t)

        @block.vector
        def _(dve):
            dve.wait_ge(small_in, 64)
            dve.wait_ge(gated, 1)
            for b, at, width in SPREAD:
                dve.tensor_tensor(gate[:, at:at + width], bank[:, b, 0:width],
                                  bias[:].rearrange("p a n -> p (a n)")[:, 0:width], ALU.add).then_inc(biased, 1)
            dve.memset(state[:, 0], 0.0).then_inc(state_zero, 1)
            dve.wait_ge(gate_act, 3)
            for b, at, width in SPREAD:
                cols = slice(at, at + width)
                dve.scalar_tensor_tensor(log_a[:, cols], gate[:, cols], 0.0, decay[:, cols], ALU.min,
                                         ALU.subtract).then_inc(log_done, 1)
            dve.wait_ge(log_done, len(SPREAD))
            for b, at, width in SPREAD:
                dve.wait_ge(summed, b + 1)
                dve.tensor_scalar(gate[:, at:at + width], bank[:, b, 0:width], -LIMIT, LIMIT, ALU.max,
                                  ALU.min).then_inc(clamped, 1)
            chain = Chain(dve, chain_s)
            for t in range(TILES + 2):
                if t < TILES:
                    cols = slice(t * QK, (t + 1) * QK)
                    dve.wait_ge(qkvr_in, 16 * TILES)
                    dve.wait_ge(grown, 2 * (t * QK // N + 1))
                    dve.scalar_tensor_tensor(q[:, t], q[:, t], DK ** -0.5, grow[:, cols], ALU.mult,
                                             ALU.mult).then_inc(scaled, 1)
                    dve.tensor_tensor(k[:, t], k[:, t], shrink[:, cols], ALU.mult).then_inc(scaled, 1)
                if 1 <= t <= TILES:
                    state_step(dve, chain, t - 1)
                if t >= 2:
                    u = t - 2
                    dve.wait_ge(atted, u + 1)
                    if u >= 2:
                        dve.wait_ge(masked, 2 * u - 2)
                    dve.tensor_scalar(clean[:, u % 2], bank[:, 4 + u % 2].rearrange("p (h c) -> p h c", c=P), -3e38,
                                      3e38, ALU.max, ALU.min).then_inc(masked, 1)
                    dve.wait_ge(masked, 2 * u + 1)
                    dve.tensor_tensor(att[:, u], clean[:, u % 2],
                                      s.causal[:].unsqueeze(1).to_broadcast([P, H_A, P]), ALU.mult).then_inc(masked, 1)
                    if u >= 2:
                        output(dve, u - 2)
            output(dve, TILES - 2)
            output(dve, TILES - 1)

        @block.gpsimd
        def _(pool):
            pool.memset(turned_q[:], 0.0).then_inc(zeroed, 1)
            pool.wait_ge(small_in, 64)
            for t in range(TILES):
                pool.wait_ge(summed_sq, t + 1)
                pool.tensor_scalar(stat[:, 1, t], stat[:, 0, t], 1.0 / DV, EPS, ALU.mult, ALU.add).then_inc(rooted, 1)
                pool.wait_ge(rooted, 2 * t + 1)
                pool.tensor_tensor(stat[:, 2, t], stat[:, 1, t], s.root[:], ALU.pow).then_inc(rooted, 1)
                pool.wait_ge(opened, t + 1)
                pool.tensor_tensor(swish[:, t], swish[:, t], r[:, t], ALU.mult).then_inc(swish_gain, 1)
                pool.wait_ge(swish_gain, 2 * t + 1)
                heads = swish[:, t].rearrange("p (h v) -> p h v", v=DV)
                pool.tensor_tensor(heads, heads, gain[:].unsqueeze(1).to_broadcast([P, H_A, DV]),
                                   ALU.mult).then_inc(swish_gain, 1)
                pool.wait_ge(swish_gain, 2 * t + 2)
                pool.wait_ge(scaled_o, t + 1)
                pool.tensor_tensor(swish[:, t], swish[:, t], normed[:, t % 2], ALU.mult).then_inc(gated_o, 1)


def merge(nc, s, io):
    RAW, PIECES = 2, 2 * KD
    with ExitStack() as ctx:
        sb = lambda name, shape, dt=F32: ctx.enter_context(nc.sbuf_tensor(name, shape, dt))
        sem = semaphores(nc, ctx)
        w_raw = sb("wm_raw", [P, RAW, D])
        w_hi = sb("wm_hi", [P, 2, KD, D], F32R)
        w_lo = sb("wm_lo", [P, 2, KD, D], F32R)
        o_nat = sb("o_nat", [P, D])
        o_hi, o_lo = sb("o_hi", [P, KD, P], F32R), sb("o_lo", [P, KD, P], F32R)
        gates = sb("gates", [P, 2 * D])
        m, m_b = sb("m", [P, D]), sb("m_b", [P, D])
        m_hi, m_lo = sb("m_hi", [P, KD, P], F32R), sb("m_lo", [P, KD, P], F32R)
        x_t, x_new, h_new = sb("x_t", [P, D]), sb("x_new", [P, D]), sb("h_new", [P, D])
        h_turned = sb("h_turned", [P, KD, P])
        gain = sb("gain_ffn", [P, D])
        w_route, b_route = sb("w_route", [P, KD, ROUTES]), sb("b_route", [P, ROUTES])
        stat = sb("stat_ffn", [P, 3])
        square = w_raw[:, 0]
        logits, open_l = sb("logits", [P, ROUTES]), sb("open_l", [P, EXPERTS])
        cand, peak = sb("cand", [P, EXPERTS]), sb("peak", [P, 4])
        group_hot = sb("group_hot", [P, GROUPS])
        both = sb("both", [P, EXPERTS], BF16)
        place, picked = sb("place", [P, EXPERTS]), sb("picked", [P, 2, EXPERTS])
        slot_f = sb("slot_f", [P, 2, 2])
        slot = sb("slot", [P, TILES, 2], I32)
        late_slot, late_f = sb("late_slot", [P, TILES, 2], I32), sb("late_f", [P, TILES, 2])
        late_pick = m_b[:, 0:2 * TILES * EXPERTS].rearrange("p (c e) -> p c e", e=EXPERTS)
        empty = sb("empty", [P, BLOCKS + 1], I32)
        blocks_i, blocks_f = sb("blocks_i", [P, EXPERTS], I32), sb("blocks_f", [P, 4, EXPERTS])
        behind = m[0:1, 0:(BLOCKS - EXPERTS) * EXPERTS].rearrange("p (b e) -> p b e", e=EXPERTS)
        owner_f = sb("owner_f", [1, BLOCKS])
        y = ctx.enter_context(nc.psum_tensor("y_bank", [P, 2, D], F32))
        turn = ctx.enter_context(nc.psum_tensor("turn_bank", [P, KD, P], F32))
        out = ctx.enter_context(nc.psum_tensor("out_bank", [P, D], F32))

        small_in = sem("merge_small_in")
        w_loaded = [sem(f"wm_loaded{j}") for j in range(RAW)]
        w_high, w_split = sem("wm_high"), sem("wm_split")
        o_in, gates_in, x_in = sem("o_in"), sem("gates_in"), sem("x_in_merge")
        o_turned, o_high, o_low = sem("o_turned"), sem("o_high"), sem("o_low")
        opened, a_done, b_done, m_chain, m_done = (sem("gates_open"), sem("branch_a"), sem("branch_b"), sem("m_chain"),
                                                   sem("m_done"))
        m_turned, m_high, m_low, out_done = sem("m_turned"), sem("m_high"), sem("m_low"), sem("out_done")
        x_done, squared, meaned, rooted, h_done = (sem("x_done"), sem("squared_ffn"), sem("meaned"), sem("rooted_ffn"),
                                                   sem("h_done"))
        h_turned_s, h_out, routed, logits_read = sem("h_turned_s"), sem("h_out"), sem("routed"), sem("logits_read")
        route_chain, hot_done, counted, counts_read = (sem("route_chain"), sem("hot_done"), sem("counted"),
                                                       sem("counts_read"))
        place_chain, slots_ready, late_chain = sem("place_chain"), sem("slots_ready"), sem("late_chain")
        x_stored, h_stored, cleared = sem("x_stored"), sem("h_stored"), sem("carry_cleared")
        empty_set, table_cleared, scattered, late_ready = (sem("empty_set"), sem("table_cleared"), sem("scattered"),
                                                           sem("late_ready"))
        block = ctx.enter_context(nc.Block())

        def load_tile(sp, t, kind, sample=False):
            if kind == "o":
                sp.dma_start(o_nat[:], io["mixed"][bass.ds(t * P, P), :]).then_inc(o_in, 16)
            elif kind == "gates":
                sp.dma_start(gates[:], io["projected"][bass.ds(t * P, P), COL_GATES:MAIN]).then_inc(gates_in, 16)
            else:
                src = io["x_rows"] if sample else io["x_prompt"]
                sp.dma_start(x_t[:], src[bass.ds(t * P, P), :]).then_inc(x_in, 16)

        def feed(sp, t, sample_next=False, last=False):
            if not last:
                sp.wait_ge(o_turned, t + 1)
                load_tile(sp, t + 1, "o")
                sp.wait_ge(m_done, t + 1)
                load_tile(sp, t + 1, "gates")
            sp.wait_ge(x_done, t + 1)
            sp.dma_start(io["x_mid"][bass.ds(t * P, P), :], x_new[:]).then_inc(x_stored, 16)
            if not last:
                load_tile(sp, t + 1, "x", sample_next)
            sp.wait_ge(h_done, t + 1)
            sp.dma_start(io["h_mid"][bass.ds(t * P, P), :], h_new[:]).then_inc(h_stored, 16)

        @block.sync
        def _(sp):
            load_tile(sp, 0, "o")
            load_tile(sp, 0, "gates")
            load_tile(sp, 0, "x")
            for j in range(PIECES):
                src = (io["w_branch"], io["w_out"])[j // KD]
                if j >= RAW:
                    sp.wait_ge(w_split, j - RAW + 1)
                sp.dma_start(w_raw[:, j % RAW], src[j % KD * P:(j % KD + 1) * P, :]).then_inc(w_loaded[j % RAW], 16)
                if j == 0:
                    sp.dma_start(gain[:], io["norm_ffn_gain"].partition_broadcast(P)).then_inc(small_in, 16)
                    sp.dma_start(b_route[:], io["b_router"].partition_broadcast(P)).then_inc(small_in, 16)
                    sp.dma_start(w_route[:], io["w_router"].rearrange("(k p) n -> p k n", p=P)).then_inc(small_in, 16)
            with sp.Fori(0, SAMPLE - 1) as t:
                feed(sp, t)
            feed(sp, SAMPLE - 1, sample_next=True)
            feed(sp, SAMPLE, last=True)
            sp.wait_ge(x_stored, 16 + 16 * TILES)
            sp.wait_ge(h_stored, 16 + 16 * TILES)

        def branch(pe, which):
            for n in range(D // N):
                cols = slice(n * N, (n + 1) * N)
                for k in range(which * KD // 2, (which + 1) * KD // 2):
                    first, final = k % 4 == 0, k % 4 == 3
                    pe.matmul(y[:, which, cols], o_hi[:, k], w_hi[:, 0, k, cols], start=first, stop=False)
                    pe.matmul(y[:, which, cols], o_hi[:, k], w_lo[:, 0, k, cols], start=False, stop=False)
                    last = pe.matmul(y[:, which, cols], o_lo[:, k], w_hi[:, 0, k, cols], start=False, stop=final)
            return last

        def turned(pe, source):
            for k in range(KD):
                last = pe.transpose(turn[:, k], source[:, k * P:(k + 1) * P], s.ident[:])
            return last

        def output_half(pe, n):
            cols = slice(n * N, (n + 1) * N)
            for k in range(KD):
                pe.matmul(out[:, cols], m_hi[:, k], w_hi[:, 1, k, cols], start=(k == 0), stop=False)
                pe.matmul(out[:, cols], m_hi[:, k], w_lo[:, 1, k, cols], start=False, stop=False)
                last = pe.matmul(out[:, cols], m_lo[:, k], w_hi[:, 1, k, cols], start=False, stop=(k == KD - 1))
            return last

        def turn_h(pe, t):
            pe.wait_ge(h_done, t + 1)
            turned(pe, h_new).then_inc(h_turned_s, 1)

        def route(pe, t):
            pe.wait_ge(h_out, t + 1)
            for k in range(KD):
                last = pe.matmul(out[:, 0:ROUTES], h_turned[:, k], w_route[:, k], start=(k == 0), stop=(k == KD - 1))
            last.then_inc(routed, 1)

        def count(pe, t):
            pe.wait_ge(hot_done, t + 1)
            pe.matmul(y[:, 0, 0:EXPERTS], s.before_b[:], both[:], start=True, stop=True)
            pe.matmul(y[:, 0, EXPERTS:2 * EXPERTS], s.ones_b[:], both[:], start=True, stop=True).then_inc(counted, 1)

        def tile_pe(pe, t, first=False, last=False):
            pe.wait_ge(o_low, t + 1)
            if not first:
                pe.wait_ge(counts_read, t - 1)
            branch(pe, 0).then_inc(a_done, 1)
            if not first:
                turn_h(pe, t - 1)
            branch(pe, 1).then_inc(b_done, 1)
            if not first:
                route(pe, t - 1)
            pe.wait_ge(m_done, t + 1)
            turned(pe, m).then_inc(m_turned, 1)
            pe.wait_ge(m_low, t + 1)
            if first:
                pe.wait_ge(w_split, PIECES)
            else:
                pe.wait_ge(logits_read, t)
            output_half(pe, 0)
            if not last:
                pe.wait_ge(o_in, t * 16 + 32)
                turned(pe, o_nat).then_inc(o_turned, 1)
            output_half(pe, 1).then_inc(out_done, 1)
            if not first:
                count(pe, t - 1)

        @block.tensor
        def _(pe):
            pe.wait_ge(o_in, 16)
            turned(pe, o_nat).then_inc(o_turned, 1)
            pe.wait_ge(w_split, KD)
            tile_pe(pe, 0, first=True)
            with pe.Fori(1, SAMPLE) as t:
                tile_pe(pe, t)
            tile_pe(pe, SAMPLE, last=True)
            turn_h(pe, SAMPLE)
            pe.wait_ge(small_in, 48)
            route(pe, SAMPLE)
            count(pe, SAMPLE)

        def h_evac(act, t):
            act.wait_ge(h_turned_s, t + 1)
            act.activation(h_turned[:], turn[:], ACT.Copy).then_inc(h_out, 1)

        def tile_act(act, t, first=False, last=False):
            if not first:
                h_evac(act, t - 1)
            act.wait_ge(m_turned, t + 1)
            act.activation(m_hi[:], turn[:], ACT.Copy).then_inc(m_high, 1)
            if not last:
                act.wait_ge(gates_in, t * 16 + 32)
                act.activation(gates[:], gates[:], ACT.Sigmoid).then_inc(opened, 1)
                act.wait_ge(o_turned, t + 2)
                act.activation(o_hi[:], turn[:], ACT.Copy).then_inc(o_high, 1)
            act.wait_ge(x_done, t + 1)
            act.wait_ge(meaned, t + 1)
            act.activation(square, x_new[:], ACT.Square, accum_out=stat[:, 0:1]).then_inc(squared, 1)

        @block.scalar
        def _(act):
            act.sem_inc(x_stored, 16)
            act.sem_inc(h_stored, 16)
            act.sem_inc(meaned, 1)
            for j in range(PIECES):
                if j == 1:
                    act.wait_ge(gates_in, 16)
                    act.activation(gates[:], gates[:], ACT.Sigmoid).then_inc(opened, 1)
                    act.wait_ge(o_turned, 1)
                    act.activation(o_hi[:], turn[:], ACT.Copy).then_inc(o_high, 1)
                act.wait_ge(w_loaded[j % RAW], 16 * (j // RAW + 1))
                act.activation(w_hi[:, j // KD, j % KD], w_raw[:, j % RAW], ACT.Copy).then_inc(w_high, 1)
            act.wait_ge(w_split, PIECES)
            tile_act(act, 0, first=True)
            with act.Fori(1, SAMPLE) as t:
                tile_act(act, t)
            tile_act(act, SAMPLE, last=True)
            h_evac(act, SAMPLE)

        def first_peak(dve, chain, values, width, top, number, iota):
            chain.link(dve.tensor_reduce(top, values, X, ALU.max))
            chain.link(dve.tensor_scalar(cand[:, 0:width], values, top, 64.0, ALU.is_lt, ALU.mult))
            chain.link(dve.tensor_tensor(cand[:, 0:width], cand[:, 0:width], iota, ALU.add))
            chain.link(dve.tensor_reduce(number, cand[:, 0:width], X, ALU.min))

        def choose(dve, t, base):
            chain = Chain(dve, route_chain, base)
            iota_e, iota_g = s.iota[:, 0:EXPERTS], s.iota[:, EXPERTS:]
            first_peak(dve, chain, logits[:, EXPERTS:], GROUPS, peak[:, 0:1], peak[:, 1:2], iota_g)
            chain.mark(dve.tensor_scalar(s.group_rel[:, bass.ds(t, 1)].rearrange("p a g -> p (a g)"), logits[:, EXPERTS:],
                                         peak[:, 0:1], None, ALU.subtract))
            chain.link(dve.tensor_scalar(group_hot[:], iota_g, peak[:, 1:2], None, ALU.is_equal))
            chain.link(dve.tensor_scalar(group_hot[:], group_hot[:], -1.0, -MASKED, ALU.add, ALU.mult))
            chain.link(dve.tensor_tensor(open_l[:].rearrange("p (g e) -> p g e", e=PER_GROUP),
                                         logits[:, 0:EXPERTS].rearrange("p (g e) -> p g e", e=PER_GROUP),
                                         group_hot[:].unsqueeze(2).to_broadcast([P, GROUPS, PER_GROUP]), ALU.add))
            for j in range(2):
                number = s.number[:, bass.ds(t * 2 + j, 1)]
                first_peak(dve, chain, open_l[:], EXPERTS, peak[:, 2 + j:3 + j], number, iota_e)
                hot = s.hot[:, bass.ds(t * 2 + j, 1)].rearrange("p a e -> p (a e)")
                chain.link(dve.tensor_scalar(hot, iota_e, number, None, ALU.is_equal))
                if j == 0:
                    chain.link(dve.scalar_tensor_tensor(open_l[:], hot, 3 * MASKED, open_l[:], ALU.mult, ALU.add))
            chain.mark(dve.tensor_tensor(s.gap[:, bass.ds(t, 1)], peak[:, 2:3], peak[:, 3:4], ALU.subtract))
            hots = s.hot[:, bass.ds(t * 2, 2)]
            chain.link(dve.tensor_scalar(hots, hots, s.valid[:, bass.ds(t, 1)], None, ALU.mult))
            dve.tensor_tensor(both[:], s.hot[:, bass.ds(t * 2, 1)].rearrange("p a e -> p (a e)"),
                              s.hot[:, bass.ds(t * 2 + 1, 1)].rearrange("p a e -> p (a e)"), ALU.add).then_inc(hot_done, 1)
            return chain.count

        def assign(dve, t, base):
            chain = Chain(dve, place_chain, base)
            dve.wait_ge(counted, t + 1)
            chain.link(dve.tensor_tensor(place[:], y[:, 0, 0:EXPERTS], s.carry[:], ALU.add))
            dve.tensor_tensor(s.carry[:], s.carry[:], y[:, 0, EXPERTS:2 * EXPERTS], ALU.add).then_inc(counts_read, 1)
            chain.link(dve.tensor_tensor(picked[:], s.hot[:, bass.ds(t * 2, 2)],
                                         place[:].unsqueeze(1).to_broadcast([P, 2, EXPERTS]), ALU.mult))
            at = s.at[:, bass.ds(t * 2, 2)]
            chain.link(dve.tensor_reduce(at, picked[:], X, ALU.add))
            chain.mark(dve.tensor_scalar(slot_f[:, 0], at, float(P), float(NOWHERE), ALU.is_ge, ALU.mult))
            chain.link(dve.scalar_tensor_tensor(slot_f[:, 1], s.number[:, bass.ds(t * 2, 2)], float(P), at, ALU.mult,
                                                ALU.add))
            dve.scalar_tensor_tensor(slot[:, bass.ds(t, 1)].rearrange("p a k -> p (a k)"), slot_f[:, 0],
                                     s.nowhere[:, bass.ds(t, 1)], slot_f[:, 1], ALU.add, ALU.add).then_inc(slots_ready, 1)
            return chain.count

        ROUTE_LINKS, PLACE_LINKS = 21, 5

        def read_logits(dve, t):
            dve.wait_ge(routed, t + 1)
            dve.tensor_tensor(logits[:], out[:, 0:ROUTES], b_route[:], ALU.add).then_inc(logits_read, 1)

        def tile_dve(dve, t, first=False, last=False):
            chain = Chain(dve, m_chain, t * 2)
            dve.wait_ge(a_done, t + 1)
            dve.wait_ge(opened, t + 1)
            chain.mark(dve.tensor_tensor(m[:], y[:, 0], gates[:, 0:D], ALU.mult))
            dve.wait_ge(b_done, t + 1)
            chain.link(dve.tensor_tensor(m_b[:], y[:, 1], gates[:, D:], ALU.mult))
            dve.tensor_tensor(m[:], m[:], m_b[:], ALU.add).then_inc(m_done, 1)
            if not first:
                read_logits(dve, t - 1)
            dve.wait_ge(m_high, t + 1)
            dve.tensor_tensor(m_lo[:], turn[:], m_hi[:].bitcast(F32), ALU.subtract).then_inc(m_low, 1)
            if not first:
                dve.wait_ge(logits_read, t)
                assert choose(dve, t - 1, (t - 1) * ROUTE_LINKS) == ROUTE_LINKS
            if not last:
                dve.wait_ge(o_high, t + 2)
                dve.tensor_tensor(o_lo[:], turn[:], o_hi[:].bitcast(F32), ALU.subtract).then_inc(o_low, 1)
            dve.wait_ge(out_done, t + 1)
            dve.wait_ge(x_in, t * 16 + 16)
            dve.wait_ge(x_stored, t * 16 + 16)
            dve.tensor_tensor(x_new[:], out[:], x_t[:], ALU.add).then_inc(x_done, 1)
            dve.wait_ge(squared, t + 1)
            dve.tensor_scalar(stat[:, 1:2], stat[:, 0:1], 1.0 / D, EPS, ALU.mult, ALU.add).then_inc(meaned, 1)
            dve.wait_ge(rooted, t + 1)
            dve.wait_ge(h_stored, t * 16 + 16)
            dve.scalar_tensor_tensor(h_new[:], x_new[:], stat[:, 2:3], gain[:], ALU.mult, ALU.mult).then_inc(h_done, 1)
            if not first:
                assert assign(dve, t - 1, (t - 1) * PLACE_LINKS) == PLACE_LINKS

        def late(dve):
            chain = Chain(dve, late_chain)
            dve.wait_ge(counts_read, TILES)
            dve.wait_ge(place_chain, TILES * PLACE_LINKS)
            extra, upto, start, zero = (blocks_f[:, j] for j in range(4))
            chain.link(dve.tensor_scalar(blocks_i[:], s.carry[:], float(P - 1), None, ALU.add))
            chain.link(dve.tensor_scalar(blocks_i[:], blocks_i[:], 7, None, ALU.arith_shift_right))
            chain.link(dve.tensor_scalar(extra, blocks_i[:], -1.0, 0.0, ALU.add, ALU.max))
            chain.link(dve.memset(zero, 0.0))
            chain.link(dve.tensor_tensor_scan(upto, extra, zero, zero[:, 0:1], ALU.add, ALU.add))
            chain.link(dve.tensor_tensor(start, upto, extra, ALU.subtract))
            chain.link(dve.tensor_scalar(start, start, float(EXPERTS - 1), float(P), ALU.add, ALU.mult))
            chain.link(dve.tensor_tensor(late_pick, s.hot[:], start.unsqueeze(1).to_broadcast([P, 2 * TILES, EXPERTS]),
                                         ALU.mult))
            pick = late_f[:].rearrange("p t k -> p (t k)")
            chain.link(dve.tensor_reduce(pick, late_pick, X, ALU.add))
            chain.link(dve.tensor_tensor(pick, pick, s.at[:], ALU.add))
            early = late_pick[:, 0, 0:2 * TILES]
            chain.link(dve.tensor_scalar(early, s.at[:], float(P), float(NOWHERE), ALU.is_lt, ALU.mult))
            chain.link(dve.tensor_tensor(late_slot[:].rearrange("p t k -> p (t k)"), pick, early, ALU.add))
            more = BLOCKS - EXPERTS
            chain.link(dve.tensor_tensor(behind, upto[0:1, :].unsqueeze(1).to_broadcast([1, more, EXPERTS]),
                                         s.iota[0:1, 0:more].unsqueeze(2).to_broadcast([1, more, EXPERTS]), ALU.is_le))
            chain.link(dve.tensor_reduce(owner_f[:, EXPERTS:], behind, X, ALU.add))
            chain.link(dve.tensor_scalar(owner_f[:, EXPERTS:], owner_f[:, EXPERTS:], float(EXPERTS - 1), None, ALU.min))
            chain.link(dve.tensor_copy(owner_f[:, 0:EXPERTS], s.iota[0:1, 0:EXPERTS]))
            chain.link(dve.tensor_copy(s.owner[:, 0:BLOCKS], owner_f[:]))
            chain.link(dve.tensor_scalar(s.owner[:, BLOCKS:BLOCKS + 1], upto[0:1, EXPERTS - 1:EXPERTS], float(EXPERTS),
                                         None, ALU.add))
            dve.tensor_copy(s.owner[:, BLOCKS + 1:BLOCKS + 2], upto[0:1, EXPERTS - 1:EXPERTS]).then_inc(late_ready, 1)
            dve.wait_ge(late_ready, 1)

        def scatter(pool, slots, t):
            rows = DEC if t == SAMPLE else P
            for j in range(2):
                pool.indirect_dma_start(io["slot_table"], bass.IndirectOffsetOnAxis(ap=slots[0:rows, t, j:j + 1], axis=0),
                                        s.assignment[0:rows, t, j:j + 1], None, bounds_check=SLOTS - 1,
                                        oob_is_err=False).then_inc(scattered, 16)

        @block.vector
        def _(dve):
            dve.memset(s.carry[:], 0.0).then_inc(cleared, 1)
            dve.wait_ge(cleared, 1)
            for j in range(PIECES):
                if j == 1:
                    dve.wait_ge(o_high, 1)
                    dve.tensor_tensor(o_lo[:], turn[:], o_hi[:].bitcast(F32), ALU.subtract).then_inc(o_low, 1)
                dve.wait_ge(w_high, j + 1)
                dve.tensor_tensor(w_lo[:, j // KD, j % KD], w_raw[:, j % RAW], w_hi[:, j // KD, j % KD].bitcast(F32),
                                  ALU.subtract).then_inc(w_split, 1)
            dve.wait_ge(small_in, 48)
            tile_dve(dve, 0, first=True)
            with dve.Fori(1, SAMPLE) as t:
                tile_dve(dve, t)
            tile_dve(dve, SAMPLE, last=True)
            read_logits(dve, SAMPLE)
            dve.wait_ge(logits_read, TILES)
            choose(dve, SAMPLE, SAMPLE * ROUTE_LINKS)
            assign(dve, SAMPLE, SAMPLE * PLACE_LINKS)
            late(dve)

        @block.gpsimd
        def _(pool):
            pool.memset(empty[:], NOWHERE).then_inc(empty_set, 1)
            pool.wait_ge(empty_set, 1)
            pool.dma_start(io["slot_table"].rearrange("(p b) a -> p (b a)", p=P), empty[:]).then_inc(table_cleared, 16)
            for t in range(TILES + 1):
                if t < TILES:
                    pool.wait_ge(meaned, t + 2)
                    pool.tensor_tensor(stat[:, 2:3], stat[:, 1:2], s.root[:, 0:1], ALU.pow).then_inc(rooted, 1)
                if t:
                    pool.wait_ge(slots_ready, t)
                    if t == 1:
                        pool.wait_ge(table_cleared, 16)
                    scatter(pool, slot, t - 1)
            pool.wait_ge(late_ready, 1)
            more = pool.value_load(s.owner[0:1, BLOCKS + 1:BLOCKS + 2])
            with pool.If(more > 0):
                for t in range(TILES):
                    scatter(pool, late_slot, t)
                pool.wait_ge(scattered, 16 * 4 * TILES)
            pool.wait_ge(scattered, 16 * 2 * TILES)


def experts(nc, s, io):
    G0, U0, G1, U1, D0, D1 = range(6)
    HALF = KD // 2
    FK = FF // P
    with ExitStack() as ctx:
        sb = lambda name, shape, dt=F32: ctx.enter_context(nc.sbuf_tensor(name, shape, dt))
        sem = semaphores(nc, ctx)
        w_raw = sb("we_raw", [P, 6, 4 * N])
        w_hi, w_lo = sb("we_hi", [P, 6, 4 * N], F32R), sb("we_lo", [P, 6, 4 * N], F32R)
        x_nat = sb("x_nat", [P, D])
        x_hi, x_lo = sb("x_hi", [P, KD, P], F32R), sb("x_lo", [P, KD, P], F32R)
        opened, hidden = sb("opened", [P, FF]), sb("hidden", [P, FF])
        a_hi, a_lo = sb("a_hi", [P, FK, P], F32R), sb("a_lo", [P, FK, P], F32R)
        y_out = sb("y_out", [P, D])
        table_i, table_f = sb("table_i", [BLOCKS + 1, P], I32), sb("table_f", [BLOCKS + 1, P])
        choice, frame = sb("choice", [P, BLOCKS + 1], I32), sb("frame", [P, BLOCKS + 1], I32)
        gather_at, scatter_at = sb("gather_at", [P, 1], I32), sb("scatter_at", [P, 1], I32)
        gu = ctx.enter_context(nc.psum_tensor("gu_bank", [P, 2, N], F32))
        y = ctx.enter_context(nc.psum_tensor("ye_bank", [P, D], F32))
        turn_x = ctx.enter_context(nc.psum_tensor("turn_x", [P, KD, P], F32))
        turn_a = ctx.enter_context(nc.psum_tensor("turn_a", [P, FK, P], F32))
        table_t = turn_a[:, 0, 0:BLOCKS + 1]

        table_in, table_cast, table_turned, choice_ready, frame_ready = (
            sem("table_in"), sem("table_cast"), sem("table_turned"), sem("choice_ready"), sem("frame_ready"))
        x_zeroed = sem("x_nat_zeroed")
        loaded = [sem(f"we_loaded{j}") for j in range(6)]
        high = [sem(f"we_high{j}") for j in range(6)]
        split = [sem(f"we_split{j}") for j in range(6)]
        gathered, x_turned, x_high, x_low = sem("gathered"), sem("x_turned"), sem("x_high"), sem("x_low")
        gu_used, d_used = sem("gu_used"), sem("d_used")
        sig_done, gated, a_done, a_turned, a_high, a_low = (sem("sig_done"), sem("gated_e"), sem("a_done"),
                                                            sem("a_turned"), sem("a_high"), sem("a_low"))
        y_moved, y_scattered = sem("y_moved"), sem("y_scattered")
        gather_set, scatter_set = sem("gather_set"), sem("scatter_set")
        gather_begun, scatter_begun = sem("gather_begun"), sem("scatter_begun")
        block = ctx.enter_context(nc.Block())

        def count_of(engine):
            return engine.value_load(s.owner[0:1, BLOCKS + 1:BLOCKS + 2], min_val=0, max_val=BLOCKS - EXPERTS) + EXPERTS

        def load_piece(sp, j, b, expert):
            sp.wait_ge(split[j], b + 1)
            if j < D0:
                part = (io["w_exp_gate"], io["w_exp_up"])[j % 2][bass.ds(expert * D + (j // 2) * (HALF * P), HALF * P), :]
            else:
                part = io["w_exp_down"][bass.ds(expert * FF + (j - D0) * (2 * P), 2 * P), :]
            sp.dma_start(w_raw[:, j].rearrange("p (k n) -> p k n", n=FF if j < D0 else D),
                         part.rearrange("(k p) n -> p k n", p=P)).then_inc(loaded[j], 16)

        def owner_of(sp, b):
            return sp.value_load(s.owner[0:1, bass.ds(b, 1)], min_val=0, max_val=EXPERTS - 1)

        @block.sync
        def _(sp):
            for j in (G0, U0, G1, U1, D0, D1):
                load_piece(sp, j, 0, 0)
            sp.dma_start(table_i[:], io["slot_table"].rearrange("(b p) a -> b (p a)", p=P)).then_inc(table_in, 16)
            for b in (1, 2):
                for j in (G0, U0, G1, U1):
                    load_piece(sp, j, b, b)
            end = count_of(sp)
            with sp.Fori(1, end - 2) as i:
                now, later = owner_of(sp, i), owner_of(sp, i + 2)
                for j, b, expert in ((D0, i, now), (G0, i + 2, later), (D1, i, now), (U0, i + 2, later),
                                     (G1, i + 2, later), (U1, i + 2, later)):
                    load_piece(sp, j, b, expert)
            for back in (2, 1):
                expert = owner_of(sp, end - back)
                for j in (D0, D1):
                    load_piece(sp, j, end - back, expert)

        def turn_rows(pe, i):
            pe.wait_ge(gathered, i * 16 + 16)
            pe.wait_ge(x_low, i)
            for k in range(KD):
                last = pe.transpose(turn_x[:, k], x_nat[:, k * P:(k + 1) * P], s.ident[:])
            last.then_inc(x_turned, 1)

        def gate_up(pe, i):
            pe.wait_ge(x_low, i + 1)
            pe.wait_ge(a_done, i)
            for j in (G0, U0, G1, U1):
                pe.wait_ge(split[j], i + 2)
                for kk in range(HALF):
                    k = (j // 2) * HALF + kk
                    cols = slice(kk * FF, (kk + 1) * FF)
                    out = gu[:, j % 2]
                    pe.matmul(out, x_hi[:, k], w_hi[:, j, cols], start=(k == 0), stop=False)
                    pe.matmul(out, x_hi[:, k], w_lo[:, j, cols], start=False, stop=False)
                    last = pe.matmul(out, x_lo[:, k], w_hi[:, j, cols], start=False, stop=(k == KD - 1))
                last.then_inc(gu_used, 1)

        def down(pe, i):
            pe.wait_ge(a_low, i + 1)
            pe.wait_ge(y_moved, i + 1)
            for j in (D0, D1):
                pe.wait_ge(split[j], i + 2)
                for kk in range(2):
                    k = (j - D0) * 2 + kk
                    for n in range(2):
                        cols = slice(kk * D + n * N, kk * D + (n + 1) * N)
                        out = y[:, n * N:(n + 1) * N]
                        pe.matmul(out, a_hi[:, k], w_hi[:, j, cols], start=(k == 0), stop=False)
                        pe.matmul(out, a_hi[:, k], w_lo[:, j, cols], start=False, stop=False)
                        last = pe.matmul(out, a_lo[:, k], w_hi[:, j, cols], start=False, stop=(k == FK - 1))
                last.then_inc(d_used, 1)

        def turn_hidden(pe, i):
            pe.wait_ge(a_done, i + 1)
            pe.wait_ge(a_low, i)
            for k in range(FK):
                last = pe.transpose(turn_a[:, k], hidden[:, k * P:(k + 1) * P], s.ident[:])
            last.then_inc(a_turned, 1)

        @block.tensor
        def _(pe):
            pe.sem_inc(gu_used, 4)
            pe.sem_inc(d_used, 2)
            pe.wait_ge(table_cast, 1)
            pe.transpose(table_t, table_f[:], s.ident[0:BLOCKS + 1, 0:BLOCKS + 1]).then_inc(table_turned, 1)
            end = count_of(pe)
            turn_rows(pe, 0)
            gate_up(pe, 0)
            turn_rows(pe, 1)
            turn_hidden(pe, 0)
            with pe.Fori(1, end - 1) as i:
                gate_up(pe, i)
                turn_rows(pe, i + 1)
                down(pe, i - 1)
                turn_hidden(pe, i)
            gate_up(pe, end - 1)
            down(pe, end - 2)
            turn_hidden(pe, end - 1)
            down(pe, end - 1)

        def high_part(act, j, b):
            act.wait_ge(loaded[j], b * 16 + 16)
            if j < D0:
                act.wait_ge(gu_used, b * 4 + (j + 1))
            else:
                act.wait_ge(d_used, b * 2 + (j - D0 + 1))
            act.activation(w_hi[:, j], w_raw[:, j], ACT.Copy).then_inc(high[j], 1)

        def rows_high(act, i):
            act.wait_ge(x_turned, i + 1)
            act.wait_ge(gu_used, i * 4 + 4)
            act.activation(x_hi[:], turn_x[:], ACT.Copy).then_inc(x_high, 1)

        def sigmoid(act, i):
            act.wait_ge(gu_used, i * 4 + 8)
            act.wait_ge(gated, i)
            act.activation(opened[:], gu[:, 0], ACT.Sigmoid).then_inc(sig_done, 1)

        def hidden_high(act, i):
            act.wait_ge(a_turned, i + 1)
            act.wait_ge(d_used, i * 2 + 2)
            act.activation(a_hi[:], turn_a[:], ACT.Copy).then_inc(a_high, 1)

        def move_y(act, i, first=False):
            act.wait_ge(d_used, i * 2 + 4)
            if not first:
                act.wait_ge(y_scattered, i * 16)
            act.activation(y_out[:], y[:], ACT.Copy).then_inc(y_moved, 1)

        def block_act(act, i, hidden_before=True, y_before=True, first_y=False, last=False):
            if hidden_before:
                hidden_high(act, i - 1)
            if y_before:
                move_y(act, i - 2, first_y)
            if hidden_before:
                high_part(act, D0, i - 1)
            if not last:
                high_part(act, G0, i + 1)
            if hidden_before:
                high_part(act, D1, i - 1)
            if not last:
                high_part(act, U0, i + 1)
                high_part(act, G1, i + 1)
            sigmoid(act, i)
            if not last:
                high_part(act, U1, i + 1)
                rows_high(act, i + 1)

        @block.scalar
        def _(act):
            end = count_of(act)
            act.sem_inc(y_moved, 1)
            for j in (G0, U0, G1, U1):
                high_part(act, j, 0)
            rows_high(act, 0)
            block_act(act, 0, hidden_before=False, y_before=False)
            block_act(act, 1, y_before=False)
            block_act(act, 2, first_y=True)
            with act.Fori(3, end - 1) as i:
                block_act(act, i)
            block_act(act, end - 1, last=True)
            hidden_high(act, end - 1)
            move_y(act, end - 2)
            high_part(act, D0, end - 1)
            high_part(act, D1, end - 1)
            move_y(act, end - 1)

        def low_part(engine, j, b):
            engine.wait_ge(high[j], b + 1)
            engine.tensor_tensor(w_lo[:, j], w_raw[:, j], w_hi[:, j].bitcast(F32), ALU.subtract).then_inc(split[j], 1)

        def rows_low(dve, i):
            dve.wait_ge(x_high, i + 1)
            dve.tensor_tensor(x_lo[:], turn_x[:], x_hi[:].bitcast(F32), ALU.subtract).then_inc(x_low, 1)

        def hide(dve, i):
            dve.wait_ge(sig_done, i + 1)
            dve.wait_ge(a_turned, i)
            dve.tensor_tensor(hidden[:], gu[:, 0], opened[:], ALU.mult).then_inc(gated, 1)
            dve.wait_ge(gated, i + 1)
            dve.tensor_tensor(hidden[:], hidden[:], gu[:, 1], ALU.mult).then_inc(a_done, 1)

        def hidden_low(dve, i):
            dve.wait_ge(a_high, i + 1)
            dve.tensor_tensor(a_lo[:], turn_a[:], a_hi[:].bitcast(F32), ALU.subtract).then_inc(a_low, 1)

        def block_dve(dve, i, hidden_before=True, last=False):
            if hidden_before:
                hidden_low(dve, i - 1)
                low_part(dve, D0, i - 1)
            if not last:
                for j in (G0, U0, G1):
                    low_part(dve, j, i + 1)
            hide(dve, i)
            if not last:
                low_part(dve, U1, i + 1)
                rows_low(dve, i + 1)

        @block.vector
        def _(dve):
            for j in range(6):
                dve.sem_inc(split[j], 1)
            dve.memset(x_nat[:], 0.0).then_inc(x_zeroed, 1)
            dve.wait_ge(table_in, 16)
            dve.tensor_copy(table_f[:], table_i[:]).then_inc(table_cast, 1)
            dve.wait_ge(table_turned, 1)
            dve.tensor_copy(choice[:], table_t).then_inc(choice_ready, 1)
            dve.wait_ge(choice_ready, 1)
            dve.tensor_scalar(frame[:], choice[:], 1, None, ALU.arith_shift_right).then_inc(frame_ready, 1)
            end = count_of(dve)
            for j in (G0, U0, G1, U1):
                low_part(dve, j, 0)
            rows_low(dve, 0)
            block_dve(dve, 0, hidden_before=False)
            with dve.Fori(1, end - 1) as i:
                block_dve(dve, i)
            block_dve(dve, end - 1, last=True)
            hidden_low(dve, end - 1)
            low_part(dve, D0, end - 1)

        @block.gpsimd
        def _(pool):
            pool.wait_ge(frame_ready, 1)
            pool.wait_ge(x_zeroed, 1)
            last_choice, last_frame = pool.to_reg(ASSIGNED - 1), pool.to_reg(SEQ + DEC - 1)
            end = count_of(pool)

            def gather(pool, i):
                pool.wait_ge(x_turned, i)
                pool.tensor_copy(gather_at[:], frame[:, bass.ds(i, 1)]).then_inc(gather_set, 1)
                pool.wait_ge(gather_set, i + 1)
                pool.sem_inc(gather_begun, 1)
                pool.indirect_dma_start(x_nat[:], None, io["h_mid"], bass.IndirectOffsetOnAxis(ap=gather_at[:], axis=0),
                                        bounds_check=last_frame, oob_is_err=False).then_inc(gathered, 16)

            def scatter_y(pool, i):
                pool.wait_ge(y_moved, i + 2)
                pool.tensor_copy(scatter_at[:], choice[:, bass.ds(i, 1)]).then_inc(scatter_set, 1)
                pool.wait_ge(scatter_set, i + 1)
                pool.sem_inc(scatter_begun, 1)
                pool.indirect_dma_start(io["expert_rows"], bass.IndirectOffsetOnAxis(ap=scatter_at[:], axis=0), y_out[:], None,
                                        bounds_check=last_choice, oob_is_err=False).then_inc(y_scattered, 16)

            gather(pool, 0)
            gather(pool, 1)
            gather(pool, 2)
            low_part(pool, D1, 0)
            gather(pool, 3)
            with pool.Fori(2, end - 1) as i:
                scatter_y(pool, i - 2)
                low_part(pool, D1, i - 1)
                gather(pool, i + 2)
            scatter_y(pool, end - 3)
            low_part(pool, D1, end - 2)
            scatter_y(pool, end - 2)
            low_part(pool, D1, end - 1)
            scatter_y(pool, end - 1)
            pool.wait_ge(y_scattered, end * 16)
            pool.wait_ge(gathered, end * 16 + 16)


def final(nc, s, io):
    with ExitStack() as ctx:
        sb = lambda name, shape, dt=F32: ctx.enter_context(nc.sbuf_tensor(name, shape, dt))
        sem = semaphores(nc, ctx)
        x, rows = sb("x_final", [P, TILES, D]), sb("rows_final", [P, TILES, 2, D])
        square = sb("square_final", [P, D])
        gain = sb("gain_final", [P, D])
        share = sb("share", [P, TILES, GROUPS])
        total, weights = sb("total", [P, TILES]), sb("weights", [P, 2, TILES])
        stat = sb("stat_final", [P, 3, TILES])
        gain_in = sem("gain_final_in")
        x_in = [sem(f"x_final_in{t}") for t in range(TILES)]
        chances, totaled, weighted = sem("chances"), sem("totaled"), sem("weighted")
        added, squared, rooted, normed, stored = (sem("added"), sem("squared_final"), sem("rooted_final"),
                                                  sem("normed_final"), sem("stored_final"))
        block = ctx.enter_context(nc.Block())

        def height(t):
            return DEC if t == SAMPLE else P

        def store(act, t):
            act.wait_ge(normed, t + 1)
            out = io["y_sample"][0] if t == SAMPLE else io["y_prompt"][0, t * P:(t + 1) * P, :]
            act.dma_start(out, rows[0:height(t), t, 0]).then_inc(stored, 16)

        @block.sync
        def _(sp):
            for t in range(TILES):
                h = height(t)
                sp.dma_start(x[0:h, t], io["x_mid"][t * P:t * P + h, :]).then_inc(x_in[t], 16)
                sp.dma_start(rows[0:h, t], io["expert_rows"][2 * t * P:2 * (t * P + h), :].rearrange(
                    "(p k) d -> p k d", k=2)).then_inc(x_in[t], 16)
                if t == 0:
                    sp.dma_start(gain[:], io["norm_final_gain"].partition_broadcast(P)).then_inc(gain_in, 16)

        @block.scalar
        def _(act):
            act.activation(share[:], s.group_rel[:], ACT.Exp).then_inc(chances, 1)
            act.activation(weights[:, 0], s.gap[:], ACT.Sigmoid).then_inc(chances, 1)
            act.activation(weights[:, 1], s.gap[:], ACT.Sigmoid, scale=-1.0).then_inc(chances, 1)
            for t in range(TILES):
                h = height(t)
                act.wait_ge(added, 2 * t + 2)
                if t:
                    act.wait_ge(squared, t)
                act.activation(square[0:h], x[0:h, t], ACT.Square, accum_out=stat[0:h, 0, t:t + 1]).then_inc(squared, 1)
                if t:
                    store(act, t - 1)
            store(act, TILES - 1)
            act.wait_ge(stored, 16 * TILES)

        @block.gpsimd
        def _(pool):
            for t in range(TILES):
                h = slice(0, height(t))
                pool.wait_ge(squared, t + 1)
                pool.tensor_scalar(stat[h, 1, t:t + 1], stat[h, 0, t:t + 1], 1.0 / D, EPS, ALU.mult, ALU.add)\
                    .then_inc(rooted, 1)
                pool.wait_ge(rooted, 2 * t + 1)
                pool.tensor_tensor(stat[h, 2, t:t + 1], stat[h, 1, t:t + 1], s.root[h, 0:1], ALU.pow).then_inc(rooted, 1)

        @block.vector
        def _(dve):
            chain = Chain(dve, totaled)
            dve.wait_ge(chances, 3)
            chain.link(dve.tensor_reduce(total[:], share[:], X, ALU.add))
            chain.link(dve.reciprocal(total[:], total[:]))
            dve.tensor_tensor(weights[:], weights[:], total[:].unsqueeze(1).to_broadcast([P, 2, TILES]),
                              ALU.mult).then_inc(weighted, 1)
            dve.wait_ge(weighted, 1)
            dve.wait_ge(gain_in, 16)
            for t in range(TILES + 1):
                if t < TILES:
                    h = slice(0, height(t))
                    dve.wait_ge(x_in[t], 32)
                    for k in range(2):
                        if k:
                            dve.wait_ge(added, 2 * t + 1)
                        dve.scalar_tensor_tensor(x[h, t], rows[h, t, k], weights[h, k, t:t + 1], x[h, t], ALU.mult,
                                                 ALU.add).then_inc(added, 1)
                if t:
                    u = t - 1
                    h = slice(0, height(u))
                    dve.wait_ge(rooted, 2 * u + 2)
                    dve.scalar_tensor_tensor(rows[h, u, 0], x[h, u], stat[h, 2, u:u + 1], gain[h], ALU.mult,
                                             ALU.mult).then_inc(normed, 1)


SCRATCH = {"projected": ((ROWS, MAIN), F32), "x_rows": ((ROWS, D), F32), "mixed": ((ROWS, D), F32),
           "x_mid": ((ROWS, D), F32), "h_mid": ((ROWS, D), F32), "slot_table": ((SLOTS, 1), I32),
           "expert_rows": ((ASSIGNED, D), F32)}


class Shared:

    def __init__(self, nc, ctx):
        sb = lambda name, shape, dt=F32: ctx.enter_context(nc.sbuf_tensor(name, shape, dt))
        self.ident, self.ident_b = sb("ident", [P, P]), sb("ident_b", [P, P], BF16)
        self.later_b, self.before_b = sb("later_b", [P, P], BF16), sb("before_b", [P, P], BF16)
        self.ones_b = sb("ones_b", [P, P], BF16)
        self.causal, self.tri_mid = sb("causal", [P, P]), sb("tri_mid", [P, P])
        self.spans, self.valid, self.nowhere = sb("spans", [P, 3]), sb("valid", [P, TILES]), sb("nowhere", [P, TILES])
        self.root, self.iota = sb("root", [P, H_A]), sb("iota", [P, EXPERTS + GROUPS])
        self.assignment, self.rank_t = sb("assignment", [P, TILES, 2], I32), sb("rank_t", [RANK, ROWS])
        self.group_rel, self.gap = sb("group_rel", [P, TILES, GROUPS]), sb("gap", [P, TILES])
        self.number, self.hot = sb("number", [P, 2 * TILES]), sb("hot", [P, 2 * TILES, EXPERTS])
        self.at, self.carry = sb("at", [P, 2 * TILES]), sb("carry", [P, EXPERTS])
        self.owner = sb("owner", [1, BLOCKS + 2], I32)


def build(nc, ins, outs):
    scratch = {n: nc.dram_tensor(n, shape, dt, kind="Internal").ap() for n, (shape, dt) in SCRATCH.items()}
    io = {**ins, **outs, **scratch}
    with ExitStack() as ctx:
        s = Shared(nc, ctx)
        constants(nc, s)
        for stage in STAGES:
            stage(nc, s, io)


STAGES = (project, stick, gla, merge, experts, final)
_OUTS = {
    "y_prompt": (1, SEQ, D), "y_sample": (1, DEC, D), "gla_prompt": (1, 1, H_A, DK, DV),
    "k_prompt": (1, 1, SEQ, H_B, DH), "v_prompt": (1, 1, SEQ, H_B, DH), "gla_sample": (1, 1, H_A, DK, DV),
    "k_sample": (1, 1, DEC, H_B, DH), "v_sample": (1, 1, DEC, H_B, DH),
}


def laid_out(inputs):
    a = {k: np.ascontiguousarray(v) for k, v in inputs.items()}
    lr = 2 * QK + 2 * MIX
    w_in = a["w_in"][0]
    return {
        "x_prompt": a["x_prompt"][0], "x_sample": a["x_sample"][0], "state_gla": a["state_gla"][0, 0],
        "cache_k": a["cache_sb_k"].reshape(PAST, MIX), "cache_v": a["cache_sb_v"].reshape(PAST, MIX),
        "norm_mix_gain": a["norm_mix_gain"][0],
        "w_main": np.concatenate([w_in[:, :lr], w_in[:, lr + RANK:]], axis=1),
        "w_rank": np.ascontiguousarray(w_in[:, lr:lr + RANK]),
        "w_gate_up": a["w_gla_gate_up"][0], "b_gate": a["b_gla_gate"][0], "gla_gain": a["gla_norm_gain"][0],
        "w_branch": a["w_branch"].reshape(2 * MIX, D), "w_out": a["w_out"][0], "norm_ffn_gain": a["norm_ffn_gain"][0],
        "w_router": np.concatenate([a["w_router_expert"][0], a["w_router_group"][0]], axis=1),
        "b_router": np.concatenate([a["b_router_expert"][0], a["b_router_group"][0]]),
        "w_exp_gate": a["w_exp_gate"].reshape(EXPERTS * D, FF), "w_exp_up": a["w_exp_up"].reshape(EXPERTS * D, FF),
        "w_exp_down": a["w_exp_down"].reshape(EXPERTS * FF, D), "norm_final_gain": a["norm_final_gain"],
    }


def kernel(**inputs):
    import concourse.bacc as _bacc
    from concourse.bass_utils import run_bass_kernel_spmd as _run

    nc = _bacc.Bacc("TRN2", target_bir_lowering=False, num_devices=1)
    arrays, ins, outs = {}, {}, {}
    for name, a in laid_out(inputs).items():
        arrays[f"in_{name}"] = a
        ins[name] = nc.dram_tensor(f"in_{name}", a.shape, mybir.dt.from_np(a.dtype), kind="ExternalInput").ap()
    for name, shape in _OUTS.items():
        outs[name] = nc.dram_tensor(f"out_{name}", shape, F32, kind="ExternalOutput").ap()
    build(nc, ins, outs)
    r = _run(nc, [arrays], core_ids=[0])
    return tuple(r.results[0][f"out_{name}"] for name in _OUTS)
```

```python
from contextlib import ExitStack

import numpy as np

import concourse.bass as bass
from concourse import mybir

P = 128
D = 1024
SEQ, DEC, PAST = 1024, 64, 1024
TILES = (SEQ + DEC + P - 1) // P
PROMPT_TILES = SEQ // P
ROWS = TILES * P
SAMPLE = TILES - 1
KD = D // P
MIX = D // 2
H_A, DV = 4, 128
DK = 64
QK = H_A * DK
H_B, DH = 8, 64
PAIRS = H_B // 2
RANK = 16
GATE_TAU = 16.0
GROUPS, PER_GROUP, EXPERTS = 4, 8, 32
ROUTES = GROUPS + EXPERTS
FF = D // 2
EPS = 1e-6
N = 512
CHUNKS = 10
MAIN = CHUNKS * N
COL_QKVR = 0
COL_QB, COL_KB, COL_VB = 1536, 2048, 2560
COL_GATES = 3072
ASSIGNED = 2 * (SEQ + DEC)
BLOCKS = EXPERTS + ASSIGNED // P
SLOTS = (BLOCKS + 1) * P
NOWHERE = 1 << 20
MASKED = -1e30

F32 = mybir.dt.float32
F32R = mybir.dt.float32r
BF16 = mybir.dt.bfloat16
I32 = mybir.dt.int32
ALU = mybir.AluOpType
ACT = mybir.ActivationFunctionType
X = mybir.AxisListType.X


def semaphores(nc, ctx):
    given = []

    def clear():
        nc.clear_and_free_semaphores(given)
        nc.all_engine_barrier()

    ctx.callback(clear)

    def named(name):
        given.append(nc.alloc_semaphore(name=name))
        return given[-1]

    return named


class Chain:

    def __init__(self, engine, sem, start=0):
        self.engine, self.sem, self.start, self.count = engine, sem, start, 0

    def link(self, ins):
        self.mark(ins)
        self.wait()

    def mark(self, ins):
        ins.then_inc(self.sem, 1)
        self.count += 1

    def wait(self):
        self.engine.wait_ge(self.sem, self.start + self.count)


def columns(i, size=P):
    return bass.ds(i * size, size)


def constants(nc, s):
    with ExitStack() as ctx:
        made = ctx.enter_context(nc.semaphore("constants_filled"))
        done = ctx.enter_context(nc.semaphore("constants_selected"))
        turned = ctx.enter_context(nc.semaphore("constants_cast"))
        iota = ctx.enter_context(nc.sbuf_tensor("iota_int", [P, EXPERTS + GROUPS], I32))
        tri = ctx.enter_context(nc.sbuf_tensor("tri_whole", [P, P], F32))
        block = ctx.enter_context(nc.Block())

        @block.gpsimd
        def _(pool):
            fills = [
                (s.ident[:], 0.0), (s.ident_b[:], 0.0), (s.later_b[:], 0.0), (s.causal[:], 1.0), (tri[:], 1 / GATE_TAU),
                (s.before_b[:], 1.0), (s.ones_b[:], 1.0), (s.spans[:], 0.0), (s.valid[:], 1.0), (s.nowhere[:], 0.0), (s.root[:], -0.5),
            ]
            for where, value in fills:
                pool.memset(where, value).then_inc(made, 1)
            pool.wait_ge(made, len(fills))
            selects = [
                (s.ident[:], ALU.not_equal, 1.0, 0, -1, 1),
                (s.ident_b[:], ALU.not_equal, 1.0, 0, -1, 1),
                (s.later_b[:], ALU.is_gt, MASKED, 0, -1, 1),
                (s.causal[:], ALU.is_ge, 0.0, 0, 1, -1),
                (tri[:], ALU.is_ge, 0.0, 0, 1, -1),
                (s.before_b[:], ALU.is_gt, 0.0, 0, 1, -1),
            ]
            for where, op, fill, base, step, mult in selects:
                pool.affine_select(out=where, in_=where, compare_op=op, fill=fill, base=base, pattern=[[step, P]],
                                   channel_multiplier=mult).then_inc(done, 1)
            pool.iota(iota[:, 0:EXPERTS], pattern=[[1, EXPERTS]], base=0, channel_multiplier=0).then_inc(done, 1)
            pool.iota(iota[:, EXPERTS:], pattern=[[1, GROUPS]], base=0, channel_multiplier=0).then_inc(done, 1)
            pool.iota(s.assignment[:], pattern=[[2 * P, TILES], [1, 2]], base=0, channel_multiplier=2).then_inc(done, 1)

        @block.vector
        def _(dve):
            dve.wait_ge(done, 9)
            dve.memset(s.spans[0:64, 0:1], 1 / GATE_TAU).then_inc(turned, 1)
            dve.memset(s.spans[64:P, 1:2], 1 / GATE_TAU).then_inc(turned, 1)
            dve.memset(s.valid[DEC:P, SAMPLE:TILES], 0.0).then_inc(turned, 1)
            dve.memset(s.nowhere[DEC:P, SAMPLE:TILES], float(NOWHERE)).then_inc(turned, 1)
            dve.tensor_copy(s.iota[:], iota[:]).then_inc(turned, 1)
            dve.tensor_scalar(s.tri_mid[0:64, :], tri[0:64, :], -1 / GATE_TAU, None, ALU.add).then_inc(turned, 1)
            dve.tensor_copy(s.tri_mid[64:P, :], tri[64:P, :]).then_inc(turned, 1)
            dve.wait_ge(turned, 7)


def project(nc, s, io):
    RAW, PIECES, STAGES, BANKS = 4, 4, 6, 6
    PER_PIECE = KD // PIECES
    with ExitStack() as ctx:
        sb = lambda name, shape, dt=F32: ctx.enter_context(nc.sbuf_tensor(name, shape, dt))
        sem = semaphores(nc, ctx)
        ht_hi = sb("ht_hi", [P, KD, ROWS], F32R)
        ht_lo = sb("ht_lo", [P, KD, ROWS], F32R)
        w_raw = sb("w_raw", [P, RAW, PER_PIECE, N])
        w_hi = sb("w_hi", [P, 2, KD, N], F32R)
        w_lo = sb("w_lo", [P, 2, KD, N], F32R)
        stage = sb("stage", [P, STAGES, N])
        x_in = sb("x_in", [P, 2, D])
        x_norm = sb("x_norm", [P, 2, D])
        gain = sb("gain_mix", [P, D])
        stat = sb("stat_mix", [P, 2, 3])
        square = sb("square_mix", [P, D])[:]
        rank_raw = sb("rank_raw", [P, KD, RANK])
        rank_hi = sb("rank_hi", [P, KD, P], F32R)
        rank_lo = sb("rank_lo", [P, KD, P], F32R)
        banks = ctx.enter_context(nc.psum_tensor("banks", [P, 8, N], F32))

        gain_in = sem("gain_in")
        x_loaded = [sem("x_loaded0"), sem("x_loaded1")]
        x_zeroed = sem("x_zeroed")
        x_kept = sem("x_kept")
        rank_in = sem("rank_in")
        rank_zero = sem("rank_zero")
        rank_high = sem("rank_high")
        rank_low = sem("rank_low")
        squared = sem("squared")
        normed = sem("normed")
        rooted = sem("rooted_mix")
        turned = sem("turned")
        ht_high = sem("ht_high")
        ht_low = sem("ht_low")
        w_loaded = [sem(f"w_loaded{j}") for j in range(RAW)]
        w_high = sem("w_high")
        w_split = sem("w_split")
        product = sem("product")
        evacuated = sem("evacuated")
        stored = [sem(f"stored{j}") for j in range(STAGES)]
        rank_product = sem("rank_product")
        rank_kept = sem("rank_kept")
        block = ctx.enter_context(nc.Block())

        turned_banks = banks[:, BANKS:].rearrange("p b (k c) -> p (b k) c", c=P)

        def high_part(act, t):
            act.wait_ge(turned, t + 1)
            act.activation(ht_hi[:, :, t * P:(t + 1) * P], turned_banks, ACT.Copy).then_inc(ht_high, 1)

        def low_part(dve, t):
            dve.wait_ge(ht_high, t + 1)
            dve.tensor_tensor(ht_lo[:, :, t * P:(t + 1) * P], turned_banks,
                              ht_hi[:, :, t * P:(t + 1) * P].bitcast(F32), ALU.subtract).then_inc(ht_low, 1)

        def load_chunk(sp, c):
            for j in range(PIECES):
                sp.wait_ge(w_split, c * PIECES + (j + 1))
                sp.dma_start(w_raw[:, j], io["w_main"][j * PER_PIECE * P:(j + 1) * PER_PIECE * P, columns(c, N)].rearrange(
                    "(k p) n -> p k n", p=P)).then_inc(w_loaded[j], 16)

        def store_pair(sp, pair, last):
            for half in range(2):
                if not (last and half):
                    load_chunk(sp, pair * 2 + (half + 1))
                for t in range(TILES):
                    g = half * TILES + t
                    sp.wait_ge(evacuated, pair * (2 * TILES) + (BANKS + g + 1))
                    sp.dma_start(io["projected"][t * P:(t + 1) * P, bass.ds(pair * (2 * N) + half * N, N)],
                                 stage[:, g % STAGES]).then_inc(stored[g % STAGES], 16)

        @block.sync
        def _(sp):
            for t in range(TILES):
                if t >= 2:
                    sp.wait_ge(normed, t - 1)
                    if t == SAMPLE:
                        sp.wait_ge(x_zeroed, 1)
                if t < SAMPLE:
                    sp.dma_start(x_in[:, t % 2], io["x_prompt"][t * P:(t + 1) * P, :]).then_inc(x_loaded[t % 2], 16)
                else:
                    sp.dma_start(x_in[0:DEC, t % 2], io["x_sample"]).then_inc(x_loaded[t % 2], 16)
                if t == 0:
                    sp.dma_start(gain[:], io["norm_mix_gain"].partition_broadcast(P)).then_inc(gain_in, 16)
                if t == 1:
                    load_chunk(sp, 0)
                    sp.dma_start(rank_raw[:], io["w_rank"].rearrange("(k p) n -> p k n", p=P)).then_inc(rank_in, 16)
            sp.wait_ge(x_loaded[SAMPLE % 2], 16 * (SAMPLE // 2 + 1))
            sp.dma_start(io["x_rows"][SEQ:ROWS, :], x_in[:, SAMPLE % 2]).then_inc(x_kept, 16)
            with sp.Fori(0, CHUNKS // 2 - 1) as pair:
                store_pair(sp, pair, False)
            store_pair(sp, CHUNKS // 2 - 1, True)
            for j in range(STAGES):
                sp.wait_ge(stored[j], 16 + 16 * CHUNKS * TILES // STAGES)
            sp.wait_ge(x_kept, 16)

        @block.gpsimd
        def _(pool):
            pool.memset(rank_hi[:].bitcast(F32), 0.0).then_inc(rank_zero, 1)
            pool.memset(rank_lo[:].bitcast(F32), 0.0).then_inc(rank_zero, 1)
            chain = Chain(pool, rooted)
            for t in range(TILES):
                if t == SAMPLE - 1:
                    pool.wait_ge(normed, SAMPLE - 1)
                    pool.memset(x_in[DEC:P, SAMPLE % 2], 0.0).then_inc(x_zeroed, 1)
                    pool.wait_ge(x_zeroed, 1)
                st = stat[:, t % 2]
                pool.wait_ge(squared, t + 1)
                chain.link(pool.tensor_scalar(st[:, 1:2], st[:, 0:1], 1.0 / D, EPS, ALU.mult, ALU.add))
                chain.mark(pool.tensor_tensor(st[:, 2:3], st[:, 1:2], s.root[:, 0:1], ALU.pow))

            def low_pieces(pair, half):
                for j in range(PIECES):
                    pool.wait_ge(w_high, pair * (2 * PIECES) + (half * PIECES + j + 1))
                    pool.wait_ge(rank_zero, 2)
                    ks = slice(j * PER_PIECE, (j + 1) * PER_PIECE)
                    pool.tensor_tensor(w_lo[:, half, ks], w_raw[:, j], w_hi[:, half, ks].bitcast(F32),
                                       ALU.subtract).then_inc(w_split, 1)

            low_pieces(0, 1)
            with pool.Fori(1, CHUNKS // 2) as pair:
                for half in range(2):
                    low_pieces(pair, half)

        def high_piece(act, pair, half, j):
            act.wait_ge(w_loaded[j], pair * 32 + 16 * (half + 1))
            act.activation(w_hi[:, half, j * PER_PIECE:(j + 1) * PER_PIECE], w_raw[:, j],
                           ACT.Copy).then_inc(w_high, 1)

        def high_pieces(act, pair, half):
            act.wait_ge(product, pair * (2 * TILES) + TILES * (half + 1))
            for j in range(PIECES):
                high_piece(act, pair, half, j)

        @block.scalar
        def _(act):
            act.sem_inc(w_split, PIECES)
            for t in range(TILES):
                act.wait_ge(x_loaded[t % 2], 16 * (t // 2 + 1))
                if t == SAMPLE:
                    act.wait_ge(x_zeroed, 1)
                if t:
                    act.wait_ge(squared, t)
                if t >= 2:
                    act.wait_ge(normed, t - 1)
                act.activation(square, x_in[:, t % 2], ACT.Square, accum_out=stat[:, t % 2, 0:1]).then_inc(squared, 1)
                if t:
                    high_part(act, t - 1)
                if 1 <= t <= 2:
                    for j in range(PIECES // 2):
                        high_piece(act, 0, 0, (t - 1) * PIECES // 2 + j)
            high_part(act, TILES - 1)
            act.wait_ge(rank_in, 16)
            act.wait_ge(rank_zero, 2)
            act.activation(rank_hi[:, :, 0:RANK], rank_raw[:], ACT.Copy).then_inc(rank_high, 1)
            high_pieces(act, 0, 1)
            with act.Fori(1, CHUNKS // 2) as pair:
                for half in range(2):
                    high_pieces(act, pair, half)
            act.wait_ge(rank_product, 1)
            act.activation(s.rank_t[:], banks[0:RANK, 0:3, :].rearrange("p b n -> p (b n)")[:, 0:ROWS],
                           ACT.Copy).then_inc(rank_kept, 1)
            act.wait_ge(rank_kept, 1)

        def evacuate(dve, pair, g):
            dve.wait_ge(product, pair * (2 * TILES) + (2 * TILES + g + 1))
            dve.wait_ge(stored[g % STAGES], pair * (16 * 2 * TILES // STAGES) + 16 * (g // STAGES + 1))
            dve.tensor_copy(stage[:, g % STAGES], banks[:, g % BANKS]).then_inc(evacuated, 1)

        @block.vector
        def _(dve):
            dve.sem_inc(evacuated, BANKS)
            for j in range(STAGES):
                dve.sem_inc(stored[j], 16)
            dve.wait_ge(gain_in, 16)
            for t in range(TILES):
                st = stat[:, t % 2]
                dve.wait_ge(rooted, 2 * t + 2)
                if t >= 2:
                    dve.wait_ge(turned, t - 1)
                dve.scalar_tensor_tensor(x_norm[:, t % 2], x_in[:, t % 2], st[:, 2:3], gain[:],
                                         ALU.mult, ALU.mult).then_inc(normed, 1)
                if t:
                    low_part(dve, t - 1)
                if 1 <= t <= 2:
                    for j in range((t - 1) * PIECES // 2, t * PIECES // 2):
                        dve.wait_ge(w_high, j + 1)
                        ks = slice(j * PER_PIECE, (j + 1) * PER_PIECE)
                        dve.tensor_tensor(w_lo[:, 0, ks], w_raw[:, j], w_hi[:, 0, ks].bitcast(F32),
                                          ALU.subtract).then_inc(w_split, 1)
                if t >= 3:
                    evacuate(dve, 0, t - 3)
            low_part(dve, TILES - 1)
            dve.wait_ge(rank_high, 1)
            dve.tensor_tensor(rank_lo[:, :, 0:RANK], rank_raw[:], rank_hi[:, :, 0:RANK].bitcast(F32),
                              ALU.subtract).then_inc(rank_low, 1)
            for g in range(TILES - 3, 2 * TILES):
                evacuate(dve, 0, g)
            with dve.Fori(1, CHUNKS // 2) as pair:
                for g in range(2 * TILES):
                    evacuate(dve, pair, g)

        def turn(pe, t):
            pe.wait_ge(normed, t + 1)
            if t:
                pe.wait_ge(ht_low, t)
            for k in range(KD):
                last = pe.transpose(turned_banks[:, k], x_norm[:, t % 2, k * P:(k + 1) * P], s.ident[:])
            last.then_inc(turned, 1)

        def multiply(pe, pair, half, t):
            g = half * TILES + t
            rows = slice(t * P, (t + 1) * P)
            pe.wait_ge(evacuated, pair * (2 * TILES) + (g + 1))
            for k in range(KD):
                out = banks[:, g % BANKS]
                pe.matmul(out, ht_hi[:, k, rows], w_hi[:, half, k], start=(k == 0), stop=False)
                pe.matmul(out, ht_hi[:, k, rows], w_lo[:, half, k], start=False, stop=False)
                last = pe.matmul(out, ht_lo[:, k, rows], w_hi[:, half, k], start=False, stop=(k == KD - 1))
            last.then_inc(product, 1)

        def multiply_chunk(pe, pair, half):
            pe.wait_ge(w_split, pair * (2 * PIECES) + PIECES * (half + 2))
            for t in range(TILES):
                multiply(pe, pair, half, t)

        @block.tensor
        def _(pe):
            pe.sem_inc(product, 2 * TILES)
            turn(pe, 0)
            for t in range(TILES):
                if t + 1 < TILES:
                    turn(pe, t + 1)
                if t == 0:
                    pe.wait_ge(w_split, 2 * PIECES)
                pe.wait_ge(ht_low, t + 1)
                multiply(pe, 0, 0, t)
            multiply_chunk(pe, 0, 1)
            with pe.Fori(1, CHUNKS // 2) as pair:
                for half in range(2):
                    multiply_chunk(pe, pair, half)
            pe.wait_ge(rank_low, 1)
            pe.wait_ge(evacuated, BANKS + CHUNKS * TILES)
            for b, width in enumerate((N, N, P)):
                cols = slice(b * N, b * N + width)
                for k in range(KD):
                    out = banks[:, b, 0:width]
                    pe.matmul(out, rank_hi[:, k], ht_hi[:, k, cols], start=(k == 0), stop=False)
                    pe.matmul(out, rank_hi[:, k], ht_lo[:, k, cols], start=False, stop=False)
                    last = pe.matmul(out, rank_lo[:, k], ht_hi[:, k, cols], start=False, stop=(k == KD - 1))
            last.then_inc(rank_product, 1)


def stick(nc, s, io):
    CHUNK = 4
    LAG_T, LAG_AV = 5, 7
    Z, KEEP, BETA, W, WT, PROD, TB = 3, 3, 4, 4, 3, 3, 2
    NAT_K, NAT_C, NATS = TILES, 2 * TILES, 2 * TILES + PROMPT_TILES
    GROUP_STARTS = list(range(0, NATS, 4))
    chunks = []
    for i in range(TILES):
        starts = [i] + list(range(0, i, CHUNK)) [::-1] if i == SAMPLE else list(range(0, i + 1, CHUNK))[::-1]
        ends = [i + 1] + starts[:-1]
        chunks += [(i, a, b - a) for a, b in zip(starts, ends)]
    PER_PAIR = 2 * len(chunks)
    PER_BODY = 2 * PER_PAIR
    UNITS_BODY = 4 * TILES

    def work(u):
        return (u // PER_PAIR, u % PER_PAIR // len(chunks), *chunks[u % len(chunks)])

    steps = []
    turns = 0
    for step in range(PER_BODY + LAG_AV):
        ev = {"z": None, "t": None, "prep": None, "av": None}
        if step < PER_BODY:
            ev["z"] = step
        if 0 <= step - LAG_T < PER_BODY:
            ev["t"] = (step - LAG_T, turns)
            turns += 1
        half, local = divmod(step, PER_PAIR)
        if half < 2 and local % 3 == 1 and 4 <= local < 4 + 3 * len(GROUP_STARTS):
            ev["prep"] = (half, (local - 4) // 3, turns)
            turns += 1
        if step >= LAG_AV:
            ev["av"] = step - LAG_AV
        steps.append(ev)
    turn_of = {ev["t"][0]: ev["t"][1] for ev in steps if ev["t"]}
    PREPS = len(GROUP_STARTS)
    pair_one_ready = max(ev["prep"][2] for ev in steps if ev["prep"] and ev["prep"][0] == 0) + 1
    assert turns % TB == 0 and PER_BODY % Z == 0 and PER_BODY % W == 0 and UNITS_BODY % PROD == 0 and PREPS % 2 == 1

    with ExitStack() as ctx:
        sb = lambda name, shape, dt=F32: ctx.enter_context(nc.sbuf_tensor(name, shape, dt))
        sem = semaphores(nc, ctx)
        nat = sb("nat_qk", [P, 2, NATS, P])
        nat_v = sb("nat_v", [P, 2, TILES + PROMPT_TILES, P])
        qk_hi = sb("qk_hi", [P, 2, NATS * P], F32R)
        qk_lo = sb("qk_lo", [P, 2, NATS * P], F32R)
        keep = sb("keep", [P, KEEP, CHUNK * P])
        beta = sb("beta", [P, BETA, CHUNK * P])
        weight = sb("weight", [P, W, CHUNK * P])
        weight_t = sb("weight_t", [P, WT, CHUNK * P])
        prod = sb("prod", [P, PROD, ROWS + 1])
        o_nat = sb("o_nat_b", [P, 2, TILES, P])
        z_bank = ctx.enter_context(nc.psum_tensor("z_bank", [P, Z, N], F32))
        t_bank = ctx.enter_context(nc.psum_tensor("t_bank", [P, TB, N], F32))
        o_bank = ctx.enter_context(nc.psum_tensor("o_bank", [P, 2, N], F32))
        o_last = ctx.enter_context(nc.psum_tensor("o_last", [P, 2, DH], F32))

        qk_loaded = [sem("qk_loaded0"), sem("qk_loaded1")]
        v_loaded = [sem("v_loaded0"), sem("v_loaded1")]
        ones_set = sem("ones_set")
        scored = sem("scored")
        kept = sem("kept")
        betaed = sem("betaed")
        scanned = sem("scanned")
        weighed = sem("weighed")
        turned = sem("turned_b")
        high = sem("qk_high")
        moved = sem("moved")
        attended = sem("attended")
        o_moved = sem("o_moved")
        o_stored = [sem("o_stored0"), sem("o_stored1")]
        kv_out = sem("kv_out")
        block = ctx.enter_context(nc.Block())

        def last_before(u):
            pair, head, i, _, _ = work(u)
            unit = (pair * 2 + head) * TILES + i - PROD
            return max([v + 1 for v in range(u) if unit_of(v) <= unit], default=0)

        def unit_of(u):
            pair, head, i, _, _ = work(u)
            return (pair * 2 + head) * TILES + i

        def key_columns(i, a, n):
            first = NAT_C + a if i == SAMPLE and a < SAMPLE else NAT_K + a
            return slice(first * P, (first + n) * P)

        def load_qk(sp, col, half):
            for j, (src, at, first, n) in enumerate((
                    (io["projected"], COL_QB, 0, TILES), (io["projected"], COL_KB, NAT_K, TILES),
                    (io["cache_k"], 0, NAT_C, PROMPT_TILES))):
                sp.dma_start(nat[:, half, first:first + n], src[:, bass.ds(col + at, P)].rearrange(
                    "(t p) c -> p t c", p=P)).then_inc(qk_loaded[half], 16)

        def load_v(sp, col, half):
            for src, at, first, n in ((io["projected"], COL_VB, 0, TILES), (io["cache_v"], 0, TILES, PROMPT_TILES)):
                sp.dma_start(nat_v[:, half, first:first + n], src[:, bass.ds(col + at, P)].rearrange(
                    "(t p) c -> p t c", p=P)).then_inc(v_loaded[half], 16)

        @block.sync
        def _(sp):
            for half in range(2):
                load_qk(sp, half * P, half)
                load_v(sp, half * P, half)
            for at, prompt, sample in ((COL_KB, io["k_prompt"], io["k_sample"]), (COL_VB, io["v_prompt"], io["v_sample"])):
                sp.dma_start(prompt.rearrange("a b s h d -> (a b s) (h d)"),
                             io["projected"][0:SEQ, at:at + MIX]).then_inc(kv_out, 16)
                sp.dma_start(sample.rearrange("a b s h d -> (a b s) (h d)"),
                             io["projected"][SEQ:SEQ + DEC, at:at + MIX]).then_inc(kv_out, 16)
            for t in range(TILES):
                sp.dma_start(s.qkvr[:, t], io["projected"][t * P:(t + 1) * P, 0:COL_QB]).then_inc(s.qkvr_in, 16)
            with sp.Fori(0, PAIRS // 2) as body:
                for half in range(2):
                    col = (body * -2 + (2 + half)) * P
                    out_col = body * (2 * P) + (half * P + MIX)
                    sp.wait_ge(moved, body * turns + (TB + PREPS + (pair_one_ready if half else 0)))
                    load_qk(sp, col, half)
                    sp.wait_ge(o_moved, body * 8 + (4 + 4 * (half + 1)))
                    sp.dma_start(io["mixed"][:, bass.ds(out_col, P)].rearrange(
                        "(t p) c -> p t c", p=P), o_nat[:, half]).then_inc(o_stored[half], 16)
                    load_v(sp, col, half)
            for half in range(2):
                sp.wait_ge(o_stored[half], 16 + 16 * (PAIRS // 2))
                sp.wait_ge(qk_loaded[half], 48 * (PAIRS // 2 + 1))
                sp.wait_ge(v_loaded[half], 32 * (PAIRS // 2 + 1))
            sp.wait_ge(kv_out, 64)

        def sigmoids(act, body, u):
            _, _, i, a, n = work(u)
            act.wait_ge(scored, body * PER_BODY + (u + 1))
            act.wait_ge(scanned, body * PER_BODY + (u + 1))
            act.activation(keep[:, u % KEEP, 0:n * P], z_bank[:, u % Z, 0:n * P], ACT.Sigmoid,
                           scale=-DH ** -0.5).then_inc(kept, 1)
            act.wait_ge(weighed, body * PER_BODY + (u + 1))
            act.activation(beta[:, u % BETA, 0:n * P], z_bank[:, u % Z, 0:n * P], ACT.Sigmoid,
                           scale=DH ** -0.5).then_inc(betaed, 1)

        def prep_columns(group):
            first = GROUP_STARTS[group]
            return first, min(4, NATS - first)

        def high_part(act, half, group, turn, turn_count):
            first, n = prep_columns(group)
            act.wait_ge(turned, turn_count)
            act.activation(qk_hi[:, half, first * P:(first + n) * P], t_bank[:, turn % TB, 0:n * P],
                           ACT.Copy).then_inc(high, 1)

        def output(act, body, u):
            pair, head, i, a, n = work(u)
            if a or i < PROMPT_TILES - 1:
                return
            act.wait_ge(attended, body * PER_BODY + (WT + u + 1))
            act.wait_ge(o_stored[pair], body * 16 + 16)
            if i < SAMPLE:
                act.activation(o_nat[:, pair, 0:PROMPT_TILES, head * DH:(head + 1) * DH],
                               o_bank[:, head].rearrange("p (t d) -> p t d", d=DH), ACT.Copy).then_inc(o_moved, 1)
            else:
                act.activation(o_nat[:, pair, SAMPLE, head * DH:(head + 1) * DH], o_last[:, head],
                               ACT.Copy).then_inc(o_moved, 1)

        @block.scalar
        def _(act):
            act.sem_inc(betaed, Z)
            act.sem_inc(o_moved, 4)
            for half in range(2):
                act.sem_inc(o_stored[half], 16)
            for group in range(PREPS):
                high_part(act, 0, group, group, group + 1)
            with act.Fori(0, PAIRS // 2) as body:
                for ev in steps:
                    if ev["z"] is not None:
                        sigmoids(act, body, ev["z"])
                    if ev["prep"]:
                        half, group, turn = ev["prep"]
                        high_part(act, 1 - half, group, turn + PREPS, body * turns + (PREPS + turn + 1))
                    if ev["av"] is not None:
                        output(act, body, ev["av"])

        @block.vector
        def _(dve):
            dve.sem_inc(scanned, KEEP)
            dve.sem_inc(moved, TB)
            dve.memset(prod[:, :, ROWS:ROWS + 1], 1.0).then_inc(ones_set, 1)

            def low_part(half, group, turn, high_count):
                first, n = prep_columns(group)
                cols = slice(first * P, (first + n) * P)
                dve.wait_ge(high, high_count)
                dve.tensor_tensor(qk_lo[:, half, cols], t_bank[:, turn % TB, 0:n * P],
                                  qk_hi[:, half, cols].bitcast(F32), ALU.subtract).then_inc(moved, 1)

            for group in range(PREPS):
                low_part(0, group, group, group + 1)
            dve.wait_ge(ones_set, 1)
            with dve.Fori(0, PAIRS // 2) as body:
                for ev in steps:
                    if ev["t"]:
                        u, turn = ev["t"]
                        n = work(u)[4]
                        dve.wait_ge(turned, body * turns + (PREPS + turn + 1))
                        dve.wait_ge(attended, body * PER_BODY + (u + 1))
                        dve.tensor_copy(weight_t[:, u % WT, 0:n * P],
                                        t_bank[:, (PREPS + turn) % TB, 0:n * P]).then_inc(moved, 1)
                    if ev["z"] is not None:
                        u = ev["z"]
                        pair, head, i, a, n = work(u)
                        unit = (pair * 2 + head) * TILES + i
                        at = ROWS - (i + 1) * P + a * P
                        dve.wait_ge(kept, body * PER_BODY + (u + 1))
                        dve.wait_ge(weighed, body * PER_BODY + (BETA + last_before(u)))
                        if a + n <= i:
                            dve.wait_ge(scanned, body * PER_BODY + (KEEP + u))
                        line = keep[:, u % KEEP, 0:n * P][:, ::-1]
                        dve.tensor_tensor_scan(prod[:, unit % PROD, at:at + n * P][:, ::-1], line, line,
                                               prod[:, unit % PROD, at + n * P:at + n * P + 1], ALU.mult,
                                               ALU.min).then_inc(scanned, 1)
                    if ev["prep"]:
                        half, group, turn = ev["prep"]
                        low_part(1 - half, group, PREPS + turn,
                                 body * (2 * PREPS) + (PREPS + half * PREPS + group + 1))

        @block.gpsimd
        def _(pool):
            pool.sem_inc(weighed, BETA)
            with pool.Fori(0, PAIRS // 2) as body:
                for u in range(PER_BODY):
                    _, _, i, a, n = work(u)
                    at = ROWS - (i + 1) * P + a * P
                    pool.wait_ge(scanned, body * PER_BODY + (KEEP + u + 1))
                    pool.wait_ge(betaed, body * PER_BODY + (Z + u + 1))
                    back = turn_of[u - W] + 1 if u >= W else 0
                    pool.wait_ge(turned, body * turns + (PREPS + back))
                    pool.tensor_tensor(weight[:, u % W, 0:n * P], beta[:, u % BETA, 0:n * P],
                                       prod[:, unit_of(u) % PROD, at + 1:at + 1 + n * P], ALU.mult).then_inc(weighed, 1)

        @block.tensor
        def _(pe):
            pe.sem_inc(attended, WT)

            def prep(half, group, turn, moved_count):
                first, n = prep_columns(group)
                pe.wait_ge(moved, moved_count)
                for j in range(n):
                    last = pe.transpose(t_bank[:, turn % TB, j * P:(j + 1) * P], nat[:, half, first + j], s.ident[:])
                last.then_inc(turned, 1)

            pe.wait_ge(qk_loaded[0], 48)
            for group in range(PREPS):
                prep(0, group, group, group + 1)
            with pe.Fori(0, PAIRS // 2) as body:
                for ev in steps:
                    if ev["z"] is not None:
                        u = ev["z"]
                        pair, head, i, a, n = work(u)
                        if u % PER_PAIR == 0:
                            pe.wait_ge(moved, body * turns + (TB + PREPS + (pair_one_ready if pair else 0)))
                        pe.wait_ge(betaed, body * PER_BODY + (u + 1))
                        rows = slice(head * DH, (head + 1) * DH)
                        q = slice(i * P, (i + 1) * P)
                        keys = key_columns(i, a, n)
                        out = z_bank[:, u % Z, 0:n * P]
                        masked = a + n == i + 1
                        pe.matmul(out, qk_hi[rows, pair, q], qk_hi[rows, pair, keys], start=True, stop=False)
                        pe.matmul(out, qk_hi[rows, pair, q], qk_lo[rows, pair, keys], start=False, stop=False)
                        last = pe.matmul(out, qk_lo[rows, pair, q], qk_hi[rows, pair, keys], start=False, stop=not masked)
                        if masked:
                            last = pe.matmul(z_bank[:, u % Z, (n - 1) * P:n * P], s.ident_b[:], s.later_b[:],
                                             start=False, stop=True)
                        last.then_inc(scored, 1)
                    if ev["t"]:
                        u, turn = ev["t"]
                        n = work(u)[4]
                        pe.wait_ge(weighed, body * PER_BODY + (BETA + u + 1))
                        pe.wait_ge(moved, body * turns + (PREPS + turn + 1))
                        for j in range(n):
                            last = pe.transpose(t_bank[:, (PREPS + turn) % TB, j * P:(j + 1) * P],
                                                weight[:, u % W, j * P:(j + 1) * P], s.ident[:])
                        last.then_inc(turned, 1)
                    if ev["prep"]:
                        half, group, turn = ev["prep"]
                        if group == 0:
                            pe.wait_ge(qk_loaded[1 - half], body * 48 + (48 + 48 * half))
                        prep(1 - half, group, PREPS + turn, body * turns + (PREPS + turn + 1))
                    if ev["av"] is not None:
                        u = ev["av"]
                        pair, head, i, a, n = work(u)
                        if u % PER_PAIR == 0:
                            pe.wait_ge(v_loaded[pair], body * 32 + 32)
                        pe.wait_ge(moved, body * turns + (TB + PREPS + turn_of[u] + 1))
                        if i == 0 or a == SAMPLE:
                            pe.wait_ge(o_moved, body * 8 + 2 * (2 * pair + head) + (2 if i else 1))
                        out = o_last[:, head] if i == SAMPLE else o_bank[:, head, i * DH:(i + 1) * DH]
                        for j in range(n):
                            v = TILES + a + j if i == SAMPLE and a < SAMPLE else a + j
                            last = pe.matmul(out, weight_t[:, u % WT, j * P:(j + 1) * P],
                                             nat_v[:, pair, v, head * DH:(head + 1) * DH],
                                             start=(a + n == i + 1 and j == 0), stop=(a == 0 and j == n - 1))
                        last.then_inc(attended, 1)


def gla(nc, s, io):
    LIMIT = 40.0
    AHEAD = 6
    G = 2
    WIDTH = TILES * QK
    SPREAD = [(b, b * N, min(N, WIDTH - b * N)) for b in range((WIDTH + N - 1) // N)]
    with ExitStack() as ctx:
        sb = lambda name, shape, dt=F32: ctx.enter_context(nc.sbuf_tensor(name, shape, dt))
        sem = semaphores(nc, ctx)
        qkvr, qkvr_in = s.qkvr, s.qkvr_in
        q, k = qkvr[:, :, 0:QK], qkvr[:, :, QK:2 * QK]
        v, r = qkvr[:, :, 2 * QK:2 * QK + MIX], qkvr[:, :, 2 * QK + MIX:COL_QB]
        gate_up = sb("gate_up", [RANK, QK])
        bias = sb("gate_bias", [P, 2, QK])
        gain = sb("gain_gla", [P, DV])
        gate = sb("gate", [P, WIDTH])
        decay = sb("decay", [P, WIDTH])
        log_a = sb("log_a", [P, WIDTH])
        grow = sb("grow", [P, WIDTH])
        shrink = sb("shrink", [P, WIDTH])
        ends = sb("ends", [P, TILES, G, 2])
        turned_q = sb("turned_q", [P, TILES, 2, G, P])
        turned_k = sb("turned_k", [P, TILES, G, P])
        att = sb("att", [P, TILES, H_A, P])
        clean = sb("att_clean", [P, 2, H_A, P])
        state = sb("state", [P, 2, G, DV])
        state_mid = sb("state_mid", [P, TILES, G, DV])
        added = sb("state_added", [P, G, DV])
        square = sb("square_gla", [P, 2, MIX])
        stat = sb("stat_gla", [P, 3, TILES, H_A])
        swish = sb("swish", [P, TILES, MIX])
        normed = sb("normed_gla", [P, 2, MIX])
        bank = ctx.enter_context(nc.psum_tensor("bank_gla", [P, 8, N], F32))
        flat = bank[:].rearrange("p b n -> p (b n)")

        small_in, state_in = sem("gla_small_in"), sem("state_in")
        gated, biased, gate_act, log_done = sem("gated"), sem("biased"), sem("gate_act"), sem("log_done")
        summed, clamped, grown, ended = sem("summed"), sem("clamped"), sem("grown"), sem("ended")
        scaled, turned, turned_out = sem("scaled"), sem("turned_gla"), sem("turned_out_gla")
        atted, masked, kved = sem("atted"), sem("masked"), sem("kved")
        state_zero, chain_s, stated = sem("state_zero"), sem("chain_state"), sem("stated")
        mixed, squared, summed_sq, rooted = sem("mixed_gla"), sem("squared_gla"), sem("summed_sq"), sem("rooted_gla")
        opened, swish_gain = sem("opened"), sem("swish_gain")
        scaled_o, gated_o = sem("scaled_o"), sem("gated_o")
        zeroed = sem("turned_q_zeroed")
        o_out, state_out = sem("gla_out"), sem("state_out")
        block = ctx.enter_context(nc.Block())

        def attend(pe, t):
            pe.wait_ge(turned_out, 3 * t + 3)
            pe.wait_ge(ended, 1)
            if t >= 2:
                pe.wait_ge(masked, 2 * t - 2)
            for h in range(H_A):
                g, u = divmod(h, 2)
                last = pe.matmul(bank[:, 4 + t % 2, h * P:(h + 1) * P], turned_k[:, t, g], turned_q[:, t, u, g],
                                 start=True, stop=True)
            last.then_inc(atted, 1)

        def mix(pe, t):
            pe.wait_ge(masked, 2 * t + 2)
            pe.wait_ge(stated, t + 1)
            for h in range(H_A):
                g, u = divmod(h, 2)
                out = bank[:, t % 4, h * DV:(h + 1) * DV]
                pe.matmul(out, att[:, t, h], v[:, t, h * DV:(h + 1) * DV], start=True, stop=False)
                last = pe.matmul(out, turned_q[:, t, u, g], state_mid[:, t, g], start=False, stop=True)
            last.then_inc(mixed, 1)

        def squares(act, t):
            act.wait_ge(mixed, t + 1)
            if t >= 2:
                act.wait_ge(summed_sq, t - 1)
            act.activation(square[:, t % 2], bank[:, t % 4], ACT.Square).then_inc(squared, 1)

        def state_step(dve, chain, t):
            j = 1 if t == SAMPLE else 0
            dve.wait_ge(kved, t + 1)
            dve.wait_ge(ended, 1)
            if t == 0:
                dve.wait_ge(state_zero, 1)
            elif t == SAMPLE:
                dve.wait_ge(state_in, 64)
            else:
                dve.wait_ge(stated, t)
            for g in range(G):
                chain.mark(dve.tensor_scalar(state_mid[:, t, g], state[:, j, g], ends[:, t, g, 0:1], None, ALU.mult))
            chain.wait()
            chain.link(dve.tensor_tensor(added[:], bank[:, 6 + t % 2, 0:G * DV].rearrange("p (g v) -> p g v", g=G),
                                         state_mid[:, t], ALU.add))
            chain.link(dve.tensor_scalar(state[:, j, 0], added[:, 0], ends[:, t, 0, 1:2], None, ALU.mult))
            dve.tensor_scalar(state[:, j, 1], added[:, 1], ends[:, t, 1, 1:2], None, ALU.mult).then_inc(stated, 1)

        def output(dve, t):
            dve.wait_ge(squared, t + 1)
            dve.tensor_reduce(stat[:, 0, t], square[:, t % 2].rearrange("p (h v) -> p h v", v=DV), X,
                              ALU.add).then_inc(summed_sq, 1)
            dve.wait_ge(rooted, 2 * t + 2)
            if t >= 2:
                dve.wait_ge(gated_o, t - 1)
            dve.tensor_tensor(normed[:, t % 2].rearrange("p (h v) -> p h v", v=DV),
                              bank[:, t % 4].rearrange("p (h v) -> p h v", v=DV),
                              stat[:, 2, t].unsqueeze(2).to_broadcast([P, H_A, DV]), ALU.mult).then_inc(scaled_o, 1)

        @block.sync
        def _(sp):
            sp.dma_start(gate_up[:], io["w_gate_up"]).then_inc(small_in, 16)
            for j in range(2):
                sp.dma_start(bias[:, j], io["b_gate"].partition_broadcast(P)).then_inc(small_in, 16)
            sp.dma_start(gain[:], io["gla_gain"].partition_broadcast(P)).then_inc(small_in, 16)
            for g in range(G):
                for u in range(2):
                    sp.dma_start(state[u * DK:(u + 1) * DK, 1, g], io["state_gla"][2 * g + u]).then_inc(state_in, 16)
            for t in range(TILES):
                sp.wait_ge(gated_o, t + 1)
                sp.dma_start(io["mixed"][t * P:(t + 1) * P, 0:MIX], swish[:, t]).then_inc(o_out, 16)
            sp.wait_ge(stated, TILES)
            for j, out in ((0, io["gla_prompt"]), (1, io["gla_sample"])):
                rows = out.rearrange("a b h k v -> (a b h) k v")
                for g in range(G):
                    for u in range(2):
                        sp.dma_start(rows[2 * g + u], state[u * DK:(u + 1) * DK, j, g]).then_inc(state_out, 16)
            sp.wait_ge(o_out, 16 * TILES)
            sp.wait_ge(state_out, 16 * 8)

        @block.tensor
        def _(pe):
            pe.wait_ge(small_in, 64)
            for t in range(TILES):
                last = pe.matmul(flat[:, t * QK:(t + 1) * QK], s.rank_t[:, t * P:(t + 1) * P], gate_up[:],
                                 start=True, stop=True)
                if (t + 1) * QK % N == 0 or t == TILES - 1:
                    last.then_inc(gated, 1)
            for b, at, width in SPREAD:
                pe.wait_ge(log_done, b + 1)
                pe.matmul(bank[:, b, 0:width], s.tri_mid[:], log_a[:, at:at + width], start=True,
                          stop=True).then_inc(summed, 1)
            for t in range(TILES):
                spans = s.spans[:, 0:3:2] if t == SAMPLE else s.spans[:, 0:2]
                for g in range(G):
                    at = t * QK + g * P
                    last = pe.matmul(bank[:, 5, 4 * t + 2 * g:4 * t + 2 * g + 2], log_a[:, at:at + P], spans,
                                     start=True, stop=True)
            last.then_inc(summed, 1)
            for t in range(TILES):
                pe.wait_ge(scaled, 2 * t + 2)
                pe.wait_ge(clamped, len(SPREAD))
                if t >= 4:
                    pe.wait_ge(scaled_o, t - 3)
                for j in range(4):
                    last = pe.transpose(bank[:, t % 4, j * P:(j + 1) * P], qkvr[:, t, j * P:(j + 1) * P], s.ident[:])
                last.then_inc(turned, 1)
                if t >= 2:
                    pe.wait_ge(stated, t - 1)
                for h in range(H_A):
                    g, u = divmod(h, 2)
                    last = pe.matmul(bank[u * DK:(u + 1) * DK, 6 + t % 2, g * DV:(g + 1) * DV],
                                     k[:, t, h * DK:(h + 1) * DK], v[:, t, h * DV:(h + 1) * DV], start=True, stop=True)
                last.then_inc(kved, 1)
                if t:
                    attend(pe, t - 1)
                if t > 1:
                    mix(pe, t - 2)
            attend(pe, TILES - 1)
            mix(pe, TILES - 2)
            mix(pe, TILES - 1)

        @block.scalar
        def _(act):
            act.wait_ge(qkvr_in, 16 * TILES)
            for t in range(TILES):
                act.activation(swish[:, t], r[:, t], ACT.Sigmoid).then_inc(opened, 1)
            chain = Chain(act, gate_act)
            for b, at, width in SPREAD:
                part = decay[:, at:at + width]
                act.wait_ge(biased, b + 1)
                chain.link(act.activation(part, gate[:, at:at + width], ACT.Abs))
                chain.link(act.activation(part, part, ACT.Exp, scale=-1.0))
            for b, at, width in SPREAD:
                part = decay[:, at:at + width]
                chain.mark(act.activation(part, part, ACT.Ln, bias=1.0))
            for b, at, width in SPREAD:
                act.wait_ge(clamped, b + 1)
                cols = slice(at, at + width)
                act.activation(grow[:, cols], gate[:, cols], ACT.Exp).then_inc(grown, 1)
                act.activation(shrink[:, cols], gate[:, cols], ACT.Exp, scale=-1.0).then_inc(grown, 1)
            act.wait_ge(summed, len(SPREAD) + 1)
            act.activation(ends[:].rearrange("p t g c -> p (t g c)"), bank[:, 5, 0:4 * TILES], ACT.Exp).then_inc(ended, 1)
            act.wait_ge(zeroed, 1)
            for t in range(TILES):
                if t > 3:
                    squares(act, t - 4)
                act.wait_ge(turned, t + 1)
                blocks = bank[:, t % 4].rearrange("p (j c) -> p j c", c=P)
                for u in range(2):
                    rows = slice(u * DK, (u + 1) * DK)
                    act.activation(turned_q[rows, t, u], blocks[rows, 0:G], ACT.Copy).then_inc(turned_out, 1)
                act.activation(turned_k[:, t], blocks[:, G:2 * G], ACT.Copy).then_inc(turned_out, 1)
            for t in range(TILES - 4, TILES):
                squares(act, t)

        @block.vector
        def _(dve):
            dve.wait_ge(small_in, 64)
            for b, at, width in SPREAD:
                dve.wait_ge(gated, b + 1)
                dve.tensor_tensor(gate[:, at:at + width], bank[:, b, 0:width],
                                  bias[:].rearrange("p a n -> p (a n)")[:, 0:width], ALU.add).then_inc(biased, 1)
            dve.memset(state[:, 0], 0.0).then_inc(state_zero, 1)
            for b, at, width in SPREAD:
                dve.wait_ge(gate_act, 2 * len(SPREAD) + b + 1)
                cols = slice(at, at + width)
                dve.scalar_tensor_tensor(log_a[:, cols], gate[:, cols], 0.0, decay[:, cols], ALU.min,
                                         ALU.subtract).then_inc(log_done, 1)
            dve.wait_ge(log_done, len(SPREAD))
            for b, at, width in SPREAD:
                dve.wait_ge(summed, b + 1)
                dve.tensor_scalar(gate[:, at:at + width], bank[:, b, 0:width], -LIMIT, LIMIT, ALU.max,
                                  ALU.min).then_inc(clamped, 1)
            chain = Chain(dve, chain_s)
            for t in range(TILES + 2):
                if t < TILES:
                    cols = slice(t * QK, (t + 1) * QK)
                    dve.wait_ge(qkvr_in, 16 * TILES)
                    dve.wait_ge(grown, 2 * (t * QK // N + 1))
                    dve.scalar_tensor_tensor(q[:, t], q[:, t], DK ** -0.5, grow[:, cols], ALU.mult,
                                             ALU.mult).then_inc(scaled, 1)
                    dve.tensor_tensor(k[:, t], k[:, t], shrink[:, cols], ALU.mult).then_inc(scaled, 1)
                if 1 <= t <= TILES:
                    state_step(dve, chain, t - 1)
                if t >= 2:
                    u = t - 2
                    dve.wait_ge(atted, u + 1)
                    if u >= 2:
                        dve.wait_ge(masked, 2 * u - 2)
                    dve.tensor_scalar(clean[:, u % 2], bank[:, 4 + u % 2].rearrange("p (h c) -> p h c", c=P), -3e38,
                                      3e38, ALU.max, ALU.min).then_inc(masked, 1)
                    dve.wait_ge(masked, 2 * u + 1)
                    dve.tensor_tensor(att[:, u], clean[:, u % 2],
                                      s.causal[:].unsqueeze(1).to_broadcast([P, H_A, P]), ALU.mult).then_inc(masked, 1)
                    if u >= 2:
                        output(dve, u - 2)
            output(dve, TILES - 2)
            output(dve, TILES - 1)

        @block.gpsimd
        def _(pool):
            pool.memset(turned_q[:], 0.0).then_inc(zeroed, 1)
            pool.wait_ge(small_in, 64)

            def gains(t):
                pool.wait_ge(opened, t + 1)
                pool.tensor_tensor(swish[:, t], swish[:, t], r[:, t], ALU.mult).then_inc(swish_gain, 1)
                pool.wait_ge(swish_gain, 2 * t + 1)
                heads = swish[:, t].rearrange("p (h v) -> p h v", v=DV)
                pool.tensor_tensor(heads, heads, gain[:].unsqueeze(1).to_broadcast([P, H_A, DV]),
                                   ALU.mult).then_inc(swish_gain, 1)

            for t in range(AHEAD):
                gains(t)
            for t in range(TILES):
                if t + AHEAD < TILES:
                    gains(t + AHEAD)
                pool.wait_ge(summed_sq, t + 1)
                pool.tensor_scalar(stat[:, 1, t], stat[:, 0, t], 1.0 / DV, EPS, ALU.mult, ALU.add).then_inc(rooted, 1)
                pool.wait_ge(rooted, 2 * t + 1)
                pool.tensor_tensor(stat[:, 2, t], stat[:, 1, t], s.root[:], ALU.pow).then_inc(rooted, 1)
                pool.wait_ge(swish_gain, 2 * t + 2)
                pool.wait_ge(scaled_o, t + 1)
                pool.tensor_tensor(swish[:, t], swish[:, t], normed[:, t % 2], ALU.mult).then_inc(gated_o, 1)


def mixers(nc, s, io):
    with ExitStack() as ctx:
        s.qkvr = ctx.enter_context(nc.sbuf_tensor("qkvr", [P, TILES, COL_QB], F32))
        stick(nc, s, io)
        gla(nc, s, io)


def expert_piece(s, io, j, expert):
    place = s.expert_raw[:, j]
    if j < 4:
        first = expert * D + (j // 2) * (D // 2)
        source, width = (io["w_exp_gate"], io["w_exp_up"])[j % 2][bass.ds(first, D // 2), :], FF
    else:
        source, width = io["w_exp_down"][bass.ds(expert * FF + (j - 4) * (2 * P), 2 * P), :], D
    return place.rearrange("p (k n) -> p k n", n=width), source.rearrange("(k p) n -> p k n", p=P)


def merge(nc, s, io):
    PIECES = 2 * KD
    with ExitStack() as ctx:
        sb = lambda name, shape, dt=F32: ctx.enter_context(nc.sbuf_tensor(name, shape, dt))
        sem = semaphores(nc, ctx)
        w_hi = [s.place(nc, f"wm_hi{w}", [P, KD, D], F32R, 2 * w * KD * D) for w in range(2)]
        w_lo = [s.place(nc, f"wm_lo{w}", [P, KD, D], F32R, (2 * w + 1) * KD * D) for w in range(2)]
        w_raw = [s.place(nc, f"wm_raw{w}", [P, KD, D], F32, (2 * w + 1) * KD * D) for w in range(2)]
        o_nat = sb("o_nat", [P, D])
        o_hi, o_lo = sb("o_hi", [P, KD, P], F32R), sb("o_lo", [P, KD, P], F32R)
        gates = sb("gates", [P, 2 * D])
        m, m_b = sb("m", [P, D]), sb("m_b", [P, D])
        m_hi, m_lo = sb("m_hi", [P, KD, P], F32R), sb("m_lo", [P, KD, P], F32R)
        x_t, x_new, h_new = sb("x_t", [P, D]), sb("x_new", [P, D]), sb("h_new", [P, D])
        h_turned = sb("h_turned", [P, KD, P])
        gain = sb("gain_ffn", [P, D])
        w_route, b_route = sb("w_route", [P, KD, ROUTES]), sb("b_route", [P, ROUTES])
        stat = sb("stat_ffn", [P, 3])
        square = sb("square_ffn", [P, D])[:]
        logits, open_l = sb("logits", [P, ROUTES]), sb("open_l", [P, EXPERTS])
        cand, peak = sb("cand", [P, EXPERTS]), sb("peak", [P, 4])
        group_hot = sb("group_hot", [P, GROUPS])
        hot_rows = sb("hot_rows", [P, 2 * TILES, EXPERTS])
        both = sb("both", [P, EXPERTS], BF16)
        place, picked = sb("place", [P, EXPERTS]), sb("picked", [P, 2, EXPERTS])
        slot_f = sb("slot_f", [P, 2, 2])
        slot = sb("slot", [P, TILES, 2], I32)
        late_slot, late_f = sb("late_slot", [P, TILES, 2], I32), sb("late_f", [P, TILES, 2])
        late_pick = m_b[:, 0:2 * TILES * EXPERTS].rearrange("p (c e) -> p c e", e=EXPERTS)
        empty = sb("empty", [P, BLOCKS + 1], I32)
        blocks_i, blocks_f = sb("blocks_i", [P, EXPERTS], I32), sb("blocks_f", [P, 4, EXPERTS])
        behind = m[0:1, 0:(BLOCKS - EXPERTS) * EXPERTS].rearrange("p (b e) -> p b e", e=EXPERTS)
        owner_f = sb("owner_f", [1, BLOCKS])
        y = ctx.enter_context(nc.psum_tensor("y_bank", [P, 2, D], F32))
        turn = ctx.enter_context(nc.psum_tensor("turn_bank", [P, KD, P], F32))
        out = ctx.enter_context(nc.psum_tensor("out_bank", [P, D], F32))

        route_out = out[:, N:N + ROUTES]

        small_in = sem("merge_small_in")
        w_loaded = [sem(f"wm_loaded{j}") for j in range(PIECES)]
        w_high, w_split = sem("wm_high"), sem("wm_split")
        o_in, gates_in, x_in = sem("o_in"), sem("gates_in"), sem("x_in_merge")
        o_turned, o_high, o_low = sem("o_turned"), sem("o_high"), sem("o_low")
        opened, a_done, b_done, m_chain, m_done = (sem("gates_open"), sem("branch_a"), sem("branch_b"), sem("m_chain"),
                                                   sem("m_done"))
        m_turned, m_high, m_low, out_done = sem("m_turned"), sem("m_high"), sem("m_low"), sem("out_done")
        x_done, squared, meaned, rooted, h_done = (sem("x_done"), sem("squared_ffn"), sem("meaned"), sem("rooted_ffn"),
                                                   sem("h_done"))
        h_turned_s, h_out, routed, logits_read = sem("h_turned_s"), sem("h_out"), sem("routed"), sem("logits_read")
        route_chain, hot_done, counted, counts_read = (sem("route_chain"), sem("hot_done"), sem("counted"),
                                                       sem("counts_read"))
        place_chain, slots_ready, late_chain = sem("place_chain"), sem("slots_ready"), sem("late_chain")
        x_stored, h_stored, cleared = sem("x_stored"), sem("h_stored"), sem("carry_cleared")
        empty_set, table_cleared, scattered, late_ready = (sem("empty_set"), sem("table_cleared"), sem("scattered"),
                                                           sem("late_ready"))
        block = ctx.enter_context(nc.Block())

        def load_tile(sp, t, kind, sample=False):
            if kind == "o":
                sp.dma_start(o_nat[:], io["mixed"][bass.ds(t * P, P), :]).then_inc(o_in, 16)
            elif kind == "gates":
                sp.dma_start(gates[:], io["projected"][bass.ds(t * P, P), COL_GATES:MAIN]).then_inc(gates_in, 16)
            else:
                src = io["x_rows"] if sample else io["x_prompt"]
                sp.dma_start(x_t[:], src[bass.ds(t * P, P), :]).then_inc(x_in, 16)

        def feed(sp, t, gates_next=True, o_after=True, output=True, x_next="prompt"):
            if gates_next:
                sp.wait_ge(m_done, t + 1)
                load_tile(sp, t + 1, "gates")
            if o_after:
                sp.wait_ge(o_turned, t + 2)
                load_tile(sp, t + 2, "o")
            if output:
                sp.wait_ge(x_done, t)
                sp.dma_start(io["x_mid"][bass.ds((t - 1) * P, P), :], x_new[:]).then_inc(x_stored, 16)
                if x_next:
                    load_tile(sp, t, "x", x_next == "sample")
                sp.wait_ge(h_done, t)
                sp.dma_start(io["h_mid"][bass.ds((t - 1) * P, P), :], h_new[:]).then_inc(h_stored, 16)

        @block.sync
        def _(sp):
            load_tile(sp, 0, "o")
            load_tile(sp, 0, "gates")
            load_tile(sp, 0, "x")
            for j in range(PIECES):
                src = (io["w_branch"], io["w_out"])[j // KD]
                sp.dma_start(w_raw[j // KD][:, j % KD], src[j % KD * P:(j % KD + 1) * P, :])\
                    .then_inc(w_loaded[j], 16)
                if j == 0:
                    sp.dma_start(gain[:], io["norm_ffn_gain"].partition_broadcast(P)).then_inc(small_in, 16)
                    sp.dma_start(b_route[:], io["b_router"].partition_broadcast(P)).then_inc(small_in, 16)
                    sp.dma_start(w_route[:], io["w_router"].rearrange("(k p) n -> p k n", p=P)).then_inc(small_in, 16)
            sp.wait_ge(o_turned, 1)
            load_tile(sp, 1, "o")
            feed(sp, 0, output=False)
            with sp.Fori(1, SAMPLE - 1) as t:
                feed(sp, t)
            feed(sp, SAMPLE - 1, o_after=False)
            feed(sp, SAMPLE, gates_next=False, o_after=False, x_next="sample")
            feed(sp, SAMPLE + 1, gates_next=False, o_after=False, x_next=None)
            sp.wait_ge(b_done, TILES)
            for j in range(6):
                sp.dma_start(*expert_piece(s, io, j, 0)).then_inc(s.first_loaded, 16)
            sp.wait_ge(x_stored, 16 + 16 * TILES)
            sp.wait_ge(h_stored, 16 + 16 * TILES)

        def branch(pe, which):
            for n in range(D // N):
                cols = slice(n * N, (n + 1) * N)
                for k in range(which * KD // 2, (which + 1) * KD // 2):
                    first, final = k % 4 == 0, k % 4 == 3
                    pe.matmul(y[:, which, cols], o_hi[:, k], w_hi[0][:, k, cols], start=first, stop=False)
                    pe.matmul(y[:, which, cols], o_hi[:, k], w_lo[0][:, k, cols], start=False, stop=False)
                    last = pe.matmul(y[:, which, cols], o_lo[:, k], w_hi[0][:, k, cols], start=False, stop=final)
            return last

        def turned(pe, source):
            for k in range(KD):
                last = pe.transpose(turn[:, k], source[:, k * P:(k + 1) * P], s.ident[:])
            return last

        def output_half(pe, n):
            cols = slice(n * N, (n + 1) * N)
            for k in range(KD):
                pe.matmul(out[:, cols], m_hi[:, k], w_hi[1][:, k, cols], start=(k == 0), stop=False)
                pe.matmul(out[:, cols], m_hi[:, k], w_lo[1][:, k, cols], start=False, stop=False)
                last = pe.matmul(out[:, cols], m_lo[:, k], w_hi[1][:, k, cols], start=False, stop=(k == KD - 1))
            return last

        def turn_h(pe, t):
            pe.wait_ge(h_done, t + 1)
            turned(pe, h_new).then_inc(h_turned_s, 1)

        def route(pe, t):
            pe.wait_ge(h_out, t + 1)
            for k in range(KD):
                last = pe.matmul(route_out, h_turned[:, k], w_route[:, k], start=(k == 0), stop=(k == KD - 1))
            last.then_inc(routed, 1)

        def count(pe, t):
            pe.wait_ge(hot_done, t + 1)
            pe.matmul(y[:, 1, 0:EXPERTS], s.before_b[:], both[:], start=True, stop=True)
            pe.matmul(y[:, 1, EXPERTS:2 * EXPERTS], s.ones_b[:], both[:], start=True, stop=True).then_inc(counted, 1)

        def step_pe(pe, t, branches=True, o_next=True, output=True, routes=True):
            if branches:
                pe.wait_ge(o_low, t + 1)
                branch(pe, 0).then_inc(a_done, 1)
            if output and not branches:
                pe.wait_ge(m_low, t)
                output_half(pe, 0)
            if routes:
                pe.wait_ge(m_low, t if branches else TILES)
                turn_h(pe, t - 2)
                pe.wait_ge(counts_read, t - 1)
            if branches:
                branch(pe, 1).then_inc(b_done, 1)
            if routes:
                route(pe, t - 2)
            if output and branches:
                pe.wait_ge(m_low, t)
                output_half(pe, 0)
            if o_next:
                pe.wait_ge(o_in, t * 16 + 32)
                turned(pe, o_nat).then_inc(o_turned, 1)
            if output:
                if routes:
                    pe.wait_ge(logits_read, t - 1)
                output_half(pe, 1).then_inc(out_done, 1)
            if branches:
                pe.wait_ge(m_done, t + 1)
                if o_next:
                    pe.wait_ge(o_low, t + 2)
                turned(pe, m).then_inc(m_turned, 1)
            if routes:
                count(pe, t - 2)

        @block.tensor
        def _(pe):
            pe.wait_ge(o_in, 16)
            turned(pe, o_nat).then_inc(o_turned, 1)
            pe.wait_ge(w_split, KD)
            step_pe(pe, 0, output=False, routes=False)
            pe.wait_ge(w_split, PIECES)
            step_pe(pe, 1, routes=False)
            pe.wait_ge(small_in, 48)
            with pe.Fori(2, SAMPLE) as t:
                step_pe(pe, t)
            step_pe(pe, SAMPLE, o_next=False)
            step_pe(pe, SAMPLE + 1, branches=False, o_next=False)
            step_pe(pe, SAMPLE + 2, branches=False, o_next=False, output=False)

        def h_evac(act, t):
            act.wait_ge(h_turned_s, t + 1)
            act.activation(h_turned[:], turn[:], ACT.Copy).then_inc(h_out, 1)

        def step_act(act, t, branches=True, o_next=True, output=True, routes=True):
            if routes:
                h_evac(act, t - 2)
            if o_next:
                act.wait_ge(o_turned, t + 2)
                act.activation(o_hi[:], turn[:], ACT.Copy).then_inc(o_high, 1)
                act.wait_ge(gates_in, t * 16 + 32)
                act.activation(gates[:], gates[:], ACT.Sigmoid).then_inc(opened, 1)
            if branches:
                act.wait_ge(m_turned, t + 1)
                act.activation(m_hi[:], turn[:], ACT.Copy).then_inc(m_high, 1)
            if output:
                act.wait_ge(x_done, t)
                act.wait_ge(meaned, t)
                act.activation(square, x_new[:], ACT.Square, accum_out=stat[:, 0:1]).then_inc(squared, 1)

        @block.scalar
        def _(act):
            act.sem_inc(x_stored, 16)
            act.sem_inc(h_stored, 16)
            act.sem_inc(meaned, 1)
            for j in range(PIECES):
                if j == 1:
                    act.wait_ge(gates_in, 16)
                    act.activation(gates[:], gates[:], ACT.Sigmoid).then_inc(opened, 1)
                    act.wait_ge(o_turned, 1)
                    act.activation(o_hi[:], turn[:], ACT.Copy).then_inc(o_high, 1)
                act.wait_ge(w_loaded[j], 16)
                act.activation(w_hi[j // KD][:, j % KD], w_raw[j // KD][:, j % KD],
                               ACT.Copy).then_inc(w_high, 1)
            step_act(act, 0, output=False, routes=False)
            step_act(act, 1, routes=False)
            with act.Fori(2, SAMPLE) as t:
                step_act(act, t)
            step_act(act, SAMPLE, o_next=False)
            step_act(act, SAMPLE + 1, branches=False, o_next=False)
            step_act(act, SAMPLE + 2, branches=False, o_next=False, output=False)

        def first_peak(dve, chain, values, width, top, number, iota):
            chain.link(dve.tensor_reduce(top, values, X, ALU.max))
            chain.link(dve.tensor_scalar(cand[:, 0:width], values, top, 64.0, ALU.is_lt, ALU.mult))
            chain.link(dve.tensor_tensor(cand[:, 0:width], cand[:, 0:width], iota, ALU.add))
            chain.link(dve.tensor_reduce(number, cand[:, 0:width], X, ALU.min))

        def choose(dve, t, base):
            chain = Chain(dve, route_chain, base)
            iota_e, iota_g = s.iota[:, 0:EXPERTS], s.iota[:, EXPERTS:]
            first_peak(dve, chain, logits[:, EXPERTS:], GROUPS, peak[:, 0:1], peak[:, 1:2], iota_g)
            chain.mark(dve.tensor_scalar(s.group_rel[:, bass.ds(t, 1)].rearrange("p a g -> p (a g)"), logits[:, EXPERTS:],
                                         peak[:, 0:1], None, ALU.subtract))
            chain.link(dve.tensor_scalar(group_hot[:], iota_g, peak[:, 1:2], None, ALU.is_equal))
            chain.link(dve.tensor_scalar(group_hot[:], group_hot[:], -1.0, -MASKED, ALU.add, ALU.mult))
            chain.link(dve.tensor_tensor(open_l[:].rearrange("p (g e) -> p g e", e=PER_GROUP),
                                         logits[:, 0:EXPERTS].rearrange("p (g e) -> p g e", e=PER_GROUP),
                                         group_hot[:].unsqueeze(2).to_broadcast([P, GROUPS, PER_GROUP]), ALU.add))
            for j in range(2):
                number = s.number[:, bass.ds(t * 2 + j, 1)]
                first_peak(dve, chain, open_l[:], EXPERTS, peak[:, 2 + j:3 + j], number, iota_e)
                hot = hot_rows[:, bass.ds(t * 2 + j, 1)].rearrange("p a e -> p (a e)")
                chain.link(dve.tensor_scalar(hot, iota_e, number, None, ALU.is_equal))
                if j == 0:
                    chain.link(dve.scalar_tensor_tensor(open_l[:], hot, 3 * MASKED, open_l[:], ALU.mult, ALU.add))
            chain.mark(dve.tensor_tensor(s.gap[:, bass.ds(t, 1)], peak[:, 2:3], peak[:, 3:4], ALU.subtract))
            hots = hot_rows[:, bass.ds(t * 2, 2)]
            chain.link(dve.tensor_scalar(hots, hots, s.valid[:, bass.ds(t, 1)], None, ALU.mult))
            dve.tensor_tensor(both[:], hot_rows[:, bass.ds(t * 2, 1)].rearrange("p a e -> p (a e)"),
                              hot_rows[:, bass.ds(t * 2 + 1, 1)].rearrange("p a e -> p (a e)"), ALU.add).then_inc(hot_done, 1)
            return chain.count

        def assign(dve, t, base):
            chain = Chain(dve, place_chain, base)
            dve.wait_ge(counted, t + 1)
            chain.link(dve.tensor_tensor(place[:], y[:, 1, 0:EXPERTS], s.carry[:], ALU.add))
            dve.tensor_tensor(s.carry[:], s.carry[:], y[:, 1, EXPERTS:2 * EXPERTS], ALU.add).then_inc(counts_read, 1)
            chain.link(dve.tensor_tensor(picked[:], hot_rows[:, bass.ds(t * 2, 2)],
                                         place[:].unsqueeze(1).to_broadcast([P, 2, EXPERTS]), ALU.mult))
            at = s.at[:, bass.ds(t * 2, 2)]
            chain.link(dve.tensor_reduce(at, picked[:], X, ALU.add))
            chain.mark(dve.tensor_scalar(slot_f[:, 0], at, float(P), float(NOWHERE), ALU.is_ge, ALU.mult))
            chain.link(dve.scalar_tensor_tensor(slot_f[:, 1], s.number[:, bass.ds(t * 2, 2)], float(P), at, ALU.mult,
                                                ALU.add))
            dve.scalar_tensor_tensor(slot[:, bass.ds(t, 1)].rearrange("p a k -> p (a k)"), slot_f[:, 0],
                                     s.nowhere[:, bass.ds(t, 1)], slot_f[:, 1], ALU.add, ALU.add).then_inc(slots_ready, 1)
            return chain.count

        ROUTE_LINKS, PLACE_LINKS = 21, 5

        def read_logits(dve, t):
            dve.wait_ge(routed, t + 1)
            dve.tensor_tensor(logits[:], route_out, b_route[:], ALU.add).then_inc(logits_read, 1)

        def step_dve(dve, t, branches=True, o_next=True, output=True, routes=True):
            if branches:
                chain = Chain(dve, m_chain, t * 2)
                dve.wait_ge(a_done, t + 1)
                dve.wait_ge(opened, t + 1)
                chain.mark(dve.tensor_tensor(m[:], y[:, 0], gates[:, 0:D], ALU.mult))
                dve.wait_ge(b_done, t + 1)
                chain.link(dve.tensor_tensor(m_b[:], y[:, 1], gates[:, D:], ALU.mult))
                dve.tensor_tensor(m[:], m[:], m_b[:], ALU.add).then_inc(m_done, 1)
            if routes:
                read_logits(dve, t - 2)
                dve.wait_ge(logits_read, t - 1)
                assert choose(dve, t - 2, (t - 2) * ROUTE_LINKS) == ROUTE_LINKS
            if o_next:
                dve.wait_ge(o_high, t + 2)
                dve.tensor_tensor(o_lo[:], turn[:], o_hi[:].bitcast(F32), ALU.subtract).then_inc(o_low, 1)
            if output:
                dve.wait_ge(out_done, t)
                dve.wait_ge(x_in, t * 16)
                dve.wait_ge(x_stored, t * 16)
                dve.tensor_tensor(x_new[:], out[:], x_t[:], ALU.add).then_inc(x_done, 1)
            if branches:
                dve.wait_ge(m_high, t + 1)
                dve.tensor_tensor(m_lo[:], turn[:], m_hi[:].bitcast(F32), ALU.subtract).then_inc(m_low, 1)
            if output:
                dve.wait_ge(squared, t)
                dve.tensor_scalar(stat[:, 1:2], stat[:, 0:1], 1.0 / D, EPS, ALU.mult, ALU.add).then_inc(meaned, 1)
                dve.wait_ge(rooted, t)
                dve.wait_ge(h_stored, t * 16)
                dve.scalar_tensor_tensor(h_new[:], x_new[:], stat[:, 2:3], gain[:], ALU.mult, ALU.mult).then_inc(h_done, 1)
            if routes:
                assert assign(dve, t - 2, (t - 2) * PLACE_LINKS) == PLACE_LINKS

        def late(dve):
            chain = Chain(dve, late_chain)
            dve.wait_ge(counts_read, TILES + 1)
            dve.wait_ge(place_chain, TILES * PLACE_LINKS)
            extra, upto, start, zero = (blocks_f[:, j] for j in range(4))
            chain.link(dve.tensor_scalar(blocks_i[:], s.carry[:], float(P - 1), None, ALU.add))
            chain.link(dve.tensor_scalar(blocks_i[:], blocks_i[:], 7, None, ALU.arith_shift_right))
            chain.link(dve.tensor_scalar(extra, blocks_i[:], -1.0, 0.0, ALU.add, ALU.max))
            chain.link(dve.memset(zero, 0.0))
            chain.link(dve.tensor_tensor_scan(upto, extra, zero, zero[:, 0:1], ALU.add, ALU.add))
            chain.link(dve.tensor_tensor(start, upto, extra, ALU.subtract))
            chain.link(dve.tensor_scalar(start, start, float(EXPERTS - 1), float(P), ALU.add, ALU.mult))
            chain.link(dve.tensor_tensor(late_pick, hot_rows[:], start.unsqueeze(1).to_broadcast([P, 2 * TILES, EXPERTS]),
                                         ALU.mult))
            pick = late_f[:].rearrange("p t k -> p (t k)")
            chain.link(dve.tensor_reduce(pick, late_pick, X, ALU.add))
            chain.link(dve.tensor_tensor(pick, pick, s.at[:], ALU.add))
            early = late_pick[:, 0, 0:2 * TILES]
            chain.link(dve.tensor_scalar(early, s.at[:], float(P), float(NOWHERE), ALU.is_lt, ALU.mult))
            chain.link(dve.tensor_tensor(late_slot[:].rearrange("p t k -> p (t k)"), pick, early, ALU.add))
            more = BLOCKS - EXPERTS
            chain.link(dve.tensor_tensor(behind, upto[0:1, :].unsqueeze(1).to_broadcast([1, more, EXPERTS]),
                                         s.iota[0:1, 0:more].unsqueeze(2).to_broadcast([1, more, EXPERTS]), ALU.is_le))
            chain.link(dve.tensor_reduce(owner_f[:, EXPERTS:], behind, X, ALU.add))
            chain.link(dve.tensor_scalar(owner_f[:, EXPERTS:], owner_f[:, EXPERTS:], float(EXPERTS - 1), None, ALU.min))
            chain.link(dve.tensor_copy(owner_f[:, 0:EXPERTS], s.iota[0:1, 0:EXPERTS]))
            chain.link(dve.tensor_copy(s.owner[:, 0:BLOCKS], owner_f[:]))
            chain.link(dve.tensor_scalar(s.owner[:, BLOCKS:BLOCKS + 1], upto[0:1, EXPERTS - 1:EXPERTS], float(EXPERTS),
                                         None, ALU.add))
            dve.tensor_copy(s.owner[:, BLOCKS + 1:BLOCKS + 2], upto[0:1, EXPERTS - 1:EXPERTS]).then_inc(late_ready, 1)
            dve.wait_ge(late_ready, 1)

        def scatter(pool, slots, t):
            rows = DEC if t == SAMPLE else P
            for j in range(2):
                pool.indirect_dma_start(io["slot_table"], bass.IndirectOffsetOnAxis(ap=slots[0:rows, t, j:j + 1], axis=0),
                                        s.assignment[0:rows, t, j:j + 1], None, bounds_check=SLOTS - 1,
                                        oob_is_err=False).then_inc(scattered, 16)

        @block.vector
        def _(dve):
            dve.sem_inc(counts_read, 1)
            dve.memset(s.carry[:], 0.0).then_inc(cleared, 1)
            dve.wait_ge(cleared, 1)
            for j in range(PIECES):
                if j == 1:
                    dve.wait_ge(o_high, 1)
                    dve.tensor_tensor(o_lo[:], turn[:], o_hi[:].bitcast(F32), ALU.subtract).then_inc(o_low, 1)
                dve.wait_ge(w_high, j + 1)
                dve.tensor_tensor(w_lo[j // KD][:, j % KD], w_raw[j // KD][:, j % KD],
                                  w_hi[j // KD][:, j % KD].bitcast(F32), ALU.subtract).then_inc(w_split, 1)
            dve.wait_ge(small_in, 48)
            step_dve(dve, 0, output=False, routes=False)
            step_dve(dve, 1, routes=False)
            with dve.Fori(2, SAMPLE) as t:
                step_dve(dve, t)
            step_dve(dve, SAMPLE, o_next=False)
            step_dve(dve, SAMPLE + 1, branches=False, o_next=False)
            step_dve(dve, SAMPLE + 2, branches=False, o_next=False, output=False)
            late(dve)

        @block.gpsimd
        def _(pool):
            pool.memset(empty[:], NOWHERE).then_inc(empty_set, 1)
            pool.wait_ge(empty_set, 1)
            pool.dma_start(io["slot_table"].rearrange("(p b) a -> p (b a)", p=P), empty[:]).then_inc(table_cleared, 16)
            for t in range(TILES + 1):
                if t < TILES:
                    pool.wait_ge(meaned, t + 2)
                    pool.tensor_tensor(stat[:, 2:3], stat[:, 1:2], s.root[:, 0:1], ALU.pow).then_inc(rooted, 1)
                if t:
                    pool.wait_ge(slots_ready, t)
                    if t == 1:
                        pool.wait_ge(table_cleared, 16)
                    scatter(pool, slot, t - 1)
            pool.wait_ge(late_ready, 1)
            more = pool.value_load(s.owner[0:1, BLOCKS + 1:BLOCKS + 2])
            with pool.If(more > 0):
                for t in range(TILES):
                    scatter(pool, late_slot, t)
                pool.wait_ge(scattered, 16 * 4 * TILES)
            pool.wait_ge(scattered, 16 * 2 * TILES)


def experts(nc, s, io):
    G0, U0, G1, U1, D0, D1 = range(6)
    HALF = KD // 2
    FK = FF // P
    with ExitStack() as ctx:
        sb = lambda name, shape, dt=F32: ctx.enter_context(nc.sbuf_tensor(name, shape, dt))
        sem = semaphores(nc, ctx)
        w_raw, w_hi = s.expert_raw, s.place(nc, "we_hi", [P, 6, 4 * N], F32R, 2 * KD * D)
        w_lo = sb("we_lo", [P, 6, 4 * N], F32R)
        x_nat = s.place(nc, "x_nat", [P, D], F32, 24 * N)[:]
        y_out = s.place(nc, "y_out", [P, D], F32, 24 * N + D)[:]
        x_hi, x_lo = sb("x_hi", [P, KD, P], F32R), sb("x_lo", [P, KD, P], F32R)
        opened, hidden = sb("opened", [P, FF]), sb("hidden", [P, FF])
        a_hi, a_lo = sb("a_hi", [P, FK, P], F32R), sb("a_lo", [P, FK, P], F32R)
        table_i, table_f = sb("table_i", [BLOCKS + 1, P], I32), sb("table_f", [BLOCKS + 1, P])
        choice, frame = sb("choice", [P, BLOCKS + 1], I32), sb("frame", [P, BLOCKS + 1], I32)
        gather_at, scatter_at = sb("gather_at", [P, 1], I32), sb("scatter_at", [P, 1], I32)
        gu = ctx.enter_context(nc.psum_tensor("gu_bank", [P, 2, N], F32))
        y = ctx.enter_context(nc.psum_tensor("ye_bank", [P, D], F32))
        turn_x = ctx.enter_context(nc.psum_tensor("turn_x", [P, KD, P], F32))
        turn_a = ctx.enter_context(nc.psum_tensor("turn_a", [P, FK, P], F32))
        table_t = turn_a[:, 0, 0:BLOCKS + 1]

        table_in, table_cast, table_turned, choice_ready, frame_ready = (
            sem("table_in"), sem("table_cast"), sem("table_turned"), sem("choice_ready"), sem("frame_ready"))
        x_zeroed = sem("x_nat_zeroed")
        loaded = [sem(f"we_loaded{j}") for j in range(6)]
        high = [sem(f"we_high{j}") for j in range(6)]
        split = [sem(f"we_split{j}") for j in range(6)]
        gathered, x_turned, x_high, x_low = sem("gathered"), sem("x_turned"), sem("x_high"), sem("x_low")
        gu_used, d_used = sem("gu_used"), sem("d_used")
        sig_done, gated, a_done, a_turned, a_high, a_low = (sem("sig_done"), sem("gated_e"), sem("a_done"),
                                                            sem("a_turned"), sem("a_high"), sem("a_low"))
        y_moved, y_scattered = sem("y_moved"), sem("y_scattered")
        gather_set, scatter_set = sem("gather_set"), sem("scatter_set")
        gather_begun, scatter_begun = sem("gather_begun"), sem("scatter_begun")
        block = ctx.enter_context(nc.Block())

        def count_of(engine):
            return engine.value_load(s.owner[0:1, BLOCKS + 1:BLOCKS + 2], min_val=0, max_val=BLOCKS - EXPERTS) + EXPERTS

        def load_piece(sp, j, b, expert):
            sp.wait_ge(split[j], b + 1)
            sp.dma_start(*expert_piece(s, io, j, expert)).then_inc(loaded[j], 16)

        def owner_of(sp, b):
            return sp.value_load(s.owner[0:1, bass.ds(b, 1)], min_val=0, max_val=EXPERTS - 1)

        @block.sync
        def _(sp):
            sp.dma_start(table_i[:], io["slot_table"].rearrange("(b p) a -> b (p a)", p=P)).then_inc(table_in, 16)
            for b in (1, 2):
                for j in (G0, U0, G1, U1):
                    load_piece(sp, j, b, b)
            end = count_of(sp)
            with sp.Fori(1, end - 2) as i:
                now, later = owner_of(sp, i), owner_of(sp, i + 2)
                for j, b, expert in ((D0, i, now), (G0, i + 2, later), (D1, i, now), (U0, i + 2, later),
                                     (G1, i + 2, later), (U1, i + 2, later)):
                    load_piece(sp, j, b, expert)
            for back in (2, 1):
                expert = owner_of(sp, end - back)
                for j in (D0, D1):
                    load_piece(sp, j, end - back, expert)
            for t in range(SAMPLE):
                if t >= 4 and t % 2 == 0:
                    sp.wait_ge(split[(t - 4) // 2], end + 1)
                sp.dma_start(s.x_early[t][:], io["x_mid"][t * P:(t + 1) * P, :]).then_inc(s.x_early_in, 16)

        def turn_rows(pe, i):
            pe.wait_ge(gathered, i * 16 + 16)
            pe.wait_ge(x_low, i)
            for k in range(KD):
                last = pe.transpose(turn_x[:, k], x_nat[:, k * P:(k + 1) * P], s.ident[:])
            last.then_inc(x_turned, 1)

        def gate_up(pe, i):
            pe.wait_ge(x_low, i + 1)
            pe.wait_ge(a_done, i)
            for j in (G0, U0, G1, U1):
                pe.wait_ge(split[j], i + 2)
                for kk in range(HALF):
                    k = (j // 2) * HALF + kk
                    cols = slice(kk * FF, (kk + 1) * FF)
                    out = gu[:, j % 2]
                    pe.matmul(out, x_hi[:, k], w_hi[:, j, cols], start=(k == 0), stop=False)
                    pe.matmul(out, x_hi[:, k], w_lo[:, j, cols], start=False, stop=False)
                    last = pe.matmul(out, x_lo[:, k], w_hi[:, j, cols], start=False, stop=(k == KD - 1))
                last.then_inc(gu_used, 1)

        def down(pe, i):
            pe.wait_ge(a_low, i + 1)
            pe.wait_ge(y_moved, i + 1)
            for j in (D0, D1):
                pe.wait_ge(split[j], i + 2)
                for kk in range(2):
                    k = (j - D0) * 2 + kk
                    for n in range(2):
                        cols = slice(kk * D + n * N, kk * D + (n + 1) * N)
                        out = y[:, n * N:(n + 1) * N]
                        pe.matmul(out, a_hi[:, k], w_hi[:, j, cols], start=(k == 0), stop=False)
                        pe.matmul(out, a_hi[:, k], w_lo[:, j, cols], start=False, stop=False)
                        last = pe.matmul(out, a_lo[:, k], w_hi[:, j, cols], start=False, stop=(k == FK - 1))
                last.then_inc(d_used, 1)

        def turn_hidden(pe, i):
            pe.wait_ge(a_done, i + 1)
            pe.wait_ge(a_low, i)
            for k in range(FK):
                last = pe.transpose(turn_a[:, k], hidden[:, k * P:(k + 1) * P], s.ident[:])
            last.then_inc(a_turned, 1)

        @block.tensor
        def _(pe):
            pe.sem_inc(gu_used, 4)
            pe.sem_inc(d_used, 2)
            pe.wait_ge(table_cast, 1)
            pe.transpose(table_t, table_f[:], s.ident[0:BLOCKS + 1, 0:BLOCKS + 1]).then_inc(table_turned, 1)
            end = count_of(pe)
            turn_rows(pe, 0)
            gate_up(pe, 0)
            turn_rows(pe, 1)
            turn_hidden(pe, 0)
            with pe.Fori(1, end - 1) as i:
                gate_up(pe, i)
                turn_rows(pe, i + 1)
                down(pe, i - 1)
                turn_hidden(pe, i)
            gate_up(pe, end - 1)
            down(pe, end - 2)
            turn_hidden(pe, end - 1)
            down(pe, end - 1)

        def high_part(act, j, b, first=False):
            if first:
                act.wait_ge(s.first_loaded, 16 * 6)
            else:
                act.wait_ge(loaded[j], b * 16)
            if j < D0:
                act.wait_ge(gu_used, b * 4 + (j + 1))
            else:
                act.wait_ge(d_used, b * 2 + (j - D0 + 1))
            act.activation(w_hi[:, j], w_raw[:, j], ACT.Copy).then_inc(high[j], 1)

        def rows_high(act, i):
            act.wait_ge(x_turned, i + 1)
            act.wait_ge(gu_used, i * 4 + 4)
            act.activation(x_hi[:], turn_x[:], ACT.Copy).then_inc(x_high, 1)

        def sigmoid(act, i):
            act.wait_ge(gu_used, i * 4 + 8)
            act.wait_ge(gated, i)
            act.activation(opened[:], gu[:, 0], ACT.Sigmoid).then_inc(sig_done, 1)

        def hidden_high(act, i):
            act.wait_ge(a_turned, i + 1)
            act.wait_ge(d_used, i * 2 + 2)
            act.activation(a_hi[:], turn_a[:], ACT.Copy).then_inc(a_high, 1)

        def move_y(act, i, first=False):
            act.wait_ge(d_used, i * 2 + 4)
            if not first:
                act.wait_ge(y_scattered, i * 16)
            act.activation(y_out, y[:], ACT.Copy).then_inc(y_moved, 1)

        def block_act(act, i, hidden_before=True, y_before=True, first_y=False, last=False, first=False):
            if hidden_before:
                hidden_high(act, i - 1)
            if y_before:
                move_y(act, i - 2, first_y)
            if hidden_before:
                high_part(act, D0, i - 1, first)
            if not last:
                high_part(act, G0, i + 1)
            if hidden_before:
                high_part(act, D1, i - 1, first)
            if not last:
                high_part(act, U0, i + 1)
                high_part(act, G1, i + 1)
            sigmoid(act, i)
            if not last:
                high_part(act, U1, i + 1)
                rows_high(act, i + 1)

        @block.scalar
        def _(act):
            end = count_of(act)
            act.sem_inc(y_moved, 1)
            for j in (G0, U0, G1, U1):
                high_part(act, j, 0, first=True)
            rows_high(act, 0)
            block_act(act, 0, hidden_before=False, y_before=False)
            block_act(act, 1, y_before=False, first=True)
            block_act(act, 2, first_y=True)
            with act.Fori(3, end - 1) as i:
                block_act(act, i)
            block_act(act, end - 1, last=True)
            hidden_high(act, end - 1)
            move_y(act, end - 2)
            high_part(act, D0, end - 1)
            high_part(act, D1, end - 1)
            move_y(act, end - 1)

        def low_part(engine, j, b):
            engine.wait_ge(high[j], b + 1)
            engine.tensor_tensor(w_lo[:, j], w_raw[:, j], w_hi[:, j].bitcast(F32), ALU.subtract).then_inc(split[j], 1)

        def rows_low(dve, i):
            dve.wait_ge(x_high, i + 1)
            dve.tensor_tensor(x_lo[:], turn_x[:], x_hi[:].bitcast(F32), ALU.subtract).then_inc(x_low, 1)

        def hide(dve, i):
            dve.wait_ge(sig_done, i + 1)
            dve.wait_ge(a_turned, i)
            dve.tensor_tensor(hidden[:], gu[:, 0], opened[:], ALU.mult).then_inc(gated, 1)
            dve.wait_ge(gated, i + 1)
            dve.tensor_tensor(hidden[:], hidden[:], gu[:, 1], ALU.mult).then_inc(a_done, 1)

        def hidden_low(dve, i):
            dve.wait_ge(a_high, i + 1)
            dve.tensor_tensor(a_lo[:], turn_a[:], a_hi[:].bitcast(F32), ALU.subtract).then_inc(a_low, 1)

        def block_dve(dve, i, hidden_before=True, last=False):
            if hidden_before:
                hidden_low(dve, i - 1)
                low_part(dve, D0, i - 1)
            if not last:
                for j in (G0, U0, G1):
                    low_part(dve, j, i + 1)
            hide(dve, i)
            if not last:
                low_part(dve, U1, i + 1)
                rows_low(dve, i + 1)

        @block.vector
        def _(dve):
            for j in range(6):
                dve.sem_inc(split[j], 1)
            dve.memset(x_nat, 0.0).then_inc(x_zeroed, 1)
            dve.wait_ge(table_in, 16)
            dve.tensor_copy(table_f[:], table_i[:]).then_inc(table_cast, 1)
            dve.wait_ge(table_turned, 1)
            dve.tensor_copy(choice[:], table_t).then_inc(choice_ready, 1)
            dve.wait_ge(choice_ready, 1)
            dve.tensor_scalar(frame[:], choice[:], 1, None, ALU.arith_shift_right).then_inc(frame_ready, 1)
            end = count_of(dve)
            for j in (G0, U0, G1, U1):
                low_part(dve, j, 0)
            rows_low(dve, 0)
            block_dve(dve, 0, hidden_before=False)
            with dve.Fori(1, end - 1) as i:
                block_dve(dve, i)
            block_dve(dve, end - 1, last=True)
            hidden_low(dve, end - 1)
            low_part(dve, D0, end - 1)

        @block.gpsimd
        def _(pool):
            pool.wait_ge(frame_ready, 1)
            pool.wait_ge(x_zeroed, 1)
            last_choice, last_frame = pool.to_reg(ASSIGNED - 1), pool.to_reg(SEQ + DEC - 1)
            end = count_of(pool)

            def gather(pool, i):
                pool.wait_ge(x_turned, i)
                pool.tensor_copy(gather_at[:], frame[:, bass.ds(i, 1)]).then_inc(gather_set, 1)
                pool.wait_ge(gather_set, i + 1)
                pool.sem_inc(gather_begun, 1)
                pool.indirect_dma_start(x_nat, None, io["h_mid"], bass.IndirectOffsetOnAxis(ap=gather_at[:], axis=0),
                                        bounds_check=last_frame, oob_is_err=False).then_inc(gathered, 16)

            def scatter_y(pool, i):
                pool.wait_ge(y_moved, i + 2)
                pool.tensor_copy(scatter_at[:], choice[:, bass.ds(i, 1)]).then_inc(scatter_set, 1)
                pool.wait_ge(scatter_set, i + 1)
                pool.sem_inc(scatter_begun, 1)
                pool.indirect_dma_start(io["expert_rows"], bass.IndirectOffsetOnAxis(ap=scatter_at[:], axis=0), y_out, None,
                                        bounds_check=last_choice, oob_is_err=False).then_inc(y_scattered, 16)

            gather(pool, 0)
            gather(pool, 1)
            gather(pool, 2)
            low_part(pool, D1, 0)
            gather(pool, 3)
            with pool.Fori(2, end - 1) as i:
                scatter_y(pool, i - 2)
                low_part(pool, D1, i - 1)
                gather(pool, i + 2)
            scatter_y(pool, end - 3)
            low_part(pool, D1, end - 2)
            scatter_y(pool, end - 2)
            low_part(pool, D1, end - 1)
            scatter_y(pool, end - 1)
            pool.wait_ge(y_scattered, end * 16)
            pool.wait_ge(gathered, end * 16 + 16)


def feed_forward(nc, s, io):
    with ExitStack() as ctx:
        s.room_at = (nc.sbuf_base + 31) // 32 * 32
        ctx.enter_context(nc.sbuf_tensor("weights_room", [P, 4, KD * D], F32))
        s.expert_raw = s.place(nc, "we_raw", [P, 6, 4 * N], F32, 0)
        merge(nc, s, io)
        s.x_early = [s.place(nc, f"x_final{t}", [P, D], F32, place * D)
                     for t, place in enumerate([4 * KD - 4 + t for t in range(4)] + list(range(SAMPLE - 4)))]
        experts(nc, s, io)
        final(nc, s, io)


def final(nc, s, io):
    with ExitStack() as ctx:
        sb = lambda name, shape, dt=F32: ctx.enter_context(nc.sbuf_tensor(name, shape, dt))
        sem = semaphores(nc, ctx)
        x = s.x_early + [sb("x_final_sample", [P, D])]
        rows = s.place(nc, "rows_final", [P, TILES, 2, D], F32, 2 * 4 * N)
        square = sb("square_final", [P, D])
        gain = sb("gain_final", [P, D])
        share = sb("share", [P, TILES, GROUPS])
        total, weights = sb("total", [P, TILES]), sb("weights", [P, 2, TILES])
        stat = sb("stat_final", [P, 3, TILES])
        gain_in = sem("gain_final_in")
        x_in = [sem(f"x_final_in{t}") for t in range(TILES)]
        chances, totaled, weighted = sem("chances"), sem("totaled"), sem("weighted")
        added, squared, rooted, normed, stored = (sem("added"), sem("squared_final"), sem("rooted_final"),
                                                  sem("normed_final"), sem("stored_final"))
        block = ctx.enter_context(nc.Block())

        def height(t):
            return DEC if t == SAMPLE else P

        def store(act, t):
            act.wait_ge(normed, t + 1)
            out = io["y_sample"][0] if t == SAMPLE else io["y_prompt"][0, t * P:(t + 1) * P, :]
            act.dma_start(out, rows[0:height(t), t, 0]).then_inc(stored, 16)

        @block.sync
        def _(sp):
            for t in range(TILES):
                h = height(t)
                if t == SAMPLE:
                    sp.dma_start(x[t][0:h], io["x_mid"][t * P:t * P + h, :]).then_inc(x_in[t], 16)
                sp.dma_start(rows[0:h, t], io["expert_rows"][2 * t * P:2 * (t * P + h), :].rearrange(
                    "(p k) d -> p k d", k=2)).then_inc(x_in[t], 16)
                if t == 0:
                    sp.dma_start(gain[:], io["norm_final_gain"].partition_broadcast(P)).then_inc(gain_in, 16)

        @block.scalar
        def _(act):
            act.activation(share[:], s.group_rel[:], ACT.Exp).then_inc(chances, 1)
            act.activation(weights[:, 0], s.gap[:], ACT.Sigmoid).then_inc(chances, 1)
            act.activation(weights[:, 1], s.gap[:], ACT.Sigmoid, scale=-1.0).then_inc(chances, 1)
            for t in range(TILES):
                h = height(t)
                act.wait_ge(added, 2 * t + 2)
                if t:
                    act.wait_ge(squared, t)
                act.activation(square[0:h], x[t][0:h], ACT.Square, accum_out=stat[0:h, 0, t:t + 1]).then_inc(squared, 1)
                if t:
                    store(act, t - 1)
            store(act, TILES - 1)
            act.wait_ge(stored, 16 * TILES)

        @block.gpsimd
        def _(pool):
            for t in range(TILES):
                h = slice(0, height(t))
                pool.wait_ge(squared, t + 1)
                pool.tensor_scalar(stat[h, 1, t:t + 1], stat[h, 0, t:t + 1], 1.0 / D, EPS, ALU.mult, ALU.add)\
                    .then_inc(rooted, 1)
                pool.wait_ge(rooted, 2 * t + 1)
                pool.tensor_tensor(stat[h, 2, t:t + 1], stat[h, 1, t:t + 1], s.root[h, 0:1], ALU.pow).then_inc(rooted, 1)

        @block.vector
        def _(dve):
            chain = Chain(dve, totaled)
            dve.wait_ge(chances, 3)
            chain.link(dve.tensor_reduce(total[:], share[:], X, ALU.add))
            chain.link(dve.reciprocal(total[:], total[:]))
            dve.tensor_tensor(weights[:], weights[:], total[:].unsqueeze(1).to_broadcast([P, 2, TILES]),
                              ALU.mult).then_inc(weighted, 1)
            dve.wait_ge(weighted, 1)
            dve.wait_ge(gain_in, 16)
            dve.wait_ge(s.x_early_in, 16 * SAMPLE)
            for t in range(TILES + 1):
                if t < TILES:
                    h = slice(0, height(t))
                    dve.wait_ge(x_in[t], 32 if t == SAMPLE else 16)
                    for k in range(2):
                        if k:
                            dve.wait_ge(added, 2 * t + 1)
                        dve.scalar_tensor_tensor(x[t][h], rows[h, t, k], weights[h, k, t:t + 1], x[t][h], ALU.mult,
                                                 ALU.add).then_inc(added, 1)
                if t:
                    u = t - 1
                    h = slice(0, height(u))
                    dve.wait_ge(rooted, 2 * u + 2)
                    dve.scalar_tensor_tensor(rows[h, u, 0], x[u][h], stat[h, 2, u:u + 1], gain[h], ALU.mult,
                                             ALU.mult).then_inc(normed, 1)


SCRATCH = {"projected": ((ROWS, MAIN), F32), "x_rows": ((ROWS, D), F32), "mixed": ((ROWS, D), F32),
           "x_mid": ((ROWS, D), F32), "h_mid": ((ROWS, D), F32), "slot_table": ((SLOTS, 1), I32),
           "expert_rows": ((ASSIGNED, D), F32)}


class Shared:

    def __init__(self, nc, ctx):
        sb = lambda name, shape, dt=F32: ctx.enter_context(nc.sbuf_tensor(name, shape, dt))
        self.ident, self.ident_b = sb("ident", [P, P]), sb("ident_b", [P, P], BF16)
        self.later_b, self.before_b = sb("later_b", [P, P], BF16), sb("before_b", [P, P], BF16)
        self.ones_b = sb("ones_b", [P, P], BF16)
        self.causal, self.tri_mid = sb("causal", [P, P]), sb("tri_mid", [P, P])
        self.spans, self.valid, self.nowhere = sb("spans", [P, 3]), sb("valid", [P, TILES]), sb("nowhere", [P, TILES])
        self.root, self.iota = sb("root", [P, H_A]), sb("iota", [P, EXPERTS + GROUPS])
        self.assignment, self.rank_t = sb("assignment", [P, TILES, 2], I32), sb("rank_t", [RANK, ROWS])
        self.group_rel, self.gap = sb("group_rel", [P, TILES, GROUPS]), sb("gap", [P, TILES])
        self.number, self.at, self.carry = sb("number", [P, 2 * TILES]), sb("at", [P, 2 * TILES]), sb("carry", [P, EXPERTS])
        self.qkvr_in = ctx.enter_context(nc.semaphore("qkvr_in"))
        self.x_early_in = ctx.enter_context(nc.semaphore("x_early_in"))
        self.first_loaded = ctx.enter_context(nc.semaphore("we_first_loaded"))
        self.owner = sb("owner", [1, BLOCKS + 2], I32)

    def place(self, nc, name, shape, dt, at):
        return nc.alloc_sbuf_tensor_at(name, shape, dt, offset=self.room_at + 4 * at)


def build(nc, ins, outs):
    scratch = {n: nc.dram_tensor(n, shape, dt, kind="Internal").ap() for n, (shape, dt) in SCRATCH.items()}
    io = {**ins, **outs, **scratch}
    with ExitStack() as ctx:
        s = Shared(nc, ctx)
        constants(nc, s)
        for stage in STAGES:
            stage(nc, s, io)


STAGES = (project, mixers, feed_forward)
_OUTS = {
    "y_prompt": (1, SEQ, D), "y_sample": (1, DEC, D), "gla_prompt": (1, 1, H_A, DK, DV),
    "k_prompt": (1, 1, SEQ, H_B, DH), "v_prompt": (1, 1, SEQ, H_B, DH), "gla_sample": (1, 1, H_A, DK, DV),
    "k_sample": (1, 1, DEC, H_B, DH), "v_sample": (1, 1, DEC, H_B, DH),
}


def laid_out(inputs):
    a = {k: np.ascontiguousarray(v) for k, v in inputs.items()}
    lr = 2 * QK + 2 * MIX
    w_in = a["w_in"][0]
    return {
        "x_prompt": a["x_prompt"][0], "x_sample": a["x_sample"][0], "state_gla": a["state_gla"][0, 0],
        "cache_k": a["cache_sb_k"].reshape(PAST, MIX), "cache_v": a["cache_sb_v"].reshape(PAST, MIX),
        "norm_mix_gain": a["norm_mix_gain"][0],
        "w_main": np.concatenate([w_in[:, :lr], w_in[:, lr + RANK:]], axis=1),
        "w_rank": np.ascontiguousarray(w_in[:, lr:lr + RANK]),
        "w_gate_up": a["w_gla_gate_up"][0], "b_gate": a["b_gla_gate"][0], "gla_gain": a["gla_norm_gain"][0],
        "w_branch": a["w_branch"].reshape(2 * MIX, D), "w_out": a["w_out"][0], "norm_ffn_gain": a["norm_ffn_gain"][0],
        "w_router": np.concatenate([a["w_router_expert"][0], a["w_router_group"][0]], axis=1),
        "b_router": np.concatenate([a["b_router_expert"][0], a["b_router_group"][0]]),
        "w_exp_gate": a["w_exp_gate"].reshape(EXPERTS * D, FF), "w_exp_up": a["w_exp_up"].reshape(EXPERTS * D, FF),
        "w_exp_down": a["w_exp_down"].reshape(EXPERTS * FF, D), "norm_final_gain": a["norm_final_gain"],
    }


def kernel(**inputs):
    import concourse.bacc as _bacc
    from concourse.bass_utils import run_bass_kernel_spmd as _run

    nc = _bacc.Bacc("TRN2", target_bir_lowering=False, num_devices=1)
    arrays, ins, outs = {}, {}, {}
    for name, a in laid_out(inputs).items():
        arrays[f"in_{name}"] = a
        ins[name] = nc.dram_tensor(f"in_{name}", a.shape, mybir.dt.from_np(a.dtype), kind="ExternalInput").ap()
    for name, shape in _OUTS.items():
        outs[name] = nc.dram_tensor(f"out_{name}", shape, F32, kind="ExternalOutput").ap()
    build(nc, ins, outs)
    r = _run(nc, [arrays], core_ids=[0])
    return tuple(r.results[0][f"out_{name}"] for name in _OUTS)
```
